# Optimizing a Trainium2 kernel written in Bass

```python
import jax, jax.numpy as jnp
from jax import lax
import numpy as np

D_MODEL = 1024
BATCH = 1
SEQ = 256
DEPTH = 2

D_MIX = D_MODEL
CONV_CH = D_MIX // 2
SGU_CH = D_MIX - CONV_CH
CONV_GROUPS = 8
SGU_HEADS = 4
SGU_HEAD_DIM = SGU_CH // SGU_HEADS
CONV_WIDTH = 31
CHUNK = 128
D_IN = 2 * CONV_CH + 2 * SGU_CH
D_FF = 2816
N_EXPERTS = 8
TOP_K = 2
N_DENSE = (DEPTH + 1) // 2
N_MOE = DEPTH // 2
EPS = 1e-6


def rms_norm(x, g):
    xf = x.astype(jnp.float32)
    y = xf * lax.rsqrt(jnp.mean(xf * xf, axis=-1, keepdims=True) + EPS)
    return (y * g.astype(jnp.float32)).astype(x.dtype)

def group_layer_norm(x, n_groups, g, b):
    shp = x.shape
    xf = x.astype(jnp.float32).reshape(shp[:-1] + (n_groups, shp[-1] // n_groups))
    mu = jnp.mean(xf, axis=-1, keepdims=True)
    var = jnp.mean(jnp.square(xf - mu), axis=-1, keepdims=True)
    y = ((xf - mu) * lax.rsqrt(var + EPS)).reshape(shp)
    return (y * g.astype(jnp.float32) + b.astype(jnp.float32)).astype(x.dtype)

def causal_depthwise_conv(c, w, b):
    y = lax.conv_general_dilated(
        c, w, window_strides=(1,), padding=[(CONV_WIDTH - 1, 0)],
        dimension_numbers=('NWC', 'WIO', 'NWC'), feature_group_count=c.shape[-1])
    return y + b

def hybrid_mixer(h, w_in, conv_w, conv_b, conv_ng, conv_nb, sgu_ng, sgu_nb, sgu_w, sgu_b, w_out):
    B, S, _ = h.shape
    z = jnp.einsum('bsd,de->bse', h, w_in)
    a, gate, u, v = jnp.split(z, [CONV_CH, 2 * CONV_CH, 2 * CONV_CH + SGU_CH], axis=-1)
    c = a * jax.nn.sigmoid(gate)
    c = causal_depthwise_conv(c, conv_w, conv_b)
    c = jax.nn.silu(group_layer_norm(c, CONV_GROUPS, conv_ng, conv_nb))
    u = jax.nn.gelu(u, approximate=False)
    v = group_layer_norm(jax.nn.gelu(v, approximate=False), SGU_HEADS, sgu_ng, sgu_nb)
    n_chunks = S // CHUNK
    vc = v.reshape(B, n_chunks, CHUNK, SGU_HEADS, SGU_HEAD_DIM)
    mask = jnp.tril(jnp.ones((CHUNK, CHUNK), dtype=bool))
    ws = jnp.where(mask[None], sgu_w, jnp.zeros((), sgu_w.dtype))
    sp = jnp.einsum('hts,bnshd->bnthd', ws, vc) + jnp.transpose(sgu_b)[None, None, :, :, None]
    g_out = u * sp.reshape(B, S, SGU_CH)
    y = jnp.concatenate([c, g_out], axis=-1)
    return jnp.einsum('bse,ed->bsd', y, w_out)

def swiglu(h, wg, wu, wd):
    return jnp.einsum('...f,fd->...d', jax.nn.silu(h @ wg) * (h @ wu), wd)

def moe_swiglu(h, router, wg, wu, wd):
    B, S, D = h.shape
    ht = h.reshape(B * S, D)
    logits = jnp.einsum('td,de->te', ht, router).astype(jnp.float32)
    top_vals, top_idx = lax.top_k(logits, TOP_K)
    gates = jax.nn.softmax(top_vals, axis=-1)
    dense_gate = jnp.sum(jax.nn.one_hot(top_idx, N_EXPERTS, dtype=jnp.float32) * gates[..., None], axis=1)
    dense_gate = dense_gate.astype(h.dtype)
    out = jnp.zeros_like(ht)
    for e in range(N_EXPERTS):
        out = out + dense_gate[:, e:e + 1] * swiglu(ht, wg[e], wu[e], wd[e])
    return out.reshape(B, S, D)

def first_inputs(seed: int = 0) -> dict:
    key = jax.random.key(seed)
    ks = jax.random.split(key, 24)
    nrm = lambda k, shp, s: jax.random.normal(k, shp, jnp.float32) * s
    L = DEPTH
    return {
        "x": nrm(ks[0], (BATCH, SEQ, D_MODEL), 1.0),
        "norm_mix": 1.0 + nrm(ks[1], (L, D_MODEL), 0.05),
        "w_in": nrm(ks[2], (L, D_MODEL, D_IN), D_MODEL ** -0.5),
        "conv_w": nrm(ks[3], (L, CONV_WIDTH, 1, CONV_CH), CONV_WIDTH ** -0.5),
        "conv_b": nrm(ks[4], (L, CONV_CH), 0.02),
        "conv_ng": 1.0 + nrm(ks[5], (L, CONV_CH), 0.05),
        "conv_nb": nrm(ks[6], (L, CONV_CH), 0.02),
        "sgu_ng": 1.0 + nrm(ks[7], (L, SGU_CH), 0.05),
        "sgu_nb": nrm(ks[8], (L, SGU_CH), 0.02),
        "sgu_w": nrm(ks[9], (L, SGU_HEADS, CHUNK, CHUNK), CHUNK ** -0.5),
        "sgu_b": 1.0 + nrm(ks[10], (L, SGU_HEADS, CHUNK), 0.1),
        "w_out": nrm(ks[11], (L, D_MIX, D_MODEL), D_MIX ** -0.5),
        "norm_ffn": 1.0 + nrm(ks[12], (L, D_MODEL), 0.05),
        "ffn_wg": nrm(ks[13], (N_DENSE, D_MODEL, D_FF), D_MODEL ** -0.5),
        "ffn_wu": nrm(ks[14], (N_DENSE, D_MODEL, D_FF), D_MODEL ** -0.5),
        "ffn_wd": nrm(ks[15], (N_DENSE, D_FF, D_MODEL), D_FF ** -0.5),
        "moe_router": nrm(ks[16], (N_MOE, D_MODEL, N_EXPERTS), D_MODEL ** -0.5),
        "moe_wg": nrm(ks[17], (N_MOE, N_EXPERTS, D_MODEL, D_FF), D_MODEL ** -0.5),
        "moe_wu": nrm(ks[18], (N_MOE, N_EXPERTS, D_MODEL, D_FF), D_MODEL ** -0.5),
        "moe_wd": nrm(ks[19], (N_MOE, N_EXPERTS, D_FF, D_MODEL), D_FF ** -0.5),
        "norm_final": 1.0 + nrm(ks[20], (D_MODEL,), 0.05),
    }

def first_block(x, norm_mix, w_in, conv_w, conv_b, conv_ng, conv_nb, sgu_ng, sgu_nb, sgu_w, sgu_b,
              w_out, norm_ffn, ffn_wg, ffn_wu, ffn_wd, moe_router, moe_wg, moe_wu, moe_wd, norm_final):
    for l in range(DEPTH):
        h = rms_norm(x, norm_mix[l])
        x = x + hybrid_mixer(h, w_in[l], conv_w[l], conv_b[l], conv_ng[l], conv_nb[l],
                             sgu_ng[l], sgu_nb[l], sgu_w[l], sgu_b[l], w_out[l])
        h = rms_norm(x, norm_ffn[l])
        i = l // 2
        if l % 2 == 0:
            x = x + swiglu(h, ffn_wg[i], ffn_wu[i], ffn_wd[i])
        else:
            x = x + moe_swiglu(h, moe_router[i], moe_wg[i], moe_wu[i], moe_wd[i])
    return rms_norm(x, norm_final)


DEPTH_2 = 1

N_META = 16
BLOCK = 128
PAD = BLOCK - N_META
HEAD_DIM = 64
SB_HEADS = 8
SB_WIDTH = SB_HEADS * HEAD_DIM
SWA_Q_HEADS = 16
SWA_KV_HEADS = 2
SWA_GROUP = SWA_Q_HEADS // SWA_KV_HEADS
SWA_WIDTH = SWA_Q_HEADS * HEAD_DIM
SWA_KV_WIDTH = SWA_KV_HEADS * HEAD_DIM
WINDOW = 128
ROPE_THETA = 10000.0
RMS_EPS = 1e-6
SPLITS = (SB_WIDTH, SB_WIDTH, SB_WIDTH, SWA_WIDTH, SWA_KV_WIDTH, SWA_KV_WIDTH, SB_WIDTH, SWA_WIDTH, D_MODEL, D_MODEL)
IN_COLS = sum(SPLITS)


def rms_norm_2(x, g):
    xf = x.astype(jnp.float32)
    y = xf * lax.rsqrt(jnp.mean(xf * xf, axis=-1, keepdims=True) + RMS_EPS)
    return (y * g.astype(jnp.float32)).astype(x.dtype)

def rope(x, pos):
    half = HEAD_DIM // 2
    inv = ROPE_THETA ** (-jnp.arange(half, dtype=jnp.float32) / half)
    ang = pos.astype(jnp.float32)[:, None] * inv[None, :]
    cos = jnp.cos(ang)[None, :, None, :]
    sin = jnp.sin(ang)[None, :, None, :]
    x1 = x[..., :half].astype(jnp.float32)
    x2 = x[..., half:].astype(jnp.float32)
    out = jnp.concatenate([x1 * cos - x2 * sin, x2 * cos + x1 * sin], axis=-1)
    return out.astype(x.dtype)

def stick_breaking_attention(q, k, v, valid):
    B, L, H, d = q.shape
    scale = d ** -0.5
    outs = []
    for blk in range(L // BLOCK):
        q0 = blk * BLOCK
        end = q0 + BLOCK
        z = jnp.einsum('bqhd,bkhd->bhqk', q[:, q0:end], k[:, :end],
                       preferred_element_type=jnp.float32) * scale
        t = q0 + jnp.arange(BLOCK)
        s = jnp.arange(end)
        mask = (s[None, :] < t[:, None]) & valid[None, :end]
        log_beta = jax.nn.log_sigmoid(z)
        log_1m = jnp.where(mask, log_beta - z, 0.0)
        rev = lax.cumsum(log_1m, axis=3, reverse=True)
        suffix = jnp.concatenate([rev[..., 1:], jnp.zeros_like(rev[..., :1])], axis=-1)
        w = jnp.where(mask, jnp.exp(log_beta + suffix), 0.0)
        outs.append(jnp.einsum('bhqk,bkhd->bqhd', w.astype(v.dtype), v[:, :end]))
    return jnp.concatenate(outs, axis=1)

def sliding_window_sink_attention(q, k, v, sinks, valid):
    B, L, Hq, d = q.shape
    nb = L // BLOCK
    scale = d ** -0.5
    qb = q.reshape(B, nb, BLOCK, SWA_KV_HEADS, SWA_GROUP, d)

    def band(t):
        tb = t.reshape(B, nb, BLOCK, SWA_KV_HEADS, d)
        prev = jnp.pad(tb[:, :-1], ((0, 0), (1, 0), (0, 0), (0, 0), (0, 0)))
        return jnp.concatenate([prev, tb], axis=2)

    kb, vb = band(k), band(v)
    vblk = valid.reshape(nb, BLOCK)
    kvalid = jnp.concatenate([jnp.pad(vblk[:-1], ((1, 0), (0, 0)), constant_values=False), vblk], axis=1)
    scores = jnp.einsum('bnqhgd,bnkhd->bnhgqk', qb, kb,
                        preferred_element_type=jnp.float32) * scale
    diff = (BLOCK + jnp.arange(BLOCK))[:, None] - jnp.arange(2 * BLOCK)[None, :]
    mask = ((diff >= 0) & (diff < WINDOW))[None] & kvalid[:, None, :]
    scores = jnp.where(mask[None, :, None, None], scores, -jnp.inf)
    sink = sinks.astype(jnp.float32).reshape(SWA_KV_HEADS, SWA_GROUP)[None, None, :, :, None, None]
    sink = jnp.broadcast_to(sink, scores.shape[:-1] + (1,))
    probs = jax.nn.softmax(jnp.concatenate([scores, sink], axis=-1), axis=-1)[..., :-1]
    o = jnp.einsum('bnhgqk,bnkhd->bnqhgd', probs.astype(v.dtype), vb)
    return o.reshape(B, L, Hq * d)

def second_inputs(seed: int = 0) -> dict:
    key = jax.random.key(seed)
    ks = jax.random.split(key, 10)
    f32 = jnp.float32
    x = jax.random.normal(ks[0], (BATCH, SEQ, D_MODEL), f32)
    meta_tokens = jax.random.normal(ks[1], (N_META, D_MODEL), f32)
    norm_gain = 1.0 + 0.02 * jax.random.normal(ks[2], (DEPTH_2, D_MODEL), f32)
    w_in = jax.random.normal(ks[3], (DEPTH_2, D_MODEL, IN_COLS), f32) * D_MODEL ** -0.5
    w_branch_sb = jax.random.normal(ks[4], (DEPTH_2, SB_WIDTH, D_MODEL), f32) * SB_WIDTH ** -0.5
    w_branch_swa = jax.random.normal(ks[5], (DEPTH_2, SWA_WIDTH, D_MODEL), f32) * SWA_WIDTH ** -0.5
    w_out = jax.random.normal(ks[6], (DEPTH_2, D_MODEL, D_MODEL), f32) * D_MODEL ** -0.5
    attn_sinks = jax.random.normal(ks[7], (DEPTH_2, SWA_Q_HEADS), f32)
    final_norm_gain = 1.0 + 0.02 * jax.random.normal(ks[8], (D_MODEL,), f32)
    return {"x": x, "meta_tokens": meta_tokens, "norm_gain": norm_gain, "w_in": w_in,
            "w_branch_sb": w_branch_sb, "w_branch_swa": w_branch_swa, "w_out": w_out,
            "attn_sinks": attn_sinks, "final_norm_gain": final_norm_gain}

def second_block(x, meta_tokens, norm_gain, w_in, w_branch_sb, w_branch_swa, w_out, attn_sinks, final_norm_gain):
    B = x.shape[0]
    meta = jnp.broadcast_to(meta_tokens[None].astype(x.dtype), (B, N_META, D_MODEL))
    pad = jnp.zeros((B, PAD, D_MODEL), x.dtype)
    h = jnp.concatenate([pad, meta, x], axis=1)
    L = h.shape[1]
    idx = jnp.arange(L)
    valid = idx >= PAD
    pos = idx - PAD
    offsets = [int(o) for o in np.cumsum(SPLITS)[:-1]]
    for l in range(DEPTH_2):
        xn = rms_norm_2(h, norm_gain[l])
        proj = xn @ w_in[l]
        sb_q, sb_k, sb_v, sw_q, sw_k, sw_v, sb_z, sw_z, g_sb, g_sw = jnp.split(proj, offsets, axis=-1)
        o_sb = stick_breaking_attention(sb_q.reshape(B, L, SB_HEADS, HEAD_DIM),
                                        sb_k.reshape(B, L, SB_HEADS, HEAD_DIM),
                                        sb_v.reshape(B, L, SB_HEADS, HEAD_DIM), valid).reshape(B, L, SB_WIDTH)
        q = rope(sw_q.reshape(B, L, SWA_Q_HEADS, HEAD_DIM), pos)
        k = rope(sw_k.reshape(B, L, SWA_KV_HEADS, HEAD_DIM), pos)
        o_sw = sliding_window_sink_attention(q, k, sw_v.reshape(B, L, SWA_KV_HEADS, HEAD_DIM),
                                             attn_sinks[l], valid)
        y_sb = (o_sb * jax.nn.silu(sb_z)) @ w_branch_sb[l]
        y_sw = (o_sw * jax.nn.silu(sw_z)) @ w_branch_swa[l]
        merged = jax.nn.sigmoid(g_sb) * y_sb + jax.nn.sigmoid(g_sw) * y_sw
        h = h + merged @ w_out[l]
    return rms_norm_2(h, final_norm_gain)[:, BLOCK:]


def setup_inputs(seed=0):
    out = dict(first_inputs(seed))
    for name, value in second_inputs(seed + 1).items():
        if name != "x":
            out[name + "_2"] = value
    return out


def reference(
    x, norm_mix, w_in, conv_w, conv_b, conv_ng, conv_nb, sgu_ng, sgu_nb, sgu_w, sgu_b, w_out,
    norm_ffn, ffn_wg, ffn_wu, ffn_wd, moe_router, moe_wg, moe_wu, moe_wd, norm_final,
    meta_tokens_2, norm_gain_2, w_in_2, w_branch_sb_2, w_branch_swa_2, w_out_2, attn_sinks_2,
    final_norm_gain_2,
):
    x = first_block(
        x, norm_mix, w_in, conv_w, conv_b, conv_ng, conv_nb, sgu_ng, sgu_nb, sgu_w, sgu_b,
        w_out, norm_ffn, ffn_wg, ffn_wu, ffn_wd, moe_router, moe_wg, moe_wu, moe_wd, norm_final,
    )
    return second_block(
        x, meta_tokens_2, norm_gain_2, w_in_2, w_branch_sb_2, w_branch_swa_2, w_out_2,
        attn_sinks_2, final_norm_gain_2,
    )


_drawn_inputs = setup_inputs


def setup_inputs(seed=0):
    import zlib

    import numpy as np

    out = dict(_drawn_inputs(seed))
    spreads = {}
    factors = {'conv_nb': 3.478,
     'sgu_nb': 3.863,
     'norm_gain_2': 7.977,
     'attn_sinks_2': 8.0,
     'final_norm_gain_2': 2.707}
    for name, (base, spread) in spreads.items():
        noise = np.random.default_rng([zlib.crc32(name.encode()), seed]).standard_normal(out[name].shape)
        drawn = base * np.exp(spread * noise) if base else spread * noise
        out[name] = __import__('jax').numpy.asarray(drawn.astype(out[name].dtype))
    for name, factor in factors.items():
        out[name] = (out[name] * factor).astype(out[name].dtype)
    return out
```

```python
import numpy as np
import concourse.bass as bass
from concourse import mybir

F32 = mybir.dt.float32
F32R = mybir.dt.float32r
BF16 = mybir.dt.bfloat16
I32 = mybir.dt.int32
ALU = mybir.AluOpType
ACT = mybir.ActivationFunctionType
AX = mybir.AxisListType

P = 128
T = 256
NB = T // P
D = 1024
KT = D // P
CC = 512
CT = CC // P
ZC = 4 * CC
TAPS = 31
SH = 4
FF = 2816
FT = FF // P
NE = 8
EPS = 1e-6
ITEMS = NE + (2 * T) // (P + 1)
NEG = -1e30

RAWS, SPLITS = 4, 3
SLOT = 3072
MIX_CHUNKS = 12
FFN_CHUNKS = 24
GW = 704
TW = 352
LAYER_CHUNKS = MIX_CHUNKS + FFN_CHUNKS
MOE0 = LAYER_CHUNKS + MIX_CHUNKS
SLOTB = 2560
BCH_IN, BCH_SB, BCH_SW, BCH_OUT = 20, 2, 4, 4
Q2W = 320

META = 16
HD = 64
SBH, SWH, KVH = 8, 16, 2
SBW = SBH * HD
SWW = SWH * HD
KVW = KVH * HD
O_SBQ, O_SBK, O_SBV, O_SWQ = 0, 512, 1024, 1536
O_SWK, O_SWV, O_SBZ, O_SWZ = 2560, 2688, 2816, 3328
O_GSB, O_GSW = 4352, 5376
IN2 = 6400
QKV = O_SBZ


def constants():
    i = np.arange(P)
    ident = np.eye(P)
    iota = np.tile(i[None, :], (P, 1))
    small = np.concatenate([ident, iota], 1)
    causal = (i[:, None] <= i[None, :]).astype(float)
    group = (i[:, None] // 64 == i[None, :] // 64) / 64.0
    centre = ident - group
    mean8 = np.zeros((P, CT, 8))
    spread8 = np.zeros((P, CT, P))
    for t in range(CT):
        for c in range(P):
            mean8[c, t, 2 * t + c // 64] = 1 / 64
            spread8[2 * t + c // 64, t, c] = 1
    mix = np.concatenate([causal, centre, mean8.reshape(P, -1), spread8.reshape(P, -1)], 1)
    before = (i[:, None] < i[None, :]).astype(float)
    e = np.arange(NE)
    earlier = np.tile((e[None, :] < e[:, None]).astype(float).reshape(1, -1), (P, 1))
    route = np.concatenate([before, np.ones((P, P)), earlier, np.tile(e[None, :], (P, 1))], 1)
    upto = -(i[:, None] >= i[None, :]).astype(float)
    sbmask = np.where(i[:, None] < i[None, :], 0.0, NEG)
    own = np.where(i[None, :] <= i[:, None], 0.0, NEG)
    prev = np.where(i[None, :] > i[:, None], 0.0, NEG)
    meta = np.full((P, P), NEG)
    meta[:, :META] = np.where(i[:, None] < P - META + np.arange(META)[None, :], 0.0, NEG)
    half = HD // 2
    inv = np.float32(10000.0) ** (-np.arange(half, dtype=np.float32) / half)

    def angles(pos):
        a = pos.astype(np.float32)[:, None] * inv.astype(np.float32)[None, :]
        c, s = np.cos(a), np.sin(a)
        return np.concatenate([c, c], 1), np.concatenate([-s, s], 1)

    parts = [upto, -np.ones((P, P)), sbmask, np.concatenate([meta, own], 1), np.concatenate([prev, own], 1)]
    for pos in (META + i, META + P + i, i):
        parts += angles(pos)
    second = np.concatenate(parts, 1)
    return {k: np.ascontiguousarray(v, dtype=np.float32) for k, v in
            dict(c_small=small, c_mix=mix, c_route=route, c_second=second).items()}


def model_program(nc, a, out):
    at = [((nc.sbuf_base + 63) // 64) * 64]
    size = {F32: 4, F32R: 4, I32: 4, BF16: 2}

    def nbytes(shape, dt):
        return (int(np.prod(shape[1:])) * size[dt] + 31) // 32 * 32

    def place(name, shape, dt, cursor=None):
        cur = at if cursor is None else cursor
        t = nc.alloc_sbuf_tensor_at(name, list(shape), dt, offset=cur[0])
        cur[0] += nbytes(shape, dt)
        return t

    ring_at = at[0]
    raw = place("raw", [P, RAWS, SLOT], F32)
    high = place("high", [P, SPLITS, SLOT], F32R)
    low = place("low", [P, SPLITS, SLOT], F32R)
    ring_end = at[0]
    curb = [ring_at]
    rawb = place("rawb", [P, RAWS, SLOTB], F32, curb)
    highb = place("highb", [P, SPLITS, SLOTB], F32R, curb)
    lowb = place("lowb", [P, SPLITS, SLOTB], F32R, curb)
    spare = curb
    x = place("x", [P, NB, D], F32)
    xT_hi = place("xT_hi", [P, KT, T], F32R)
    xT_lo = place("xT_lo", [P, KT, T], F32R)
    gain = place("gain", [P, D], F32)
    small = place("small", [P, 2 * P], F32)
    ident, iota = small[:, 0:P], small[:, P:2 * P]
    eps = place("eps", [P, 1], F32)
    sumsq = place("sumsq", [P, NB], F32)
    std = place("std", [P, NB], F32)
    rstd = place("rstd", [P, NB], F32)
    items = place("items", [P, ITEMS, 4], F32)
    now = place("now", [P, 2], F32)
    gates_now = place("gates_now", [P, 2], F32)
    plan = place("plan", [P, 4], I32)
    R0 = at[0]
    assert R0 + 56320 <= nc.sbuf_usable_end, (R0, nc.sbuf_usable_end)

    xn = nc.alloc_sbuf_tensor_at("xn", [P, NB, D], F32, offset=R0)
    cur = [R0 + 8192]
    c_tok = place("c_tok", [P, NB, CC], F32, cur)
    sig = place("sig", [P, NB, CC], F32, cur)
    u = place("u", [P, NB, CC], F32, cur)
    v = place("v", [P, NB, CC], F32, cur)
    cT = place("cT", [P, CT, TAPS - 1 + T], F32, cur)
    yT = place("yT", [P, CT, T], F32, cur)
    sq = place("sq", [P, CT, T], F32, cur)
    cmix = place("cmix", [P, 2 * P + 8 * CT + CT * P], F32, cur)
    causal, centre = cmix[:, 0:P], cmix[:, P:2 * P]
    mean8 = cmix[:, 2 * P:2 * P + 8 * CT].rearrange("p (t g) -> p t g", t=CT)
    spread8 = cmix[0:8, 2 * P + 8 * CT:].rearrange("p (t c) -> p t c", t=CT)
    rows16 = place("rows16", [16, P], F32, cur)
    conv_rows = place("conv_rows", [TAPS, CC], F32, cur)
    cols = place("cols", [P, 16 + CT * TAPS], F32, cur)
    sgu_rows = place("sgu_rows", [P, SH, P], F32, cur)
    wsT = place("wsT", [P, SH, P], F32, cur)
    sgu_g = place("sgu_g", [P, CC], F32, cur)
    sgu_o = place("sgu_o", [P, CC], F32, cur)
    vstat = place("vstat", [P, NB * SH, 6], F32, cur)
    vmv = place("vmv", [P, NB * SH, 2], F32, cur)
    vstd = place("vstd", [P, NB * SH], F32, cur)
    vrstd = place("vrstd", [P, NB * SH], F32, cur)
    std8 = place("std8", [8, T], F32, cur)
    rstd8 = place("rstd8", [8, T], F32, cur)
    assert cur[0] <= nc.sbuf_usable_end, cur
    cur = [R0]
    hT_hi = place("hT_hi", [P, FT, T], F32R, cur)
    hT_lo = place("hT_lo", [P, FT, T], F32R, cur)
    h = place("h", [P, NB, 4 * TW], F32, cur)
    assert cur[0] <= nc.sbuf_usable_end, cur
    cur = [R0]
    eT_hi = place("eT_hi", [P, FT, P], F32R, cur)
    eT_lo = place("eT_lo", [P, FT, P], F32R, cur)
    eh = place("eh", [P, FF], F32, cur)
    xn_hi = place("xn_hi", [P, NB, D], F32R, cur)
    xn_lo = place("xn_lo", [P, NB, D], F32R, cur)
    pick = place("pick", [P, NB, P], F32R, cur)
    drop = place("drop", [P, NB, P], F32R, cur)
    assert cur[0] <= nc.sbuf_usable_end, cur
    xe_hi, eo_hi = (xT_hi[:, 4 * n:4 * n + 4, :].rearrange("p a b -> p (a b)") for n in range(2))
    xe_lo, eo_lo = (xT_lo[:, 4 * n:4 * n + 4, :].rearrange("p a b -> p (a b)") for n in range(2))
    cur = [R0 + 22528]
    croute = place("croute", [P, 2 * P + NE * NE + NE], F32, cur)
    before, ones = croute[:, 0:P], croute[:, P:2 * P]
    earlier = croute[:, 2 * P:2 * P + NE * NE].rearrange("p (a b) -> p a b", a=NE)
    number = croute[:, 2 * P + NE * NE:]
    router = place("router", [P, KT, NE], F32, cur)
    router_hi = place("router_hi", [P, KT, NE], F32R, cur)
    router_lo = place("router_lo", [P, KT, NE], F32R, cur)
    logit = place("logit", [P, NB, NE], F32, cur)
    above = place("above", [P, NB, NE, NE], F32, cur)
    equal = place("equal", [P, NB, NE, NE], F32, cur)
    rank = place("rank", [P, NB, NE], F32, cur)
    chosen = place("chosen", [P, NB, NE], F32, cur)
    top = place("top", [P, NB], F32, cur)
    share = place("share", [P, NB, NE], F32, cur)
    total = place("total", [P, NB], F32, cur)
    place_in = place("place_in", [P, NB, NE], F32, cur)
    crowd = place("crowd", [P, NE], F32, cur)
    crowds = place("crowds", [P, NE, NE], F32, cur)
    crowd_at = place("crowd_at", [P, NE], F32, cur)
    which = place("which", [P, 3, NE], F32, cur)
    planf = place("planf", [P, 4], F32, cur)
    dots = place("dots", [P, 3, 5, NE], F32, cur)
    assert cur[0] <= R0 + 22528 + 11264, cur
    meta_kv = place("meta_kv", [P, 1280], F32, spare)
    mT_hi = place("mT_hi", [P, KT, P], F32R, spare)
    mT_lo = place("mT_lo", [P, KT, P], F32R, spare)
    swqT_at = [spare[0] - 8192]
    assert spare[0] <= ring_end, (spare, ring_end)
    swqT = place("swqT", [P, SWH // 2, T], F32, swqT_at)
    cur = [R0]
    qkv = place("qkv", [P, NB, QKV], F32, cur)
    sbz = place("sbz", [P, NB, Q2W], F32, cur)
    gates_at = cur[0]
    sbqT = place("sbqT", [P, SBH // 2, T], F32, cur)
    sbkT = place("sbkT", [P, SBH // 2, T], F32, cur)
    sbkTm = place("sbkTm", [P, SBH // 2, 2, META], F32, cur)
    swkk = place("swkk", [P, NB, 2 * KVW], F32, cur)
    swkT = place("swkT", [P, KVH, T], F32, cur)
    swkTm = place("swkTm", [P, KVH, META], F32, cur)
    csec = place("csec", [P, 7 * P + 6 * HD], F32, cur)
    sbm = place("sbm", [P, P], BF16, cur)
    swm = place("swm", [P, NB, T], BF16, cur)
    identb = place("identb", [P, P], BF16, cur)
    swkm = place("swkm", [META, 2 * KVW], F32, cur)
    sinks = place("sinks", [P, SWH], F32, cur)
    one = place("one", [P, 1], F32, cur)
    meta_s = place("meta_s", [META, 4], F32, cur)
    mx, nmax, den, den2, rden, esink = (place(n, [P, 8], F32, cur) for n in ("mx", "nmax", "den", "den2", "rden", "esink"))
    work = cur[0]
    rtmp = place("rtmp", [P, (SWH + KVH) * HD], F32, [work])
    cur = [work]
    sb_a = place("sb_a", [P, 2, 3 * P], F32, cur)
    sb_m_ = place("sb_m", [P, 2, 3 * P], F32, cur)
    sb_w = place("sb_w", [P, 2, 3 * P], F32, cur)
    assert cur[0] <= nc.sbuf_usable_end, (cur, nc.sbuf_usable_end)
    prob = place("prob", [P, 8, T], F32, [work])
    assert work + 8192 <= nc.sbuf_usable_end
    left = [spare[0]]
    sb_am = place("sb_am", [META, 2 * T], F32, left)
    sb_mm = place("sb_mm", [META, 2 * T], F32, left)
    sb_wm = place("sb_wm", [META, 2 * T], F32, left)
    assert left[0] <= ring_end, (left, ring_end)
    pt = place("pt", [P, 2, 4 * P], F32, [spare[0]])
    xm = place("xm", [META, D], F32, [R0 + 8192])
    xm_junk = place("xm_junk", [META, D], F32, [R0 + 8192 + 4096])
    cur = [gates_at]
    gsig = place("gsig", [P, NB, 2 * D], F32, cur)
    sbT_hi = place("sbT_hi", [P, SBW // P, T], F32R, cur)
    sbT_lo = place("sbT_lo", [P, SBW // P, T], F32R, cur)
    assert cur[0] <= nc.sbuf_usable_end
    merged = qkv[:, :, O_SBK:O_SBK + D]

    ps = nc.alloc_psum_tensor("ps", [P, 8, 512], F32)
    TP = (4, 5)
    DOWN = (6, 7, 0, 1)

    def f(t):
        return t.bitcast(F32)

    def sem(name):
        return nc.alloc_semaphore(name)

    w_landed = [sem(f"w_landed{s}") for s in range(RAWS)]
    hi_made, lo_made, w_used = sem("hi_made"), sem("lo_made"), sem("w_used")
    wb_landed = [sem(f"wb_landed{s}") for s in range(RAWS)]
    bhi_made, blo_made, bw_used = sem("bhi_made"), sem("blo_made"), sem("bw_used")
    x_landed, small_landed, gain_landed = sem("x_landed"), sem("small_landed"), sem("gain_landed")
    mix_landed, route_landed, second_landed = sem("mix_landed"), sem("route_landed"), sem("second_landed")
    eps_made = sem("eps_made")
    sumsq_made, std_made, rstd_made, xn_made = sem("sumsq_made"), sem("std_made"), sem("rstd_made"), sem("xn_made")
    xt_filled, xt_hi, xt_lo = sem("xt_filled"), sem("xt_hi"), sem("xt_lo")
    x_made = sem("x_made")
    dve_steps, act_steps = sem("dve_steps"), sem("act_steps")
    sig_made, c_made = sem("sig_made"), sem("c_made")
    prep_filled, prep_made = sem("prep_filled"), sem("prep_made")
    pad_made, ct_filled, ct_made, conv_step = sem("pad_made"), sem("ct_filled"), sem("ct_made"), sem("conv_step")
    u_made, v_made, vvar_made, vstd_made = sem("u_made"), sem("v_made"), sem("vvar_made"), sem("vstd_made")
    vvar_stats = sem("vvar_stats")
    vnorm_ready, vnorm_made, vn_made = sem("vnorm_ready"), sem("vnorm_made"), sem("vn_made")
    vg_made = sem("vg_made")
    sp_filled, g_made, gt_filled = sem("sp_filled"), sem("g_made"), sem("gt_filled")
    cat_hi, cat_lo = sem("cat_hi"), sem("cat_lo")
    yc_filled, yc_made, sq_made, var_filled = sem("yc_filled"), sem("yc_made"), sem("sq_made"), sem("var_filled")
    std8_made, rstd8_made, rb_filled, yn_made, cs_made = (
        sem("std8_made"), sem("rstd8_made"), sem("rb_filled"), sem("yn_made"), sem("cs_made"))
    silu_made, mult_made = sem("silu_made"), sem("mult_made")
    ht_filled, ht_hi, ht_lo = sem("ht_filled"), sem("ht_hi"), sem("ht_lo")
    router_split, logits_ready, logit_made, expo_made = (
        sem("router_split"), sem("logits_ready"), sem("logit_made"), sem("expo_made"))
    chosen_made, places_ready, routed = sem("chosen_made"), sem("places_ready"), sem("routed")
    xs_hi, xs_lo = sem("xs_hi"), sem("xs_lo")
    now_made, pick_made = sem("now_made"), sem("pick_made")
    tp_filled, tp_hi, tp_freed = sem("tp_filled"), sem("tp_hi"), sem("tp_freed")
    esilu_made, emult_made = sem("esilu_made"), sem("emult_made")
    eo_hi_made, eo_lo_made = sem("eo_hi_made"), sem("eo_lo_made")

    Z_ORDER = (1, 0, 2, 3)
    OUT_ROWS = (4, 6, 0, 2)

    def down_tiles(d):
        return range(3 * d, min(3 * d + 3, FT))

    def words(c):
        j = (c - MOE0) % FFN_CHUNKS if c >= MOE0 else c % LAYER_CHUNKS - MIX_CHUNKS
        if j < 0:
            return 2048
        return 8 * TW if j < 16 else D * len(down_tiles(j - 16))

    def mixer_source(l, j):
        if j < 8:
            q, kh = Z_ORDER[j // 2], j % 2
            return a["w_in"][l, kh * 512:kh * 512 + 512, q * CC:q * CC + CC].rearrange("(t p) n -> p t n", p=P)
        k = OUT_ROWS[j - 8]
        return a["w_out"][l, k * P:(k + 2) * P, :].rearrange("(t p) n -> p t n", p=P)

    def ffn_source(j):
        if j < 16:
            w = a["ffn_wg"] if j % 2 == 0 else a["ffn_wu"]
            q = j // 2
            return w[0, :, q * TW:q * TW + TW].rearrange("(t p) n -> p t n", p=P)
        t = down_tiles(j - 16)
        return a["ffn_wd"][0, t[0] * P:(t[-1] + 1) * P, :].rearrange("(t p) n -> p t n", p=P)

    wg_v = a["moe_wg"].rearrange("l e (t p) n -> (l e) p t n", p=P)
    wu_v = a["moe_wu"].rearrange("l e (t p) n -> (l e) p t n", p=P)
    wd_v = a["moe_wd"].rearrange("l e (t p) n -> (l e) p t n", p=P)

    def expert_source(e, j):
        if j < 16:
            g, kh = j // 4, j % 2
            w = wg_v if j % 4 < 2 else wu_v
            return w[e, :, 4 * kh:4 * kh + 4, g * GW:g * GW + GW]
        t = down_tiles(j - 16)
        return wd_v[e, :, t[0]:t[-1] + 1, :]

    def chunk(i, j):
        return MOE0 + FFN_CHUNKS * i + j

    def slot_view(ring, s, rows, width, kt=None):
        return ring[:, s, 0:rows * width].rearrange("p (t n) -> p t n", t=rows)

    def load(sp, c, src):
        if c >= RAWS:
            sp.wait_ge(lo_made, c - RAWS + 1)
        rows, width = src.shape[1], src.shape[2]
        sp.dma_start(slot_view(raw, c % RAWS, rows, width), src).then_inc(w_landed[c % RAWS], 16)

    def load_item(sp, i, j, src):
        sp.wait_ge(lo_made, chunk(i, j - RAWS + 1))
        rows, width = src.shape[1], src.shape[2]
        sp.dma_start(slot_view(raw, j % RAWS, rows, width), src).then_inc(w_landed[j % RAWS], 16)

    def make_high(act, c):
        act.wait_ge(w_landed[c % RAWS], 16 * (c // RAWS + 1))
        if c >= SPLITS:
            act.wait_ge(w_used, c - SPLITS + 1)
        n = words(c)
        nc.scalar.activation(high[:, c % SPLITS, 0:n], raw[:, c % RAWS, 0:n], ACT.Copy).then_inc(hi_made, 1)

    def make_high_item(act, i, j):
        act.wait_ge(w_landed[j % RAWS], 16 * (MOE0 // RAWS + j // RAWS + 1) + i * (16 * FFN_CHUNKS // RAWS))
        act.wait_ge(w_used, chunk(i, j - SPLITS + 1))
        n = words(chunk(0, j))
        nc.scalar.activation(high[:, j % SPLITS, 0:n], raw[:, j % RAWS, 0:n], ACT.Copy).then_inc(hi_made, 1)

    def make_low(dve, c):
        dve.wait_ge(hi_made, c + 1)
        n = words(c)
        nc.vector.tensor_tensor(low[:, c % SPLITS, 0:n], raw[:, c % RAWS, 0:n], f(high[:, c % SPLITS, 0:n]),
                                ALU.subtract).then_inc(lo_made, 1)

    def make_low_item(dve, i, j):
        dve.wait_ge(hi_made, chunk(i, j + 1))
        n = words(chunk(0, j))
        nc.vector.tensor_tensor(low[:, j % SPLITS, 0:n], raw[:, j % RAWS, 0:n], f(high[:, j % SPLITS, 0:n]),
                                ALU.subtract).then_inc(lo_made, 1)

    def three(out, xh, xl, wh, wl, first, last):
        nc.tensor.matmul(out, xh, wh, start=first, stop=False)
        nc.tensor.matmul(out, xh, wl, start=False, stop=False)
        return nc.tensor.matmul(out, xl, wh, start=False, stop=last)

    def row_product(hT, lT, tiles, s, acc_of, blocks, first, last, rings=None):
        hr, lr = rings or (high, low)
        wh, wl = (slot_view(r, s, len(tiles), D) for r in (hr, lr))
        for n, t in enumerate(tiles):
            for b in range(blocks):
                for half in range(2):
                    c = slice(half * 512, half * 512 + 512)
                    mm = three(ps[:, acc_of(b, half), :], hT[:, t, b * P:b * P + P], lT[:, t, b * P:b * P + P],
                               wh[:, n, c], wl[:, n, c], first and n == 0, last and n == len(tiles) - 1)
        return mm

    BATCHES = ((0, 4), (4, 8), (8, 11), (11, 15), (15, 19), (19, 22))
    BATCH_GROUPS = (1, 2, 2, 3, 4, 4)
    AFTER_T = {6: 0, 9: 1, 10: 2, 13: 3, 17: 4, 18: 5}

    def fill_no(i, pos):
        if isinstance(i, int) and i == 0:
            return pos if pos < 4 else pos - 4
        return 16 * i - 4 + pos

    def batch_of(tile):
        return next(n for n, (lo, hi) in enumerate(BATCHES) if lo <= tile < hi)


    NORMS = 7
    xm_landed, meta_sum, meta_std, meta_made = sem("xm_landed"), sem("meta_sum"), sem("meta_std"), sem("meta_made")
    mt_zero, mt_filled, mt_hi_made, mt_lo_made = sem("mt_zero"), sem("mt_filled"), sem("mt_hi_made"), sem("mt_lo_made")
    masks_made = sem("masks_made")
    bz_read, meta_read = sem("bz_read"), sem("meta_read")
    rope_made, qk_filled, qk_made = sem("rope_made"), sem("qk_filled"), sem("qk_made")
    sbz_filled, sb_log_made, sb_m_made, sbs_filled, sb_w_made, sbo_filled, sbo_made = (
        sem("sbz_filled"), sem("sb_log_made"), sem("sb_m_made"), sem("sbs_filled"), sem("sb_w_made"),
        sem("sbo_filled"), sem("sbo_made"))
    sc_filled, max_made, prob_made, sink_made, den_made = (
        sem("sc_filled"), sem("max_made"), sem("prob_made"), sem("sink_made"), sem("den_made"))
    pt_filled, pt_act, pt_dve, pv_done, swo_made = (
        sem("pt_filled"), sem("pt_act"), sem("pt_dve"), sem("pv_done"), sem("swo_made"))
    zs_made, zmul_made, gs_made = sem("zs_made"), sem("zmul_made"), sem("gs_made")
    ot_filled, ot_hi, ot_lo = sem("ot_filled"), sem("ot_hi"), sem("ot_lo")
    merged_made, x2_made, out_written = sem("merged_made"), sem("x2_made"), sem("out_written")

    upto, minus_ones = csec[:, 0:P], csec[:, P:2 * P]
    ANG = 2 * P + P + 4 * P

    def angle(n, which):
        return csec[:, ANG + 2 * HD * n + HD * which:ANG + 2 * HD * n + HD * which + HD]

    def words_b(c):
        return KT * Q2W if c < BCH_IN else 2 * D

    META_TILES = {1: (192, 320, 0), 2: (0, 320, 128), 3: (0, 320, 448), 4: (0, 256, 768), 8: (0, 256, 1024)}
    META_ORDER = sorted(META_TILES)
    SBO, SWO = O_SBQ, O_SWQ

    def gates_of(q):
        out = []
        for kind, start, width, to in (("z", O_SBZ, SBW, SBO), ("z", O_SWZ, SWW, SWO), ("g", O_GSB, 2 * D, 0)):
            lo, hi = max(start, q * Q2W), min(start + width, (q + 1) * Q2W)
            if lo < hi:
                out.append((kind, lo - q * Q2W, hi - q * Q2W, to + lo - start))
        return out

    def sw_place(n):
        return 2 * (n % 2) + n // 4, (n // 2 % 2) * T

    def merge_bank(b, half):
        return 2 + 2 * b + half

    def second_loads(sp, n_items):
        sp.wait_ge(lo_made, chunk(n_items, 0))
        for c in range(BCH_IN + BCH_SB + BCH_SW + BCH_OUT):
            if c >= RAWS:
                sp.wait_ge(blo_made, c - RAWS + 1)
            if c < BCH_IN:
                src = a["w_in_2"][0, :, c * Q2W:c * Q2W + Q2W].rearrange("(t p) n -> p t n", p=P)
            else:
                n = c - BCH_IN
                w, n = ((a["w_branch_sb_2"], n) if n < BCH_SB else (a["w_branch_swa_2"], n - BCH_SB)
                        if n < BCH_SB + BCH_SW else (a["w_out_2"], n - BCH_SB - BCH_SW))
                src = w[0, 2 * n * P:(2 * n + 2) * P, :].rearrange("(t p) n -> p t n", p=P)
            sp.dma_start(slot_view(rawb, c % RAWS, src.shape[1], src.shape[2]), src).then_inc(wb_landed[c % RAWS], 16)
        for b in range(NB):
            sp.wait_ge(xn_made, 2 * NORMS - 1 + b)
            sp.dma_start(out[0, b * P:b * P + P, :], xn[:, b, :]).then_inc(out_written, 16)
        sp.wait_ge(out_written, 32)

    def second_small_loads(pool):
        pool.wait_ge(xn_made, 10)
        pool.dma_start(xm[:, :], a["meta_tokens_2"]).then_inc(xm_landed, 16)
        pool.dma_start(csec[:, :], a["c_second"]).then_inc(second_landed, 16)
        pool.dma_start(sinks[:, :], a["attn_sinks_2"][0:1, :].to_broadcast([P, SWH])).then_inc(second_landed, 16)
        pool.memset(f(mT_hi[:, :, :]), 0.0).then_inc(mt_zero, 1)
        pool.memset(f(mT_lo[:, :, :]), 0.0).then_inc(mt_zero, 1)
        pool.memset(sbkTm[:, :, :, :], 0.0).then_inc(mt_zero, 1)
        pool.wait_ge(second_landed, 32)
        pool.tensor_copy(sbm[:, :], csec[:, 2 * P:3 * P]).then_inc(masks_made, 1)
        pool.tensor_copy(swm[:, :, :], csec[:, 3 * P:7 * P].rearrange("p (b n) -> p b n", b=NB)).then_inc(masks_made, 1)
        pool.tensor_copy(identb[:, :], ident).then_inc(masks_made, 1)

    def second_scalar(act, n_items, norm_stats, norm_high):
        steps = [0]

        def step(ins):
            steps[0] += 1
            ins.then_inc(act_steps, 1)
            act.wait_ge(act_steps, steps[0])

        made = [0]

        def high_upto(c):
            while made[0] <= min(c, 29):
                c1 = made[0]
                act.wait_ge(wb_landed[c1 % RAWS], 16 * (c1 // RAWS + 1))
                if c1 >= SPLITS:
                    act.wait_ge(bw_used, c1 - SPLITS + 1)
                n = words_b(c1)
                nc.scalar.activation(highb[:, c1 % SPLITS, 0:n], rawb[:, c1 % RAWS, 0:n], ACT.Copy).then_inc(bhi_made, 1)
                made[0] += 1

        act.wait_ge(tp_freed, 16 * n_items)
        norm_stats(4)
        act.wait_ge(xn_made, 10)
        norm_stats(5)
        act.wait_ge(xm_landed, 16)
        nc.scalar.activation(xm_junk[:, :], xm[:, :], ACT.Square, accum_out=meta_s[:, 0:1]).then_inc(meta_sum, 1)
        act.wait_ge(meta_sum, 1)
        nc.scalar.activation(meta_s[:, 1:2], meta_s[:, 0:1], ACT.Sqrt, bias=eps[0:META, 0:1], scale=1.0 / D).then_inc(meta_std, 1)
        high_upto(0)
        norm_high(4)
        act.wait_ge(mt_filled, 1)
        act.wait_ge(mt_zero, 3)
        nc.scalar.activation(mT_hi[:, :, 0:META], ps[:, 2, 0:KT * META].rearrange("p (t n) -> p t n", t=KT),
                             ACT.Copy).then_inc(mt_hi_made, 1)
        for q in range(9):
            high_upto(q + 2)
            act.wait_ge(bw_used, q + 1)
            w = min(Q2W, QKV - q * Q2W)
            for b in range(NB):
                ins = nc.scalar.activation(qkv[:, b, q * Q2W:q * Q2W + w], ps[:, 2 * (q % 2) + b, 0:w], ACT.Copy)
                if q == 8:
                    nc.scalar.activation(sbz[:, b, 0:Q2W - w], ps[:, 2 * (q % 2) + b, w:Q2W], ACT.Silu).then_inc(zs_made, 1)
                else:
                    ins.then_inc(bz_read, 1)
        for n in range(10):
            act.wait_ge(qk_filled, n + 1)
            bank = ps[:, TP[n % 2], :]
            pair = bank.rearrange("p (t n) -> p t n", t=2)
            if n < 2:
                nc.scalar.activation(sbqT[:, 2 * n:2 * n + 2, :], pair, ACT.Copy, scale=HD ** -0.5).then_inc(qk_made, 1)
            elif n < 4:
                nc.scalar.activation(sbkT[:, 2 * n - 4:2 * n - 2, :], pair, ACT.Copy).then_inc(qk_made, 1)
            elif n == 4:
                for r in range(2):
                    rows = slice(64 * r, 64 * r + 64)
                    nc.scalar.activation(sbkTm[rows, :, r, :], bank[rows, 0:4 * META].rearrange("p (t n) -> p t n", t=4), ACT.Copy)
                nc.scalar.activation(swkTm[:, :, :], bank[:, 4 * META:6 * META].rearrange("p (t n) -> p t n", t=2),
                                     ACT.Copy).then_inc(qk_made, 1)
            elif n == 5:
                nc.scalar.activation(swkT[:, :, :], pair, ACT.Copy).then_inc(qk_made, 1)
            else:
                nc.scalar.activation(swqT[:, 2 * n - 12:2 * n - 10, :], pair, ACT.Copy, scale=HD ** -0.5).then_inc(qk_made, 1)

        def sb_log(p):
            s = 3 * (p % 2)
            act.wait_ge(sbz_filled, p + 1)
            if p:
                act.wait_ge(sb_m_made, 2 * p)
            nc.scalar.activation(sb_a[:, :, :], ps[:, s:s + 2, 0:3 * P], ACT.Abs)
            step(nc.scalar.activation(sb_am[:, :], ps[0:META, s + 2, :], ACT.Abs))
            nc.scalar.activation(sb_a[:, :, :], sb_a[:, :, :], ACT.Exp, scale=-1.0)
            step(nc.scalar.activation(sb_am[:, :], sb_am[:, :], ACT.Exp, scale=-1.0))
            nc.scalar.activation(sb_a[:, :, :], sb_a[:, :, :], ACT.Ln, bias=one[:, 0:1]).then_inc(sb_log_made, 1)
            nc.scalar.activation(sb_am[:, :], sb_am[:, :], ACT.Ln, bias=one[0:META, 0:1]).then_inc(sb_log_made, 1)

        def sb_weights(p):
            s = 3 * (p % 2)
            act.wait_ge(sbs_filled, p + 1)
            if p:
                act.wait_ge(sbo_filled, p)
            nc.scalar.activation(sb_w[:, :, :], ps[:, s:s + 2, 0:3 * P], ACT.Exp).then_inc(sb_w_made, 1)
            nc.scalar.activation(sb_wm[:, :], ps[0:META, s + 2, :], ACT.Exp).then_inc(sb_w_made, 1)

        high_upto(11)
        sb_log(0)
        for p in range(1, 4):
            sb_log(p)
            sb_weights(p - 1)
        sb_weights(3)

        for w in range(4):
            act.wait_ge(max_made, 2 * w + 2)
            if w:
                act.wait_ge(pt_filled, 4 * w)
            for n in range(8):
                ins = nc.scalar.activation(prob[:, n, :], ps[:, sw_place(n)[0], sw_place(n)[1]:sw_place(n)[1] + T], ACT.Exp,
                                           bias=nmax[:, n:n + 1], accum_out=den[:, n:n + 1])
                ins.then_inc(prob_made, 1)
            nc.scalar.activation(esink[:, :], esink[:, :], ACT.Exp).then_inc(sink_made, 1)
            for fl in (0, 2):
                k = 4 * w + fl
                act.wait_ge(pt_filled, k + 1)
                if k >= 2:
                    act.wait_ge(pv_done, k - 1)
                nc.scalar.activation(pt[:, 0, :], ps[:, TP[0], :], ACT.Copy).then_inc(pt_act, 1)
        zs = [2]
        gs = [0]
        for q in range(9, BCH_IN):
            high_upto(q + 2)
            act.wait_ge(bw_used, q + 1)
            for kind, lo, hi, to in gates_of(q):
                for b in range(NB):
                    src = ps[:, 2 * (q % 2) + b, lo:hi]
                    if kind == "z":
                        act.wait_ge(zmul_made, zs[0] // 2)
                        ins = nc.scalar.activation(sbz[:, b, lo:hi], src, ACT.Silu)
                        ins.then_inc(zs_made, 1)
                    else:
                        if not gs[0]:
                            act.wait_ge(swo_made, 4)
                        ins = nc.scalar.activation(gsig[:, b, to:to + hi - lo], src, ACT.Sigmoid)
                        ins.then_inc(gs_made, 1)
                        gs[0] += 1
                if kind == "z":
                    zs[0] += 2
            if q == 12:
                for m in range(2):
                    act.wait_ge(ot_filled, m + 1)
                    nc.scalar.activation(sbT_hi[:, 2 * m:2 * m + 2, :], ps[:, TP[m], :].rearrange("p (t n) -> p t n", t=2),
                                         ACT.Copy).then_inc(ot_hi, 1)
        norm_high(5)
        high_upto(23)
        high_upto(25)
        high_upto(27)
        norm_high(6)
        high_upto(29)
        act.wait_ge(x2_made, 4)
        norm_stats(6)

    def second_vector(dve, n_items, step, norm_apply, norm_low):
        made = [0]

        def low_upto(c):
            while made[0] <= min(c, 29):
                c1 = made[0]
                dve.wait_ge(bhi_made, c1 + 1)
                n = words_b(c1)
                nc.vector.tensor_tensor(lowb[:, c1 % SPLITS, 0:n], rawb[:, c1 % RAWS, 0:n], f(highb[:, c1 % SPLITS, 0:n]),
                                        ALU.subtract).then_inc(blo_made, 1)
                made[0] += 1

        dve.wait_ge(tp_freed, 16 * n_items)
        norm_apply(4, x)
        step(nc.vector.memset(one[:, :], 1.0))
        dve.wait_ge(xn_made, 10)
        norm_apply(5, xn)
        dve.wait_ge(meta_std, 1)
        step(nc.vector.reciprocal(meta_s[:, 2:3], meta_s[:, 1:2]))
        nc.vector.scalar_tensor_tensor(xm[:, :], xm[:, :], meta_s[:, 2:3], gain[0:META, :], ALU.mult, ALU.mult).then_inc(meta_made, 1)
        low_upto(0)
        norm_low(4)
        dve.wait_ge(mt_hi_made, 1)
        nc.vector.tensor_tensor(mT_lo[:, :, 0:META], ps[:, 2, 0:KT * META].rearrange("p (t n) -> p t n", t=KT),
                                f(mT_hi[:, :, 0:META]), ALU.subtract).then_inc(mt_lo_made, 1)
        for q in range(9):
            low_upto(q + 2)
            if q in META_TILES:
                lo, hi, to = META_TILES[q]
                k = META_ORDER.index(q)
                dve.wait_ge(bw_used, q + 1)
                nc.vector.tensor_copy(meta_kv[0:META, to:to + hi - lo], ps[0:META, 6 + k % 2, 0:hi - lo]).then_inc(meta_read, 1)
        dve.wait_ge(zs_made, 2)
        dve.wait_ge(second_landed, 32)
        half = HD // 2

        def rotate(rows, src, heads, n):
            s = src.rearrange("p (h d) -> p h d", h=heads)
            tmp = rtmp[0:rows, 0:heads * HD].rearrange("p (h d) -> p h d", h=heads)
            c, sn = (angle(n, k)[0:rows, :].rearrange("p (o d) -> p o d", o=1) for k in (0, 1))
            nc.vector.tensor_tensor(tmp[:, :, 0:half], s[:, :, half:HD], sn[:, :, 0:half].to_broadcast([rows, heads, half]), ALU.mult)
            step(nc.vector.tensor_tensor(tmp[:, :, half:HD], s[:, :, 0:half], sn[:, :, half:HD].to_broadcast([rows, heads, half]), ALU.mult))
            step(nc.vector.tensor_tensor(s, s, c.to_broadcast([rows, heads, HD]), ALU.mult))
            step(nc.vector.tensor_tensor(s, s, tmp, ALU.add))

        dve.wait_ge(meta_read, 5)
        rotate(META, meta_kv[0:META, 1024:1152], KVH, 2)
        step(nc.vector.tensor_copy(swkm[:, :].rearrange("p (g u d) -> p g u d", g=KVH, u=2),
                                   meta_kv[0:META, 1024:1152].rearrange("p (g o d) -> p g o d", g=KVH, o=1)
                                   .to_broadcast([META, KVH, 2, HD])))
        for b in range(NB):
            rotate(P, qkv[:, b, O_SWQ:O_SWV], SWH + KVH, b)
            nc.vector.tensor_copy(swkk[:, b, :].rearrange("p (g u d) -> p g u d", g=KVH, u=2),
                                  qkv[:, b, O_SWK:O_SWV].rearrange("p (g o d) -> p g o d", g=KVH, o=1)
                                  .to_broadcast([P, KVH, 2, HD])).then_inc(rope_made, 1)
        low_upto(11)

        def sb_m(p):
            s = 3 * (p % 2)
            if p:
                dve.wait_ge(sbs_filled, p)
            dve.wait_ge(sb_log_made, 2 * p + 2)
            nc.vector.scalar_tensor_tensor(sb_m_[:, :, :], ps[:, s:s + 2, 0:3 * P], 0.0, sb_a[:, :, :], ALU.max, ALU.add).then_inc(sb_m_made, 1)
            nc.vector.scalar_tensor_tensor(sb_mm[:, :], ps[0:META, s + 2, :], 0.0, sb_am[:, :], ALU.max, ALU.add).then_inc(sb_m_made, 1)

        for p in range(4):
            sb_m(p)
        for b in range(NB):
            dve.wait_ge(sbo_filled, 4)
            nc.vector.tensor_copy(qkv[:, b, SBO:SBO + SBW], ps[:, 6 + b, :]).then_inc(sbo_made, 1)
        for w in range(4):
            b, g = w // 2, w % 2
            dve.wait_ge(sc_filled, w + 1)
            step(nc.vector.tensor_reduce(mx[:, :].rearrange("p (q r) -> p r q", r=2),
                                         ps[:, 0:4, :].rearrange("p (r a) (u n) -> p r (a u) n", r=2, u=2), AX.X, ALU.max))
            step(nc.vector.tensor_tensor(mx[:, :], mx[:, :], sinks[:, 8 * g:8 * g + 8], ALU.max))
            if w:
                dve.wait_ge(den_made, w)
            nc.vector.tensor_scalar(nmax[:, :], mx[:, :], -1.0, None, ALU.mult).then_inc(max_made, 1)
            nc.vector.tensor_tensor(esink[:, :], sinks[:, 8 * g:8 * g + 8], mx[:, :], ALU.subtract).then_inc(max_made, 1)
            dve.wait_ge(sink_made, w + 1)
            step(nc.vector.tensor_tensor(den2[:, :], den[:, :], esink[:, :], ALU.add))
            nc.vector.reciprocal(rden[:, :], den2[:, :]).then_inc(den_made, 1)
            for fl in (1, 3):
                k = 4 * w + fl
                dve.wait_ge(pt_filled, k + 1)
                if k >= 2:
                    dve.wait_ge(pv_done, k - 1)
                nc.vector.tensor_copy(pt[:, 1, :], ps[:, TP[1], :]).then_inc(pt_dve, 1)
            dve.wait_ge(pv_done, 4 * w + 4)
            dve.wait_ge(den_made, w + 1)
            nc.vector.tensor_tensor(qkv[:, b, SWO + 512 * g:SWO + 512 * g + 512].rearrange("p (h d) -> p h d", h=8),
                                    ps[:, 6 + w % 2, :].rearrange("p (h d) -> p h d", h=8),
                                    rden[:, :].rearrange("p (h o) -> p h o", o=1).to_broadcast([P, 8, HD]),
                                    ALU.mult).then_inc(swo_made, 1)
        zs = [0]

        def gate_output(q):
            for kind, lo, hi, to in gates_of(q):
                if kind != "z":
                    continue
                zs[0] += 2
                dve.wait_ge(zs_made, zs[0])
                if zs[0] == 2:
                    dve.wait_ge(sbo_made, 2)
                    dve.wait_ge(swo_made, 4)
                off = lo if q != 8 else 0
                nc.vector.tensor_tensor(qkv[:, :, to:to + hi - lo], qkv[:, :, to:to + hi - lo], sbz[:, :, off:off + hi - lo],
                                        ALU.mult).then_inc(zmul_made, 1)

        gate_output(8)
        for q in range(9, BCH_IN):
            low_upto(q + 2)
            gate_output(q)
            if q == 12:
                for m in range(2):
                    dve.wait_ge(ot_hi, m + 1)
                    nc.vector.tensor_tensor(sbT_lo[:, 2 * m:2 * m + 2, :], ps[:, TP[m], :].rearrange("p (t n) -> p t n", t=2),
                                            f(sbT_hi[:, 2 * m:2 * m + 2, :]), ALU.subtract).then_inc(ot_lo, 1)
        norm_low(5)
        low_upto(23)
        for b in range(NB):
            for half_ in range(2):
                c = slice(half_ * 512, half_ * 512 + 512)
                dve.wait_ge(bw_used, BCH_IN + BCH_SB)
                dve.wait_ge(gs_made, gs_total)
                nc.vector.tensor_tensor(merged[:, b, c], ps[:, DOWN[2 * b + half_], :], gsig[:, b, c], ALU.mult).then_inc(merged_made, 1)
        low_upto(25)
        low_upto(27)
        for b in range(NB):
            for half_ in range(2):
                c = slice(half_ * 512, half_ * 512 + 512)
                g2 = gsig[:, b, D + half_ * 512:D + half_ * 512 + 512]
                dve.wait_ge(bw_used, BCH_IN + BCH_SB + BCH_SW)
                step(nc.vector.tensor_tensor(g2, ps[:, merge_bank(b, half_), :], g2, ALU.mult))
                nc.vector.tensor_tensor(merged[:, b, c], merged[:, b, c], g2, ALU.add).then_inc(merged_made, 1)
        norm_low(6)
        low_upto(29)
        for b in range(NB):
            for half_ in range(2):
                part = x[:, b, half_ * 512:half_ * 512 + 512]
                dve.wait_ge(bw_used, 30)
                nc.vector.tensor_tensor(part, part, ps[:, DOWN[2 * b + half_], :], ALU.add).then_inc(x2_made, 1)
        dve.wait_ge(x2_made, 4)
        norm_apply(6, xn)

    gs_total = 2 * sum(kind == "g" for q in range(9, BCH_IN) for kind, *_ in gates_of(q))

    def second_tensor(pe, n_items, norm_transposes):
        norm_transposes(5, 4)
        pe.wait_ge(meta_made, 1)
        for k in range(KT):
            mm = nc.tensor.transpose(ps[:, 2, k * META:k * META + META], xm[:, k * P:k * P + P], ident[0:META, 0:META])
        mm.then_inc(mt_filled, 1)
        pe.wait_ge(mt_lo_made, 1)

        def input_tile(q):
            pe.wait_ge(blo_made, q + 1)
            if q >= 2:
                pe.wait_ge(*read_of(q - 2))
            wh, wl = (slot_view(r, q % SPLITS, KT, Q2W) for r in (highb, lowb))
            if q in META_TILES:
                lo, hi, _ = META_TILES[q]
                n = META_ORDER.index(q)
                if n >= 2:
                    pe.wait_ge(meta_read, n - 1)
                for k in range(KT):
                    three(ps[:, 6 + n % 2, 0:hi - lo], mT_hi[:, k, :], mT_lo[:, k, :], wh[:, k, lo:hi], wl[:, k, lo:hi],
                          k == 0, k == KT - 1)
            for k in range(KT):
                for b in range(NB):
                    mm = three(ps[:, 2 * (q % 2) + b, 0:Q2W], xT_hi[:, k, b * P:b * P + P], xT_lo[:, k, b * P:b * P + P],
                               wh[:, k, :], wl[:, k, :], k == 0, k == KT - 1)
            mm.then_inc(bw_used, 1)

        def read_of(q):
            if q < 8:
                return bz_read, 2 * q + 2
            if q == 8:
                return zs_made, 2
            pieces = [(k, t) for t in range(8, q + 1) for k, *_ in gates_of(t)]
            last = gates_of(q)[-1][0]
            count = 2 * sum(k == last for k, _ in pieces)
            return (zs_made, count) if last == "z" else (gs_made, count)

        for q in range(9):
            input_tile(q)
        pe.wait_ge(rope_made, 2)
        for n in range(10):
            if n >= 2:
                pe.wait_ge(qk_made, n - 1)
            bank = TP[n % 2]
            if n == 4:
                for t in range(4):
                    nc.tensor.transpose(ps[:, bank, t * META:t * META + META], meta_kv[0:META, t * P:t * P + P], ident[0:META, 0:META])
                for t in range(2):
                    mm = nc.tensor.transpose(ps[:, bank, (4 + t) * META:(5 + t) * META], swkm[:, t * P:t * P + P],
                                             ident[0:META, 0:META])
            else:
                for t in range(2):
                    for b in range(NB):
                        if n < 4:
                            first = (O_SBQ if n < 2 else O_SBK) + (2 * (n % 2) + t) * P
                            src = qkv[:, b, first:first + P]
                        elif n == 5:
                            src = swkk[:, b, t * P:t * P + P]
                        else:
                            first = O_SWQ + (2 * (n - 6) + t) * P
                            src = qkv[:, b, first:first + P]
                        mm = nc.tensor.transpose(ps[:, bank, (2 * t + b) * P:(2 * t + b + 1) * P], src, ident)
            mm.then_inc(qk_filled, 1)
        pe.wait_ge(qk_made, 10)
        pe.wait_ge(masks_made, 3)
        mmx = dict(skip_group_check=True)

        def sb_scores(p):
            s = 3 * (p % 2)
            if p >= 2:
                pe.wait_ge(sb_w_made, 2 * p - 2)
            for r in range(2):
                rows = slice(64 * r, 64 * r + 64)
                nc.tensor.matmul(ps[:, s + r, 0:T], sbkT[rows, p, 0:P], sbqT[rows, p, :], start=True, stop=False, **mmx)
                nc.tensor.matmul(ps[:, s + r, T:3 * P], sbkT[rows, p, P:T], sbqT[rows, p, P:T], start=False, stop=False, **mmx)
                nc.tensor.matmul(ps[:, s + r, 0:P], identb[:, :], sbm[:, :], start=False, stop=False, **mmx)
                nc.tensor.matmul(ps[:, s + r, T:3 * P], identb[:, :], sbm[:, :], start=False, stop=False, **mmx)
                mm = nc.tensor.matmul(ps[0:META, s + 2, r * T:r * T + T], sbkTm[:, p, r, :], sbqT[:, p, :],
                                      start=(r == 0), stop=False, **mmx)
            mm.then_inc(sbz_filled, 1)

        def sb_suffix(p):
            s = 3 * (p % 2)
            pe.wait_ge(sb_m_made, 2 * p + 2)
            for r in range(2):
                nc.tensor.matmul(ps[:, s + r, 0:T], upto, sb_m_[:, r, 0:T], start=False, stop=False, **mmx)
                nc.tensor.matmul(ps[:, s + r, T:3 * P], upto, sb_m_[:, r, T:3 * P], start=False, stop=False, **mmx)
                nc.tensor.matmul(ps[:, s + r, P:T], minus_ones, sb_m_[:, r, T:3 * P], start=False, stop=True, **mmx)
                c = r * T
                nc.tensor.matmul(ps[0:META, s + 2, c:c + T], upto[0:META, 0:META], sb_mm[:, c:c + T], start=False, stop=False, **mmx)
                nc.tensor.matmul(ps[0:META, s + 2, c:c + T], minus_ones[:, 0:META], sb_m_[:, r, 0:T], start=False, stop=False, **mmx)
                mm = nc.tensor.matmul(ps[0:META, s + 2, c + P:c + T], minus_ones[:, 0:META], sb_m_[:, r, T:3 * P],
                                      start=False, stop=True, **mmx)
            mm.then_inc(sbs_filled, 1)

        def sb_output(p):
            pe.wait_ge(sb_w_made, 2 * p + 2)
            for r in range(2):
                c = HD * (2 * p + r)
                v0, v1 = (qkv[:, b, O_SBV + c:O_SBV + c + HD] for b in range(NB))
                vm = meta_kv[0:META, 512 + c:512 + c + HD]
                o0, o1 = (ps[:, 6 + b, c:c + HD] for b in range(NB))
                nc.tensor.matmul(o0, sb_w[:, r, 0:P], v0, start=True, stop=False)
                nc.tensor.matmul(o0, sb_wm[:, r * T:r * T + P], vm, start=False, stop=True)
                nc.tensor.matmul(o1, sb_w[:, r, P:T], v0, start=True, stop=False)
                nc.tensor.matmul(o1, sb_w[:, r, T:3 * P], v1, start=False, stop=False)
                mm = nc.tensor.matmul(o1, sb_wm[:, r * T + P:r * T + T], vm, start=False, stop=True)
            mm.then_inc(sbo_filled, 1)

        sb_scores(0)
        sb_scores(1)
        for p in range(4):
            sb_suffix(p)
            sb_output(p)
            if p + 2 < 4:
                sb_scores(p + 2)

        def sw_scores(w):
            b, g = w // 2, w % 2
            if w:
                pe.wait_ge(prob_made, 8 * w)
            else:
                pe.wait_ge(sb_w_made, 8)
            for n in range(8):
                bank, c = sw_place(n)
                rows, tile = slice(64 * (n % 2), 64 * (n % 2) + 64), 4 * g + n // 2
                if c == 0:
                    nc.tensor.matmul(ps[:, bank, :].rearrange("p (u n) -> p u n", u=2), identb[:, :],
                                     swm[:, b:b + 1, :].to_broadcast([P, 2, T]), start=True, stop=False, **mmx)
                qT = swqT[rows, tile, b * P:b * P + P]
                if b == 0:
                    nc.tensor.matmul(ps[:, bank, c:c + META], qT, swkTm[rows, g, :], start=False, stop=False, **mmx)
                    mm = nc.tensor.matmul(ps[:, bank, c + P:c + T], qT, swkT[rows, g, 0:P], start=False, stop=True, **mmx)
                else:
                    mm = nc.tensor.matmul(ps[:, bank, c:c + T], qT, swkT[rows, g, :], start=False, stop=True, **mmx)
            mm.then_inc(sc_filled, 1)

        def pt_fill(w, fl):
            k = 4 * w + fl
            if k >= 2:
                pe.wait_ge(pt_act if k % 2 == 0 else pt_dve, k // 2)
            else:
                pe.wait_ge(qk_made, 10)
            pe.wait_ge(prob_made, 8 * w + 2 * fl + 2)
            for n in range(2):
                for kb in range(2):
                    mm = nc.tensor.transpose(ps[:, TP[k % 2], (2 * n + kb) * P:(2 * n + kb + 1) * P],
                                             prob[:, 2 * fl + n, kb * P:kb * P + P], ident)
            mm.then_inc(pt_filled, 1)

        def sw_output(w, fl):
            b, g = w // 2, w % 2
            k = 4 * w + fl
            pe.wait_ge(pt_act if k % 2 == 0 else pt_dve, k // 2 + 1)
            if fl == 0:
                if w >= 2:
                    pe.wait_ge(swo_made, w - 1)
                else:
                    pe.wait_ge(sbo_made, w + 1)
            vc = O_SWV + HD * g
            for n in range(2):
                c = HD * (2 * fl + n)
                o = ps[:, 6 + w % 2, c:c + HD]
                if b == 0:
                    nc.tensor.matmul(o, pt[0:META, k % 2, 2 * n * P:2 * n * P + P], meta_kv[0:META, 1152 + HD * g:1152 + HD * g + HD],
                                     start=True, stop=False)
                else:
                    nc.tensor.matmul(o, pt[:, k % 2, 2 * n * P:2 * n * P + P], qkv[:, 0, vc:vc + HD], start=True, stop=False)
                mm = nc.tensor.matmul(o, pt[:, k % 2, (2 * n + 1) * P:(2 * n + 2) * P], qkv[:, b, vc:vc + HD],
                                      start=False, stop=True)
            mm.then_inc(pv_done, 1)

        for w in range(4):
            sw_scores(w)
            pt_fill(w, 0)
            pt_fill(w, 1)
            sw_output(w, 0)
            pt_fill(w, 2)
            sw_output(w, 1)
            pt_fill(w, 3)
            sw_output(w, 2)
            sw_output(w, 3)
        for q in range(9, BCH_IN):
            input_tile(q)
            if q == 12:
                pe.wait_ge(zmul_made, 1 + sum(k == "z" for t in range(9, 11) for k, *_ in gates_of(t)))
                for m in range(2):
                    for t in range(2):
                        for b in range(NB):
                            first = SBO + (2 * m + t) * P
                            mm = nc.tensor.transpose(ps[:, TP[m], (2 * t + b) * P:(2 * t + b + 1) * P], qkv[:, b, first:first + P], ident)
                    mm.then_inc(ot_filled, 1)
        pe.wait_ge(zmul_made, sum(k == "z" for t in range(8, BCH_IN) for k, *_ in gates_of(t)))
        pe.wait_ge(ot_lo, 2)
        big_transposes(lambda b, k: qkv[:, b, SWO + k * P:SWO + k * P + P])
        pe.wait_ge(xt_lo, 24)

        def branch(c, tiles, hT, lT, acc, first, last):
            pe.wait_ge(blo_made, c + 1)
            row_product(hT, lT, tiles, c % SPLITS, acc, NB, first, last, (highb, lowb)).then_inc(bw_used, 1)

        def down_bank(b, half):
            return DOWN[2 * b + half]

        pe.wait_ge(*read_of(19))
        pe.wait_ge(*read_of(18))
        for n in range(BCH_SB):
            branch(BCH_IN + n, (2 * n, 2 * n + 1), sbT_hi, sbT_lo, down_bank, n == 0, n == BCH_SB - 1)
        for n in range(BCH_SW):
            branch(BCH_IN + BCH_SB + n, (2 * n, 2 * n + 1), xT_hi, xT_lo, merge_bank, n == 0, n == BCH_SW - 1)
        pe.wait_ge(merged_made, 8)
        big_transposes(lambda b, k: merged[:, b, k * P:k * P + P])
        pe.wait_ge(xt_lo, 28)
        for n in range(BCH_OUT):
            branch(26 + n, (2 * n, 2 * n + 1), xT_hi, xT_lo, down_bank, n == 0, n == BCH_OUT - 1)

    def big_transposes(src):
        for m in range(4):
            for kk in range(2):
                for b in range(NB):
                    mm = nc.tensor.transpose(ps[:, 4 + m, (2 * kk + b) * P:(2 * kk + b + 1) * P], src(b, 2 * m + kk), ident)
            mm.then_inc(xt_filled, 1)

    DENSE_AFTER = {2: (0,), 4: (1,), 6: (2, 3), 8: (4,), 10: (5,), 12: (6, 7), 14: (8,), 16: (9, 10)}

    def dense_free(q):
        return -(-(-(-TW * (q - 3) // P)) // 2)

    def dense_transposes(pe, j):
        for m in DENSE_AFTER.get(j, ()):
            pe.wait_ge(mult_made, 2 * (-(-(2 * m + 2) * P // TW)))
            if m >= 2:
                pe.wait_ge(ht_lo, m - 1)
            for kk in range(2):
                t = (2 * m + kk) % (4 * TW // P)
                for b in range(NB):
                    mm = nc.tensor.transpose(ps[:, TP[m % 2], (2 * kk + b) * P:(2 * kk + b + 1) * P],
                                             h[:, b, t * P:t * P + P], ident)
            mm.then_inc(ht_filled, 1)

    with nc.Block() as block:

        @block.sync
        def _(sp):
            c = 0
            for l in range(2):
                for j in range(MIX_CHUNKS):
                    load(sp, c, mixer_source(l, j))
                    c += 1
                if l == 0:
                    for j in range(FFN_CHUNKS):
                        load(sp, c, ffn_source(j))
                        c += 1
            for j in range(FFN_CHUNKS):
                load(sp, c, expert_source(0, j))
                c += 1
            with sp.Fori(1, NE) as i:
                for j in range(FFN_CHUNKS):
                    load_item(sp, i, j, expert_source(i, j))
            sp.wait_ge(routed, 1)
            n_items = sp.value_load(plan[0:1, 3:4], min_val=NE - 1, max_val=ITEMS - 1) + 1
            with sp.Fori(NE, ITEMS) as i:
                with sp.If(i < n_items):
                    e = sp.value_load(plan[0:1, bass.ds(i - NE, 1)], min_val=0, max_val=NE - 1)
                    for j in range(FFN_CHUNKS):
                        load_item(sp, i, j, expert_source(e, j))
            second_loads(sp, n_items)

        @block.gpsimd
        def _(pool):
            pool.dma_start(x[:, :, :], a["x"][0].rearrange("(b p) d -> p b d", p=P)).then_inc(x_landed, 16)
            pool.dma_start(small[:, :], a["c_small"]).then_inc(small_landed, 16)

            def load_gain(n, src):
                if n:
                    pool.wait_ge(xn_made, 2 * n)
                pool.dma_start(gain[:, :], src.to_broadcast([P, D])).then_inc(gain_landed, 16)

            def load_mix(l):
                rows = rows16[:, :]
                pool.dma_start(cmix[:, :], a["c_mix"]).then_inc(mix_landed, 16)
                pool.dma_start(rows[0:4, :], a["sgu_b"][l]).then_inc(mix_landed, 16)
                for n, name in enumerate(("conv_b", "conv_ng", "conv_nb")):
                    pool.dma_start(rows[4 + 4 * n:8 + 4 * n, :], a[name][l].rearrange("(t p) -> t p", p=P)).then_inc(mix_landed, 16)
                pool.dma_start(conv_rows[:, :], a["conv_w"][l, :, 0, :]).then_inc(mix_landed, 16)
                pool.dma_start(sgu_rows[:, :, :], a["sgu_w"][l].rearrange("h t s -> t h s")).then_inc(mix_landed, 16)
                pool.dma_start(sgu_g[:, :], a["sgu_ng"][l:l + 1, :].to_broadcast([P, CC])).then_inc(mix_landed, 16)
                pool.dma_start(sgu_o[:, :], a["sgu_nb"][l:l + 1, :].to_broadcast([P, CC])).then_inc(mix_landed, 16)

            def sgu_gain(l):
                for b in range(NB):
                    pool.wait_ge(vnorm_made, NB * SH * l + SH * (b + 1))
                    pool.tensor_tensor(v[:, b, :], v[:, b, :], sgu_g[:, :], ALU.mult).then_inc(vg_made, 1)
                    pool.wait_ge(vg_made, NB * l + b + 1)
                    pool.tensor_tensor(v[:, b, :], v[:, b, :], sgu_o[:, :], ALU.add).then_inc(vn_made, 1)

            load_gain(0, a["norm_mix"][0:1, :])
            load_mix(0)
            pool.wait_ge(mix_landed, 16 * 9)
            sgu_gain(0)
            load_gain(1, a["norm_ffn"][0:1, :])
            load_gain(2, a["norm_mix"][1:2, :])
            pool.wait_ge(x_made, 8)
            load_mix(1)
            pool.wait_ge(mix_landed, 16 * 18)
            sgu_gain(1)
            load_gain(3, a["norm_ffn"][1:2, :])
            pool.wait_ge(x_made, 12)
            pool.dma_start(croute[:, :], a["c_route"]).then_inc(route_landed, 16)
            pool.dma_start(router[:, :, :], a["moe_router"][0].rearrange("(t p) e -> p t e", p=P)).then_inc(route_landed, 16)
            load_gain(4, a["norm_final"].rearrange("(o d) -> o d", o=1))
            load_gain(5, a["norm_gain_2"][0:1, :])
            second_small_loads(pool)
            pool.wait_ge(meta_made, 1)
            load_gain(6, a["final_norm_gain_2"].rearrange("(o d) -> o d", o=1))

        @block.scalar
        def _(act):
            made = [0]

            def high_upto(c):
                while made[0] <= c:
                    make_high(act, made[0])
                    made[0] += 1

            def norm_stats(n):
                nc.scalar.activation(xn[:, 0, :], x[:, 0, :], ACT.Square, accum_out=sumsq[:, 0:1]).then_inc(sumsq_made, 1)
                act.wait_ge(sumsq_made, 2 * n + 2)
                nc.scalar.activation(std[:, :], sumsq[:, :], ACT.Sqrt, bias=eps[:, 0:1], scale=1.0 / D).then_inc(std_made, 1)

            def norm_high(tn):
                for m in range(4):
                    act.wait_ge(xt_filled, 4 * tn + m + 1)
                    nc.scalar.activation(xT_hi[:, 2 * m:2 * m + 2, :], ps[:, 4 + m, :].rearrange("p (t n) -> p t n", t=2),
                                         ACT.Copy).then_inc(xt_hi, 1)

            def mixer(l):
                c0 = LAYER_CHUNKS * l
                high_upto(c0 + 3)
                for b in range(NB):
                    act.wait_ge(w_used, c0 + 2)
                    nc.scalar.activation(sig[:, b, :], ps[:, b, :], ACT.Sigmoid).then_inc(sig_made, 1)
                high_upto(c0 + 7)
                for b in range(NB):
                    act.wait_ge(w_used, c0 + 6)
                    nc.scalar.activation(u[:, b, :], ps[:, b, :], ACT.Gelu).then_inc(u_made, 1)
                for m in range(2):
                    act.wait_ge(ct_filled, 2 * l + m + 1)
                    nc.scalar.activation(cT[:, 2 * m:2 * m + 2, TAPS - 1:], ps[:, TP[m], :].rearrange("p (t n) -> p t n", t=2),
                                         ACT.Copy).then_inc(ct_made, 1)
                high_upto(c0 + 8)
                for b in range(NB):
                    act.wait_ge(w_used, c0 + 8)
                    nc.scalar.activation(v[:, b, :], ps[:, 2 + b, :], ACT.Gelu).then_inc(v_made, 1)
                high_upto(c0 + 10)
                act.wait_ge(vvar_made, NB * SH * (l + 1))
                nc.scalar.activation(vstd[:, :], vmv[:, :, 1], ACT.Sqrt, bias=eps[:, 0:1]).then_inc(vstd_made, 1)
                for n in range(NB * SH):
                    act.wait_ge(vnorm_ready, l + 1)
                    b, hh = n // SH, n % SH
                    part = v[:, b, hh * P:hh * P + P]
                    nc.scalar.activation(part, part, ACT.Identity, bias=vmv[:, n, 0:1], scale=vrstd[:, n:n + 1]).then_inc(vnorm_made, 1)
                for m in range(2):
                    act.wait_ge(gt_filled, 2 * l + m + 1)
                    nc.scalar.activation(xT_hi[:, 4 + 2 * m:6 + 2 * m, :], ps[:, TP[m], :].rearrange("p (t n) -> p t n", t=2),
                                         ACT.Copy).then_inc(cat_hi, 1)
                high_upto(c0 + 11)
                for m in range(2):
                    act.wait_ge(yc_filled, 2 * l + m + 1)
                    nc.scalar.activation(sq[:, 2 * m:2 * m + 2, :], ps[:, TP[m], :].rearrange("p (t n) -> p t n", t=2),
                                         ACT.Square).then_inc(sq_made, 1)
                act.wait_ge(var_filled, l + 1)
                nc.scalar.activation(std8[:, :], ps[0:8, 2, 0:T], ACT.Sqrt, bias=eps[0:8, 0:1]).then_inc(std8_made, 1)
                for m in range(2):
                    act.wait_ge(yn_made, 2 * l + m + 1)
                    for t in (2 * m, 2 * m + 1):
                        ins = nc.scalar.activation(sq[:, t, :], yT[:, t, :], ACT.Silu, scale=cols[:, 8 + t:9 + t],
                                                   bias=cols[:, 12 + t:13 + t])
                        ins.then_inc(cs_made, 1)
                    act.wait_ge(cs_made, 4 * l + 2 * m + 2)
                    nc.scalar.activation(xT_hi[:, 2 * m:2 * m + 2, :], sq[:, 2 * m:2 * m + 2, :], ACT.Copy).then_inc(cat_hi, 1)

            act.wait_ge(small_landed, 16)
            act.wait_ge(eps_made, 1)
            act.wait_ge(x_landed, 16)
            norm_stats(0)
            high_upto(0)
            norm_high(0)
            mixer(0)
            c0 = MIX_CHUNKS
            high_upto(c0 + 1)
            act.wait_ge(x_made, 4)
            norm_stats(1)
            norm_high(1)

            def dense_silu(q):
                for b in range(NB):
                    act.wait_ge(w_used, MIX_CHUNKS + 2 * q + 1)
                    if q >= 4:
                        act.wait_ge(ht_filled, dense_free(q))
                    nc.scalar.activation(h[:, b, (q % 4) * TW:(q % 4) * TW + TW], ps[:, b, :][:, 0:TW], ACT.Silu).then_inc(silu_made, 1)

            def dense_hidden_high(m):
                act.wait_ge(ht_filled, m + 1)
                nc.scalar.activation(hT_hi[:, 2 * m:2 * m + 2, :], ps[:, TP[m % 2], :].rearrange("p (t n) -> p t n", t=2),
                                     ACT.Copy).then_inc(ht_hi, 1)

            for j in range(FFN_CHUNKS):
                high_upto(c0 + min(j + 2, FFN_CHUNKS + 1))
                if j < 16 and j % 2 == 0:
                    dense_silu(j // 2)
                for m in DENSE_AFTER.get(j, ()):
                    dense_hidden_high(m)
            act.wait_ge(x_made, 8)
            norm_stats(2)
            norm_high(2)
            mixer(1)
            high_upto(MOE0 + 1)
            act.wait_ge(x_made, 12)
            norm_stats(3)
            norm_high(3)
            act.wait_ge(route_landed, 32)
            nc.scalar.activation(router_hi[:, :, :], router[:, :, :], ACT.Copy).then_inc(router_split, 1)
            act.wait_ge(logit_made, 1)
            nc.scalar.activation(share[:, :, :], share[:, :, :], ACT.Exp).then_inc(expo_made, 1)
            for b in range(NB):
                nc.scalar.activation(xn_hi[:, b, :], xn[:, b, :], ACT.Copy).then_inc(xs_hi, 1)

            def item(i, mh, finish):
                first = isinstance(i, int)
                if not first:
                    mh(i, 0)
                    mh(i, 1)
                for p in range(4):
                    act.wait_ge(tp_filled, fill_no(i, p) + 1)
                    nc.scalar.activation(xe_hi[:, p * 2 * P:(p + 1) * 2 * P], ps[:, TP[p % 2], 0:2 * P], ACT.Copy).then_inc(tp_hi, 1)
                if not first:
                    finish(i)
                mh(i, 2)
                for j in range(3, FFN_CHUNKS + 2):
                    if j < FFN_CHUNKS:
                        mh(i, j)
                    c = j - 2
                    if c < 16 and c % 4 == 1:
                        g = c // 4
                        act.wait_ge(w_used, chunk(i, c) + 1)
                        for t in range(2):
                            nc.scalar.activation(eh[:, g * GW + t * TW:g * GW + t * TW + TW], ps[:, t, 0:TW],
                                                 ACT.Silu).then_inc(esilu_made, 1)
                    if c in AFTER_T:
                        n = AFTER_T[c]
                        lo, hi = BATCHES[n]
                        act.wait_ge(tp_filled, fill_no(i, 10 + n) + 1)
                        nc.scalar.activation(eT_hi[:, lo:hi, :].rearrange("p t n -> p (t n)"),
                                             ps[:, TP[n % 2], 0:(hi - lo) * P], ACT.Copy).then_inc(tp_hi, 1)

            def finish(i):
                act.wait_ge(w_used, chunk(i, 0))
                for half in range(2):
                    nc.scalar.activation(eo_hi[:, half * 512:half * 512 + 512], ps[:, 6 + half, :], ACT.Copy).then_inc(eo_hi_made, 1)

            def static_high(i, j):
                if chunk(0, j) >= made[0]:
                    high_upto(chunk(0, j))

            def high_item(i, j):
                make_high_item(act, i, j)

            item(0, static_high, finish)
            with act.Fori(1, NE) as i:
                item(i, high_item, finish)
            act.wait_ge(routed, 1)
            n_items = act.value_load(plan[0:1, 3:4], min_val=NE - 1, max_val=ITEMS - 1) + 1
            with act.Fori(NE, ITEMS) as i:
                with act.If(i < n_items):
                    item(i, high_item, finish)
            finish(n_items)
            second_scalar(act, n_items, norm_stats, norm_high)

        @block.vector
        def _(dve):
            made = [0]
            steps = [0]

            def low_upto(c):
                while made[0] <= c:
                    make_low(dve, made[0])
                    made[0] += 1

            def step(ins):
                steps[0] += 1
                ins.then_inc(dve_steps, 1)
                dve.wait_ge(dve_steps, steps[0])

            def norm_apply(n, target):
                nc.vector.tensor_tensor_reduce(out=xn[:, 1, :], in0=x[:, 1, :], in1=x[:, 1, :], scale=1.0, scalar=0.0,
                                               op0=ALU.mult, op1=ALU.add, accum_out=sumsq[:, 1:2]).then_inc(sumsq_made, 1)
                dve.wait_ge(std_made, n + 1)
                nc.vector.reciprocal(rstd[:, :], std[:, :]).then_inc(rstd_made, 1)
                dve.wait_ge(rstd_made, n + 1)
                dve.wait_ge(gain_landed, 16 * (n + 1))
                for b in range(NB):
                    nc.vector.scalar_tensor_tensor(target[:, b, :], x[:, b, :], rstd[:, b:b + 1], gain[:, :], ALU.mult,
                                                   ALU.mult).then_inc(xn_made, 1)

            def norm_low(tn):
                for m in range(4):
                    dve.wait_ge(xt_hi, 4 * tn + m + 1)
                    nc.vector.tensor_tensor(xT_lo[:, 2 * m:2 * m + 2, :], ps[:, 4 + m, :].rearrange("p (t n) -> p t n", t=2),
                                            f(xT_hi[:, 2 * m:2 * m + 2, :]), ALU.subtract).then_inc(xt_lo, 1)

            def add_output(count):
                for b in range(NB):
                    for half in range(2):
                        part = x[:, b, half * 512:half * 512 + 512]
                        dve.wait_ge(w_used, count)
                        nc.vector.tensor_tensor(part, part, ps[:, DOWN[2 * b + half], :], ALU.add).then_inc(x_made, 1)

            def mixer(l):
                c0 = LAYER_CHUNKS * l
                low_upto(c0 + 4)
                dve.wait_ge(prep_filled, 2 * l + 2)
                nc.vector.tensor_copy(cols[:, :], ps[:, 6, 0:16 + CT * TAPS]).then_inc(prep_made, 1)
                nc.vector.tensor_tensor(wsT[:, :, :], ps[:, 7, :].rearrange("p (h t) -> p h t", h=SH),
                                        causal.rearrange("p (o t) -> p o t", o=1).to_broadcast([P, SH, P]),
                                        ALU.mult).then_inc(prep_made, 1)
                low_upto(c0 + 5)
                for b in range(NB):
                    dve.wait_ge(w_used, c0 + 4)
                    dve.wait_ge(sig_made, 2 * l + b + 1)
                    nc.vector.tensor_tensor(c_tok[:, b, :], sig[:, b, :], ps[:, 2 + b, :], ALU.mult).then_inc(c_made, 1)
                nc.vector.memset(cT[:, :, 0:TAPS - 1], 0.0).then_inc(pad_made, 1)
                dve.wait_ge(pad_made, l + 1)
                low_upto(c0 + 8)
                dve.wait_ge(prep_made, 2 * l + 2)
                base = CT * TAPS * l

                def conv(first_tap, last_tap):
                    for k in range(first_tap, last_tap):
                        for t in range(CT):
                            n = base + CT * k + t
                            w = cols[:, 16 + TAPS * t + k:17 + TAPS * t + k]
                            src = cT[:, t, k:k + T]
                            if k == 0:
                                dve.wait_ge(ct_made, 2 * l + t // 2 + 1)
                                ins = nc.vector.tensor_scalar(yT[:, t, :], src, w, cols[:, 4 + t:5 + t], ALU.mult, ALU.add)
                            else:
                                dve.wait_ge(conv_step, n - CT + 1)
                                ins = nc.vector.scalar_tensor_tensor(yT[:, t, :], src, w, yT[:, t, :], ALU.mult, ALU.add)
                            ins.then_inc(conv_step, 1)

                conv(0, 8)
                for n in range(NB * SH):
                    b, hh = n // SH, n % SH
                    dve.wait_ge(v_made, 2 * l + b + 1)
                    nc.vector.bn_stats(vstat[:, n, :], v[:, b, hh * P:hh * P + P]).then_inc(vvar_stats, 1)
                for n in range(NB * SH):
                    dve.wait_ge(vvar_stats, NB * SH * l + n + 1)
                    nc.vector.bn_aggr(vmv[:, n, :], vstat[:, n, :]).then_inc(vvar_made, 1)
                low_upto(c0 + 10)
                dve.wait_ge(vstd_made, l + 1)
                step(nc.vector.reciprocal(vrstd[:, :], vstd[:, :]))
                nc.vector.scalar_tensor_tensor(vmv[:, :, 0], vmv[:, :, 0], -1.0, vrstd[:, :], ALU.mult,
                                               ALU.mult).then_inc(vnorm_ready, 1)
                conv(8, 20)
                for b in range(NB):
                    dve.wait_ge(sp_filled, 2 * l + b + 1)
                    dve.wait_ge(u_made, 2 * l + b + 1)
                    for hh in range(SH):
                        part = u[:, b, hh * P:hh * P + P]
                        ins = nc.vector.scalar_tensor_tensor(part, ps[:, 2 + b, hh * P:hh * P + P], cols[:, hh:hh + 1], part,
                                                             ALU.add, ALU.mult)
                    ins.then_inc(g_made, 1)
                conv(20, 24)
                for m in range(2):
                    dve.wait_ge(cat_hi, 4 * l + m + 1)
                    nc.vector.tensor_tensor(xT_lo[:, 4 + 2 * m:6 + 2 * m, :], ps[:, TP[m], :].rearrange("p (t n) -> p t n", t=2),
                                            f(xT_hi[:, 4 + 2 * m:6 + 2 * m, :]), ALU.subtract).then_inc(cat_lo, 1)
                conv(24, TAPS)
                low_upto(c0 + 11)
                for m in range(2):
                    dve.wait_ge(sq_made, 2 * l + m + 1)
                    nc.vector.tensor_copy(yT[:, 2 * m:2 * m + 2, :], ps[:, TP[m], :].rearrange("p (t n) -> p t n", t=2)
                                          ).then_inc(yc_made, 1)
                dve.wait_ge(std8_made, l + 1)
                nc.vector.reciprocal(rstd8[:, :], std8[:, :]).then_inc(rstd8_made, 1)
                for m in range(2):
                    dve.wait_ge(rb_filled, 2 * l + m + 1)
                    dve.wait_ge(yc_made, 2 * l + m + 1)
                    nc.vector.tensor_tensor(yT[:, 2 * m:2 * m + 2, :], yT[:, 2 * m:2 * m + 2, :],
                                            ps[:, 3 - m, :].rearrange("p (t n) -> p t n", t=2), ALU.mult).then_inc(yn_made, 1)
                for m in range(2):
                    dve.wait_ge(cat_hi, 4 * l + 3 + m)
                    nc.vector.tensor_tensor(xT_lo[:, 2 * m:2 * m + 2, :], sq[:, 2 * m:2 * m + 2, :],
                                            f(xT_hi[:, 2 * m:2 * m + 2, :]), ALU.subtract).then_inc(cat_lo, 1)
                low_upto(c0 + 13)
                add_output(c0 + MIX_CHUNKS)

            nc.vector.memset(eps[:, :], EPS).then_inc(eps_made, 1)
            dve.wait_ge(x_landed, 16)
            norm_apply(0, xn)
            low_upto(0)
            norm_low(0)
            mixer(0)
            dve.wait_ge(x_made, 4)
            norm_apply(1, xn)
            norm_low(1)
            c0 = MIX_CHUNKS

            for j in range(FFN_CHUNKS):
                low_upto(c0 + min(j + 2, FFN_CHUNKS + 1))
                if j < 16 and j % 2 == 1:
                    q = j // 2
                    for b in range(NB):
                        dve.wait_ge(w_used, MIX_CHUNKS + 2 * q + 2)
                        dve.wait_ge(silu_made, 2 * q + b + 1)
                        part = h[:, b, (q % 4) * TW:(q % 4) * TW + TW]
                        nc.vector.tensor_tensor(part, part, ps[:, 2 + b, 0:TW], ALU.mult).then_inc(mult_made, 1)
                for m in DENSE_AFTER.get(j, ()):
                    dve.wait_ge(ht_hi, m + 1)
                    nc.vector.tensor_tensor(hT_lo[:, 2 * m:2 * m + 2, :], ps[:, TP[m % 2], :].rearrange("p (t n) -> p t n", t=2),
                                            f(hT_hi[:, 2 * m:2 * m + 2, :]), ALU.subtract).then_inc(ht_lo, 1)
            add_output(LAYER_CHUNKS)
            dve.wait_ge(x_made, 8)
            norm_apply(2, xn)
            norm_low(2)
            mixer(1)
            dve.wait_ge(x_made, 12)
            norm_apply(3, xn)
            norm_low(3)
            dve.wait_ge(router_split, 1)
            nc.vector.tensor_tensor(router_lo[:, :, :], router[:, :, :], f(router_hi[:, :, :]), ALU.subtract).then_inc(router_split, 1)
            dve.wait_ge(logits_ready, 1)
            step(nc.vector.tensor_copy(logit[:, :, :], ps[:, 0, 0:NB * NE].rearrange("p (b e) -> p b e", b=NB)))
            step(nc.vector.tensor_reduce(top[:, :], logit[:, :, :], AX.X, ALU.max))
            nc.vector.tensor_tensor(share[:, :, :], logit[:, :, :],
                                    top[:, :].rearrange("p (b o) -> p b o", o=1).to_broadcast([P, NB, NE]),
                                    ALU.subtract).then_inc(logit_made, 1)
            for b in range(NB):
                other = logit[:, b:b + 1, :].to_broadcast([P, NE, NE])
                own = logit[:, b, :].rearrange("p (e o) -> p e o", o=1).to_broadcast([P, NE, NE])
                nc.vector.tensor_tensor(above[:, b, :, :], other, own, ALU.is_gt)
                step(nc.vector.tensor_tensor(equal[:, b, :, :], other, own, ALU.is_equal))
                step(nc.vector.tensor_tensor(equal[:, b, :, :], equal[:, b, :, :], earlier, ALU.mult))
                step(nc.vector.tensor_tensor(above[:, b, :, :], above[:, b, :, :], equal[:, b, :, :], ALU.add))
                step(nc.vector.tensor_reduce(rank[:, b, :], above[:, b, :, :], AX.X, ALU.add))
            nc.vector.tensor_scalar(chosen[:, :, :], rank[:, :, :], 1.5, None, ALU.is_lt).then_inc(chosen_made, 1)
            dve.wait_ge(chosen_made, 1)
            dve.wait_ge(expo_made, 1)
            step(nc.vector.tensor_tensor(share[:, :, :], share[:, :, :], chosen[:, :, :], ALU.mult))
            step(nc.vector.tensor_reduce(total[:, :], share[:, :, :], AX.X, ALU.add))
            step(nc.vector.reciprocal(total[:, :], total[:, :]))
            step(nc.vector.tensor_tensor(share[:, :, :], share[:, :, :],
                                         total[:, :].rearrange("p (b o) -> p b o", o=1).to_broadcast([P, NB, NE]), ALU.mult))
            dve.wait_ge(places_ready, 1)
            step(nc.vector.scalar_tensor_tensor(place_in[:, :, :], ps[:, 1, 0:NB * NE].rearrange("p (b e) -> p b e", b=NB), 1.0,
                                                chosen[:, :, :], ALU.add, ALU.mult))
            step(nc.vector.tensor_scalar(place_in[:, :, :], place_in[:, :, :], -1.0, None, ALU.add))
            step(nc.vector.tensor_scalar(crowd[:, :], ps[:, 1, NB * NE:(NB + 1) * NE], P + 0.5, None, ALU.is_gt))
            for b in range(NB):
                step(nc.vector.tensor_copy(items[:, 0:NE, b], place_in[:, b, :]))
                step(nc.vector.tensor_copy(items[:, 0:NE, 2 + b], share[:, b, :]))
            step(nc.vector.tensor_tensor(crowds[:, :, :], crowd[:, :].rearrange("p (o e) -> p o e", o=1).to_broadcast([P, NE, NE]),
                                         earlier, ALU.mult))
            step(nc.vector.tensor_reduce(crowd_at[:, :], crowds[:, :, :], AX.X, ALU.add))
            for k in range(ITEMS - NE):
                step(nc.vector.scalar_tensor_tensor(which[:, k, :], crowd_at[:, :], float(k), crowd[:, :], ALU.is_equal, ALU.mult))
                for n, row in enumerate((place_in[:, 0, :], place_in[:, 1, :], share[:, 0, :], share[:, 1, :])):
                    step(nc.vector.tensor_tensor_reduce(out=dots[:, k, n, :], in0=which[:, k, :], in1=row, scale=1.0, scalar=0.0,
                                                        op0=ALU.mult, op1=ALU.add, accum_out=items[:, NE + k, n:n + 1]))
                step(nc.vector.tensor_tensor_reduce(out=dots[:, k, 4, :], in0=which[:, k, :], in1=number, scale=1.0, scalar=0.0,
                                                    op0=ALU.mult, op1=ALU.add, accum_out=planf[:, k:k + 1]))
            step(nc.vector.tensor_scalar(items[:, NE:ITEMS, 0:NB], items[:, NE:ITEMS, 0:NB], -float(P), None, ALU.add))
            step(nc.vector.tensor_reduce(planf[:, 3:4], crowd[:, :], AX.X, ALU.add))
            step(nc.vector.tensor_scalar(planf[:, 3:4], planf[:, 3:4], float(NE - 1), None, ALU.add))
            nc.vector.tensor_copy(plan[:, :], planf[:, :]).then_inc(routed, 1)
            for b in range(NB):
                dve.wait_ge(xs_hi, b + 1)
                nc.vector.tensor_tensor(xn_lo[:, b, :], xn[:, b, :], f(xn_hi[:, b, :]), ALU.subtract).then_inc(xs_lo, 1)

            def add_scattered(pos, half):
                for b in range(NB):
                    part = x[:, b, half * 512:half * 512 + 512]
                    dve.wait_ge(tp_filled, pos + b + 1)
                    nc.vector.scalar_tensor_tensor(part, ps[:, TP[b], :], gates_now[:, b:b + 1], part, ALU.mult,
                                                   ALU.add).then_inc(tp_freed, 1)

            def finish(i):
                for half in range(2):
                    dve.wait_ge(eo_hi_made, 2 * i + half - 1)
                    nc.vector.tensor_tensor(eo_lo[:, half * 512:half * 512 + 512], ps[:, 6 + half, :],
                                            f(eo_hi[:, half * 512:half * 512 + 512]), ALU.subtract).then_inc(eo_lo_made, 1)

            def item(i, ml):
                first = isinstance(i, int)
                ml(i, 0)
                row = items[:, i:i + 1, :] if first else items[:, bass.ds(i, 1), :]
                if not first:
                    dve.wait_ge(tp_filled, fill_no(i, 0))
                nc.vector.tensor_copy(now[:, :], row[:, 0, 0:2]).then_inc(now_made, 1)
                dve.wait_ge(now_made, 2 * i + 1)
                for b in range(NB):
                    nc.vector.tensor_scalar(pick[:, b, :], iota, now[:, b:b + 1], None, ALU.is_equal).then_inc(pick_made, 1)
                ml(i, 1)
                for p in range(4):
                    dve.wait_ge(tp_hi, 10 * i + p + 1)
                    nc.vector.tensor_copy(xe_lo[:, p * 2 * P:(p + 1) * 2 * P], ps[:, TP[p % 2], 2 * P:4 * P]).then_inc(tp_freed, 1)
                if not first:
                    finish(i)
                ml(i, 2)
                for j in range(3, FFN_CHUNKS + 2):
                    if j < FFN_CHUNKS:
                        ml(i, j)
                    c = j - 2
                    if c < 16 and c % 4 == 3:
                        g = c // 4
                        dve.wait_ge(w_used, chunk(i, c) + 1)
                        for t in range(2):
                            dve.wait_ge(esilu_made, 8 * i + 2 * g + t + 1)
                            part = eh[:, g * GW + t * TW:g * GW + t * TW + TW]
                            nc.vector.tensor_tensor(part, part, ps[:, 2 + t, 0:TW], ALU.mult).then_inc(emult_made, 1)
                    if c == 3 and not first:
                        add_scattered(fill_no(i, 4), 0)
                    if c == 4 and not first:
                        add_scattered(fill_no(i, 6), 1)
                    if c == 4:
                        if not first:
                            dve.wait_ge(tp_freed, fill_no(i, 7) + 1)
                        nc.vector.tensor_copy(gates_now[:, :], row[:, 0, 2:4]).then_inc(now_made, 1)
                        dve.wait_ge(now_made, 2 * i + 2)
                    if c == 5:
                        for b in range(NB):
                            dve.wait_ge(tp_filled, fill_no(i, 8 + b) + 1)
                            nc.vector.tensor_copy(drop[:, b, :], ps[:, TP[b], 0:P]).then_inc(tp_freed, 1)
                    if c in AFTER_T:
                        n = AFTER_T[c]
                        lo, hi = BATCHES[n]
                        dve.wait_ge(tp_hi, 10 * i + 4 + n + 1)
                        nc.vector.tensor_tensor(eT_lo[:, lo:hi, :].rearrange("p t n -> p (t n)"), ps[:, TP[n % 2], 0:(hi - lo) * P],
                                                f(eT_hi[:, lo:hi, :]).rearrange("p t n -> p (t n)"),
                                                ALU.subtract).then_inc(tp_freed, 1)

            def static_low(i, j):
                if chunk(0, j) >= made[0]:
                    low_upto(chunk(0, j))

            def low_item(i, j):
                make_low_item(dve, i, j)

            item(0, static_low)
            with dve.Fori(1, NE) as i:
                item(i, low_item)
            dve.wait_ge(routed, 1)
            n_items = dve.value_load(plan[0:1, 3:4], min_val=NE - 1, max_val=ITEMS - 1) + 1
            with dve.Fori(NE, ITEMS) as i:
                with dve.If(i < n_items):
                    item(i, low_item)
            finish(n_items)
            add_scattered(fill_no(n_items, 0), 0)
            add_scattered(fill_no(n_items, 2), 1)
            second_vector(dve, n_items, step, norm_apply, norm_low)

        @block.tensor
        def _(pe):
            def norm_transposes(n, tn):
                pe.wait_ge(xn_made, 2 * n + 2)
                for m in range(4):
                    for kk in range(2):
                        for b in range(NB):
                            k = 2 * m + kk
                            mm = nc.tensor.transpose(ps[:, 4 + m, (2 * kk + b) * P:(2 * kk + b + 1) * P],
                                                     xn[:, b, k * P:k * P + P], ident)
                    mm.then_inc(xt_filled, 1)
                pe.wait_ge(xt_lo, 4 * tn + 4)

            def token_transposes(src, banks, count):
                for m in range(2):
                    for kk in range(2):
                        for b in range(NB):
                            t = 2 * m + kk
                            mm = nc.tensor.transpose(ps[:, banks[m], (2 * kk + b) * P:(2 * kk + b + 1) * P],
                                                     src[:, b, t * P:t * P + P], ident)
                    mm.then_inc(count, 1)

            def mixer(l):
                c0 = LAYER_CHUNKS * l
                for j in range(8):
                    c = c0 + j
                    q, kh = j // 2, j % 2
                    pe.wait_ge(lo_made, c + 1)
                    if j == 4:
                        pe.wait_ge(sig_made, 2 * l + 2)
                    if j == 6:
                        pe.wait_ge(c_made, 2 * l + 2)
                    wh, wl = (slot_view(r, c % SPLITS, 4, 512) for r in (high, low))
                    for k in range(4):
                        for b in range(NB):
                            kt = 4 * kh + k
                            mm = three(ps[:, 2 * (q % 2) + b, :], xT_hi[:, kt, b * P:b * P + P], xT_lo[:, kt, b * P:b * P + P],
                                       wh[:, k, :], wl[:, k, :], kt == 0, kt == KT - 1)
                    mm.then_inc(w_used, 1)
                    if j == 2:
                        pe.wait_ge(mix_landed, 16 * 9 * (l + 1))
                        nc.tensor.transpose(ps[:, 6, 0:16], rows16[:, :], ident[0:16, 0:16])
                        for t in range(CT):
                            mm = nc.tensor.transpose(ps[:, 6, 16 + TAPS * t:16 + TAPS * (t + 1)], conv_rows[:, t * P:t * P + P],
                                                     ident[0:TAPS, 0:TAPS])
                        mm.then_inc(prep_filled, 1)
                        for hh in range(SH):
                            mm = nc.tensor.transpose(ps[:, 7, hh * P:hh * P + P], sgu_rows[:, hh, :], ident)
                        mm.then_inc(prep_filled, 1)
                    if j == 5:
                        pe.wait_ge(c_made, 2 * l + 2)
                        token_transposes(c_tok, TP, ct_filled)
                pe.wait_ge(prep_made, 2 * l + 2)
                for b in range(NB):
                    pe.wait_ge(vn_made, 2 * l + b + 1)
                    for hh in range(SH):
                        mm = nc.tensor.matmul(ps[:, 2 + b, hh * P:hh * P + P], wsT[:, hh, :], v[:, b, hh * P:hh * P + P],
                                              start=True, stop=True)
                    mm.then_inc(sp_filled, 1)
                pe.wait_ge(g_made, 2 * l + 2)
                pe.wait_ge(ct_made, 2 * l + 2)
                token_transposes(u, TP, gt_filled)

                def out_chunk(n):
                    c = c0 + 8 + n
                    pe.wait_ge(lo_made, c + 1)
                    k = OUT_ROWS[n]
                    row_product(xT_hi, xT_lo, (k, k + 1), c % SPLITS, lambda b, half: DOWN[2 * b + half], NB,
                                n == 0, n == 3).then_inc(w_used, 1)

                pe.wait_ge(cat_lo, 4 * l + 2)
                out_chunk(0)
                out_chunk(1)
                pe.wait_ge(conv_step, CT * TAPS * (l + 1))
                for m in range(2):
                    for kk in range(2):
                        mm = nc.tensor.matmul(ps[:, TP[m], kk * T:kk * T + T], centre, yT[:, 2 * m + kk, :], start=True, stop=True)
                    mm.then_inc(yc_filled, 1)
                for t in range(CT):
                    pe.wait_ge(sq_made, 2 * l + t // 2 + 1)
                    mm = nc.tensor.matmul(ps[0:8, 2, 0:T], mean8[:, t, :], sq[:, t, :], start=(t == 0), stop=(t == CT - 1))
                mm.then_inc(var_filled, 1)
                pe.wait_ge(rstd8_made, l + 1)
                for m in range(2):
                    for kk in range(2):
                        mm = nc.tensor.matmul(ps[:, 3 - m, kk * T:kk * T + T], spread8[:, 2 * m + kk, :], rstd8[:, :],
                                              start=True, stop=True)
                    mm.then_inc(rb_filled, 1)
                pe.wait_ge(cat_lo, 4 * l + 3)
                out_chunk(2)
                pe.wait_ge(cat_lo, 4 * l + 4)
                out_chunk(3)

            pe.wait_ge(small_landed, 16)
            norm_transposes(0, 0)
            mixer(0)
            norm_transposes(1, 1)
            c0 = MIX_CHUNKS
            for j in range(16):
                q, up = j // 2, j % 2
                c = c0 + j
                pe.wait_ge(lo_made, c + 1)
                if q:
                    pe.wait_ge(mult_made if up else silu_made, 2 * q)
                wh, wl = (slot_view(r, c % SPLITS, KT, TW) for r in (high, low))
                for k in range(KT):
                    for b in range(NB):
                        mm = three(ps[:, 2 * up + b, 0:TW], xT_hi[:, k, b * P:b * P + P], xT_lo[:, k, b * P:b * P + P],
                                   wh[:, k, :], wl[:, k, :], k == 0, k == KT - 1)
                mm.then_inc(w_used, 1)
                dense_transposes(pe, j)
            for d in range(8):
                c = c0 + 16 + d
                pe.wait_ge(lo_made, c + 1)
                tiles = down_tiles(d)
                pe.wait_ge(ht_lo, tiles[-1] // 2 + 1)
                if d == 0:
                    pe.wait_ge(silu_made, 16)
                row_product(hT_hi, hT_lo, tiles, c % SPLITS, lambda b, half: DOWN[2 * b + half], NB, d == 0,
                            d == 7).then_inc(w_used, 1)
                dense_transposes(pe, 16 + d)
            norm_transposes(2, 2)
            mixer(1)
            norm_transposes(3, 3)
            pe.wait_ge(router_split, 2)
            for b in range(NB):
                for k in range(KT):
                    mm = three(ps[:, 0, b * NE:b * NE + NE], xT_hi[:, k, b * P:b * P + P], xT_lo[:, k, b * P:b * P + P],
                               router_hi[:, k, :], router_lo[:, k, :], k == 0, k == KT - 1)
            mm.then_inc(logits_ready, 1)
            pe.wait_ge(chosen_made, 1)
            nc.tensor.matmul(ps[:, 1, 0:NE], before, chosen[:, 0, :], start=True, stop=True)
            nc.tensor.matmul(ps[:, 1, NE:2 * NE], before, chosen[:, 1, :], start=True, stop=False)
            nc.tensor.matmul(ps[:, 1, NE:2 * NE], ones, chosen[:, 0, :], start=False, stop=True)
            nc.tensor.matmul(ps[:, 1, 2 * NE:3 * NE], ones, chosen[:, 0, :], start=True, stop=False)
            nc.tensor.matmul(ps[:, 1, 2 * NE:3 * NE], ones, chosen[:, 1, :], start=False, stop=True).then_inc(places_ready, 1)
            pe.wait_ge(routed, 1)
            pe.wait_ge(xs_lo, 2)

            def scatter(first_fill, half):
                c = slice(half * 512, half * 512 + 512)
                for b in range(NB):
                    pe.wait_ge(tp_freed, first_fill + b - 1)
                    nc.tensor.matmul(ps[:, TP[b], :], drop[:, b, :], eo_hi[:, c], start=True, stop=False)
                    nc.tensor.matmul(ps[:, TP[b], :], drop[:, b, :], eo_lo[:, c], start=False, stop=True).then_inc(tp_filled, 1)

            def item(i):
                first = isinstance(i, int)
                pe.wait_ge(pick_made, 2 * i + 2)
                for p in range(4):
                    fill = fill_no(i, p)
                    if not first or p >= 2:
                        pe.wait_ge(tp_freed, fill - 1)
                    for part, base in ((xn_hi, 0), (xn_lo, 2 * P)):
                        for kk in range(2):
                            k = 2 * p + kk
                            for b in range(NB):
                                mm = nc.tensor.matmul(ps[:, TP[p % 2], base + kk * P:base + kk * P + P],
                                                      part[:, b, k * P:k * P + P], pick[:, b, :], start=(b == 0), stop=(b == 1))
                    mm.then_inc(tp_filled, 1)
                for j in range(16):
                    g, up, kh = j // 4, j % 4 // 2, j % 2
                    pe.wait_ge(lo_made, chunk(i, j) + 1)
                    if j == 0:
                        pe.wait_ge(tp_freed, fill_no(i, 3) + 1)
                    if kh == 0 and not (first and g == 0):
                        pe.wait_ge(emult_made if up else esilu_made, 8 * i + 2 * g)
                    wh, wl = (slot_view(r, j % SPLITS, 4, GW) for r in (high, low))
                    for k in range(4):
                        kt = 4 * kh + k
                        for t in range(2):
                            c = slice(t * TW, t * TW + TW)
                            mm = three(ps[:, 2 * up + t, 0:TW], xe_hi[:, kt * P:kt * P + P], xe_lo[:, kt * P:kt * P + P],
                                       wh[:, k, c], wl[:, k, c], kt == 0, kt == KT - 1)
                    mm.then_inc(w_used, 1)
                    if j == 3 and not first:
                        pe.wait_ge(eo_lo_made, 2 * i)
                        scatter(fill_no(i, 4), 0)
                    if j == 4 and not first:
                        scatter(fill_no(i, 6), 1)
                    if j == 5:
                        for b in range(NB):
                            pe.wait_ge(tp_freed, fill_no(i, 8 + b) - 1)
                            nc.tensor.transpose(ps[:, TP[b], 0:P], f(pick[:, b, :]), ident).then_inc(tp_filled, 1)
                    hidden_transposes(i, j)
                for d in range(8):
                    j = 16 + d
                    tiles = down_tiles(d)
                    pe.wait_ge(lo_made, chunk(i, j) + 1)
                    pe.wait_ge(tp_freed, fill_no(i, 10 + batch_of(tiles[-1])) + 1)
                    row_product(eT_hi, eT_lo, tiles, j % SPLITS, lambda b, half: 6 + half, 1, d == 0,
                                d == 7).then_inc(w_used, 1)
                    hidden_transposes(i, j)

            def hidden_transposes(i, j):
                if j in AFTER_T:
                    n = AFTER_T[j]
                    lo, hi = BATCHES[n]
                    pe.wait_ge(emult_made, 8 * i + 2 * BATCH_GROUPS[n])
                    pe.wait_ge(tp_freed, fill_no(i, 10 + n) - 1)
                    for t in range(lo, hi):
                        mm = nc.tensor.transpose(ps[:, TP[n % 2], (t - lo) * P:(t - lo + 1) * P], eh[:, t * P:t * P + P], ident)
                    mm.then_inc(tp_filled, 1)

            item(0)
            with pe.Fori(1, NE) as i:
                item(i)
            n_items = pe.value_load(plan[0:1, 3:4], min_val=NE - 1, max_val=ITEMS - 1) + 1
            with pe.Fori(NE, ITEMS) as i:
                with pe.If(i < n_items):
                    item(i)
            pe.wait_ge(eo_lo_made, 2 * n_items)
            scatter(fill_no(n_items, 0), 0)
            scatter(fill_no(n_items, 2), 1)
            second_tensor(pe, n_items, norm_transposes)



_INS = ["x", "norm_mix", "w_in", "conv_w", "conv_b", "conv_ng", "conv_nb", "sgu_ng", "sgu_nb", "sgu_w", "sgu_b", "w_out",
        "norm_ffn", "ffn_wg", "ffn_wu", "ffn_wd", "moe_router", "moe_wg", "moe_wu", "moe_wd", "norm_final",
        "meta_tokens_2", "norm_gain_2", "w_in_2", "w_branch_sb_2", "w_branch_swa_2", "w_out_2", "attn_sinks_2",
        "final_norm_gain_2"]


def kernel(**inputs):
    import concourse.bacc as bacc
    from concourse.bass_utils import run_bass_kernel_spmd

    nc = bacc.Bacc("TRN2", target_bir_lowering=False, num_devices=1)
    arrays, given = {}, {}
    named = {name: np.ascontiguousarray(inputs[name]) for name in _INS}
    named.update(constants())
    for name, value in named.items():
        arrays[f"in_{name}"] = value
        given[name] = nc.dram_tensor(f"in_{name}", value.shape, mybir.dt.from_np(value.dtype), kind="ExternalInput").ap()
    out = nc.dram_tensor("out_x", (1, T, D), F32, kind="ExternalOutput").ap()
    model_program(nc, given, out)
    r = run_bass_kernel_spmd(nc, [arrays], core_ids=[0])
    return r.results[0]["out_x"]
```

```python
import numpy as np
import concourse.bass as bass
from concourse import mybir

F32 = mybir.dt.float32
F32R = mybir.dt.float32r
BF16 = mybir.dt.bfloat16
I32 = mybir.dt.int32
ALU = mybir.AluOpType
ACT = mybir.ActivationFunctionType
AX = mybir.AxisListType

P = 128
T = 256
NB = T // P
D = 1024
KT = D // P
CC = 512
CT = CC // P
ZC = 4 * CC
TAPS = 31
SH = 4
FF = 2816
FT = FF // P
NE = 8
EPS = 1e-6
ITEMS = NE + (2 * T) // (P + 1)
NEG = -1e30

RAWS, SPLITS = 4, 3
RAWSB = 3
SLOT = 3072
MIX_CHUNKS = 12
FFN_CHUNKS = 24
GW = 704
TW = 352
LAYER_CHUNKS = MIX_CHUNKS + FFN_CHUNKS
MOE0 = LAYER_CHUNKS + MIX_CHUNKS
SLOTB = 2560
BCH_IN, BCH_SB, BCH_SW, BCH_OUT = 20, 2, 4, 4
Q2W = 320

META = 16
HD = 64
SBH, SWH, KVH = 8, 16, 2
SBW = SBH * HD
SWW = SWH * HD
KVW = KVH * HD
O_SBQ, O_SBK, O_SBV, O_SWQ = 0, 512, 1024, 1536
O_SWK, O_SWV, O_SBZ, O_SWZ = 2560, 2688, 2816, 3328
O_GSB, O_GSW = 4352, 5376
IN2 = 6400
QKV = O_SBZ


def constants():
    i = np.arange(P)
    ident = np.eye(P)
    iota = np.tile(i[None, :], (P, 1))
    small = np.concatenate([ident, iota], 1)
    causal = (i[:, None] <= i[None, :]).astype(float)
    group = (i[:, None] // 64 == i[None, :] // 64) / 64.0
    centre = ident - group
    mean8 = np.zeros((P, CT, 8))
    spread8 = np.zeros((P, CT, P))
    for t in range(CT):
        for c in range(P):
            mean8[c, t, 2 * t + c // 64] = 1 / 64
            spread8[2 * t + c // 64, t, c] = 1
    mix = np.concatenate([causal, centre, mean8.reshape(P, -1), spread8.reshape(P, -1)], 1)
    before = (i[:, None] < i[None, :]).astype(float)
    e = np.arange(NE)
    earlier = np.tile((e[None, :] < e[:, None]).astype(float).reshape(1, -1), (P, 1))
    route = np.concatenate([before, np.ones((P, P)), earlier, np.tile(e[None, :], (P, 1))], 1)
    upto = -(i[:, None] >= i[None, :]).astype(float)
    sbmask = np.where(i[:, None] < i[None, :], 0.0, NEG)
    own = np.where(i[None, :] <= i[:, None], 0.0, NEG)
    prev = np.where(i[None, :] > i[:, None], 0.0, NEG)
    meta = np.full((P, P), NEG)
    meta[:, :META] = np.where(i[:, None] < P - META + np.arange(META)[None, :], 0.0, NEG)
    half = HD // 2
    inv = np.float32(10000.0) ** (-np.arange(half, dtype=np.float32) / half)

    def angles(pos):
        a = pos.astype(np.float32)[:, None] * inv.astype(np.float32)[None, :]
        c, s = np.cos(a), np.sin(a)
        return np.concatenate([c, c], 1), np.concatenate([-s, s], 1)

    parts = [upto, -np.ones((P, P)), sbmask, np.concatenate([meta, own], 1), np.concatenate([prev, own], 1)]
    for pos in (META + i, META + P + i, i):
        parts += angles(pos)
    second = np.concatenate(parts, 1)
    return {k: np.ascontiguousarray(v, dtype=np.float32) for k, v in
            dict(c_small=small, c_mix=mix, c_route=route, c_second=second).items()}


def model_program(nc, a, out):
    at = [((nc.sbuf_base + 63) // 64) * 64]
    size = {F32: 4, F32R: 4, I32: 4, BF16: 2}

    def nbytes(shape, dt):
        return (int(np.prod(shape[1:])) * size[dt] + 31) // 32 * 32

    def place(name, shape, dt, cursor=None):
        cur = at if cursor is None else cursor
        t = nc.alloc_sbuf_tensor_at(name, list(shape), dt, offset=cur[0])
        cur[0] += nbytes(shape, dt)
        return t

    ring_at = at[0]
    raw = place("raw", [P, RAWS, SLOT], F32)
    high = place("high", [P, SPLITS, SLOT], F32R)
    low = place("low", [P, SPLITS, SLOT], F32R)
    ring_end = at[0]
    curb = [ring_at]
    rawb = place("rawb", [P, RAWSB, SLOTB], F32, curb)
    highb = place("highb", [P, SPLITS, SLOTB], F32R, curb)
    lowb = place("lowb", [P, SPLITS, SLOTB], F32R, curb)
    spare = curb
    x = place("x", [P, NB, D], F32)
    xT_hi = place("xT_hi", [P, KT, T], F32R)
    xT_lo = place("xT_lo", [P, KT, T], F32R)
    gain = place("gain", [P, D], F32)
    small = place("small", [P, 2 * P], F32)
    ident, iota = small[:, 0:P], small[:, P:2 * P]
    eps = place("eps", [P, 1], F32)
    sumsq = place("sumsq", [P, NB], F32)
    std = place("std", [P, NB], F32)
    rstd = place("rstd", [P, NB], F32)
    items = place("items", [P, ITEMS + 1, 4], F32)
    now = place("now", [P, 2], F32)
    gates_now = place("gates_now", [P, 2], F32)
    unused = place("unused", [P, 24], F32)
    plan = place("plan", [P, 4], I32)
    R0 = at[0]
    assert R0 + 56320 <= nc.sbuf_usable_end, (R0, nc.sbuf_usable_end)

    xn = nc.alloc_sbuf_tensor_at("xn", [P, NB, D], F32, offset=R0)
    cur = [R0 + 8192]
    c_tok = place("c_tok", [P, NB, CC], F32, cur)
    sig = place("sig", [P, NB, CC], F32, cur)
    u = place("u", [P, NB, CC], F32, cur)
    v = place("v", [P, NB, CC], F32, cur)
    cT = place("cT", [P, CT, TAPS - 1 + T], F32, cur)
    yT = place("yT", [P, CT, T], F32, cur)
    sq = place("sq", [P, CT, T], F32, cur)
    cmix = place("cmix", [P, 2 * P + 8 * CT + CT * P], F32, cur)
    causal, centre = cmix[:, 0:P], cmix[:, P:2 * P]
    mean8 = cmix[:, 2 * P:2 * P + 8 * CT].rearrange("p (t g) -> p t g", t=CT)
    spread8 = cmix[0:8, 2 * P + 8 * CT:].rearrange("p (t c) -> p t c", t=CT)
    rows16 = place("rows16", [16, P], F32, cur)
    conv_rows = place("conv_rows", [TAPS, CC], F32, cur)
    cols = place("cols", [P, 16 + CT * TAPS], F32, cur)
    sgu_rows = place("sgu_rows", [P, SH, P], F32, cur)
    wsT = place("wsT", [P, SH, P], F32, cur)
    sgu_g = place("sgu_g", [P, CC], F32, cur)
    sgu_o = place("sgu_o", [P, CC], F32, cur)
    vstat = place("vstat", [P, NB * SH, 6], F32, cur)
    vmv = place("vmv", [P, NB * SH, 2], F32, cur)
    vstd = place("vstd", [P, NB * SH], F32, cur)
    vrstd = place("vrstd", [P, NB * SH], F32, cur)
    std8 = place("std8", [8, T], F32, cur)
    rstd8 = place("rstd8", [8, T], F32, cur)
    diag = place("diag", [P, TAPS, P], F32, [R0])
    assert cur[0] <= nc.sbuf_usable_end, cur
    cur = [R0]
    hT_hi = place("hT_hi", [P, FT, T], F32R, cur)
    hT_lo = place("hT_lo", [P, FT, T], F32R, cur)
    h = place("h", [P, NB, 4 * TW], F32, cur)
    assert cur[0] <= nc.sbuf_usable_end, cur
    cur = [R0]
    eT_hi = place("eT_hi", [P, FT, P], F32R, cur)
    eT_lo = place("eT_lo", [P, FT, P], F32R, cur)
    eh = place("eh", [P, FF], F32, cur)
    xn_hi = place("xn_hi", [P, NB, D], F32R, cur)
    xn_lo = place("xn_lo", [P, NB, D], F32R, cur)
    pick = place("pick", [P, NB, P], F32R, cur)
    drop = place("drop", [P, NB, P], F32R, cur)
    assert cur[0] <= nc.sbuf_usable_end, cur
    xe_hi, eo_hi = (xT_hi[:, 4 * n:4 * n + 4, :].rearrange("p a b -> p (a b)") for n in range(2))
    xe_lo, eo_lo = (xT_lo[:, 4 * n:4 * n + 4, :].rearrange("p a b -> p (a b)") for n in range(2))
    cur = [nc.sbuf_usable_end // 32 * 32 - 2112]
    croute = place("croute", [P, 2 * P + NE * NE + NE], F32, cur)
    before, ones = croute[:, 0:P], croute[:, P:2 * P]
    earlier = croute[:, 2 * P:2 * P + NE * NE].rearrange("p (a b) -> p a b", a=NE)
    number = croute[:, 2 * P + NE * NE:]
    router = place("router", [P, KT, NE], F32, cur)
    router_hi = place("router_hi", [P, KT, NE], F32R, cur)
    router_lo = place("router_lo", [P, KT, NE], F32R, cur)
    assert cur[0] <= nc.sbuf_usable_end
    cur = [R0 + 22528]
    logit = place("logit", [P, NB, NE], F32, cur)
    above = place("above", [P, NB, NE, NE], F32, cur)
    equal = place("equal", [P, NB, NE, NE], F32, cur)
    rank = place("rank", [P, NB, NE], F32, cur)
    chosen = place("chosen", [P, NB, NE], F32, cur)
    top = place("top", [P, NB], F32, cur)
    share = place("share", [P, NB, NE], F32, cur)
    total = place("total", [P, NB], F32, cur)
    place_in = place("place_in", [P, NB, NE], F32, cur)
    crowd = place("crowd", [P, NE], F32, cur)
    crowds = place("crowds", [P, NE, NE], F32, cur)
    crowd_at = place("crowd_at", [P, NE], F32, cur)
    which = place("which", [P, 3, NE], F32, cur)
    planf = place("planf", [P, 4], F32, cur)
    dots = place("dots", [P, 3, 5, NE], F32, cur)
    assert cur[0] <= R0 + 22528 + 11264, cur
    meta_kv = place("meta_kv", [P, 1280], F32, spare)
    mT_hi = place("mT_hi", [P, KT, P], F32R, spare)
    mT_lo = place("mT_lo", [P, KT, P], F32R, spare)
    swqT_at = [spare[0] - 8192]
    z_sw = place("z_sw", [P, NB, SWW], F32, spare)
    assert spare[0] <= ring_end, (spare, ring_end)
    swqT = place("swqT", [P, SWH // 2, T], F32, swqT_at)
    cur = [R0]
    qkv = place("qkv", [P, NB, QKV], F32, cur)
    z_sb = place("z_sb", [P, NB, SBW], F32, cur)
    gates_at = cur[0]
    sbqT = place("sbqT", [P, SBH // 2, T], F32, cur)
    sbkT = place("sbkT", [P, SBH // 2, T], F32, cur)
    sbkTm = place("sbkTm", [P, SBH // 2, 2, META], F32, cur)
    swkk = place("swkk", [P, NB, 2 * KVW], F32, cur)
    swkT = place("swkT", [P, KVH, T], F32, cur)
    swkTm = place("swkTm", [P, KVH, META], F32, cur)
    csec = place("csec", [P, 7 * P + 6 * HD], F32, cur)
    sbm = place("sbm", [P, P], BF16, cur)
    swm = place("swm", [P, NB, T], BF16, cur)
    identb = place("identb", [P, P], BF16, cur)
    swkm = place("swkm", [META, 2 * KVW], F32, cur)
    sinks = place("sinks", [P, SWH], F32, cur)
    one = place("one", [P, 1], F32, cur)
    meta_s = place("meta_s", [META, 4], F32, cur)
    mx, nmax, den, den2, rden, esink = (place(n, [P, 8], F32, cur) for n in ("mx", "nmax", "den", "den2", "rden", "esink"))
    work = cur[0]
    rtmp = place("rtmp", [P, (SWH + KVH) * HD], F32, [work])
    cur = [work]
    sb_a = place("sb_a", [P, 2, 3 * P], F32, cur)
    sb_m_ = place("sb_m", [P, 2, 3 * P], F32, cur)
    sb_w = place("sb_w", [P, 2, 3 * P], F32, cur)
    assert cur[0] <= nc.sbuf_usable_end, (cur, nc.sbuf_usable_end)
    prob = place("prob", [P, 8, T], F32, [work])
    assert work + 8192 <= nc.sbuf_usable_end
    left = [spare[0]]
    sb_am = place("sb_am", [META, 2 * T], F32, left)
    sb_mm = place("sb_mm", [META, 2 * T], F32, left)
    sb_wm = place("sb_wm", [META, 2 * T], F32, left)
    assert left[0] <= ring_end, (left, ring_end)
    pt = place("pt", [P, 2, 4 * P], F32, [spare[0]])
    xm = place("xm", [META, D], F32, [R0 + 22528])
    gain_b = place("gain_b", [P, D], F32, [R0 + 22528 + 4096])
    xm_junk = place("xm_junk", [META, D], F32, [work])
    cur = [gates_at]
    gsig = place("gsig", [P, 2, NB, D], F32, cur)
    sbT_hi = place("sbT_hi", [P, SBW // P, T], F32R, cur)
    sbT_lo = place("sbT_lo", [P, SBW // P, T], F32R, cur)
    assert cur[0] <= nc.sbuf_usable_end
    merged = qkv[:, :, O_SBK:O_SBK + D]

    ps = nc.alloc_psum_tensor("ps", [P, 8, 512], F32)
    TP = (4, 5)
    DOWN = (6, 7, 0, 1)

    def f(t):
        return t.bitcast(F32)

    def sem(name):
        return nc.alloc_semaphore(name)

    w_landed = [sem(f"w_landed{s}") for s in range(RAWS)]
    hi_made, lo_made, w_used = sem("hi_made"), sem("lo_made"), sem("w_used")
    wb_landed = [sem(f"wb_landed{s}") for s in range(RAWSB)]
    bhi_made, blo_made, bw_used = sem("bhi_made"), sem("blo_made"), sem("bw_used")
    x_landed = [sem(f"x_landed{b}") for b in range(NB)]
    gain_landed = [sem("gain0_landed"), sem("gain_landed")]
    region_free = sem("region_free")
    small_landed, gain_b_landed = sem("small_landed"), sem("gain_b_landed")
    mix_landed, route_landed, second_landed = sem("mix_landed"), sem("route_landed"), sem("second_landed")
    eps_made = sem("eps_made")
    sumsq_made = [sem(f"sumsq_made{b}") for b in range(NB)]
    std_made, rstd_made, xn_made = sem("std_made"), sem("rstd_made"), sem("xn_made")
    xt_filled, xt_hi, xt_lo = sem("xt_filled"), sem("xt_hi"), sem("xt_lo")
    acc_ready, x_made = sem("acc_ready"), sem("x_made")
    dve_steps, act_steps = sem("dve_steps"), sem("act_steps")
    sig_made, c_made = sem("sig_made"), sem("c_made")
    prep_filled, prep_made = sem("prep_filled"), sem("prep_made")
    pad_made, ct_filled, ct_made = sem("pad_made"), sem("ct_filled"), sem("ct_made")
    conv_step = sem("conv_step")
    diag_made, pe_conv, y2_made = sem("diag_made"), sem("pe_conv"), sem("y2_made")
    u_made, v_made, vvar_made, vstd_made = sem("u_made"), sem("v_made"), sem("vvar_made"), sem("vstd_made")
    vvar_stats = sem("vvar_stats")
    vnorm_ready, vnorm_made, vn_made = sem("vnorm_ready"), sem("vnorm_made"), sem("vn_made")
    vg_made = sem("vg_made")
    sp_filled, g_made, gt_filled = sem("sp_filled"), sem("g_made"), sem("gt_filled")
    cat_hi, cat_lo = sem("cat_hi"), sem("cat_lo")
    yc_filled, yc_made, sq_made, var_filled = sem("yc_filled"), sem("yc_made"), sem("sq_made"), sem("var_filled")
    std8_made, rstd8_made, rb_filled, yn_made, cs_made = (
        sem("std8_made"), sem("rstd8_made"), sem("rb_filled"), sem("yn_made"), sem("cs_made"))
    silu_made, mult_made = sem("silu_made"), sem("mult_made")
    ht_filled, ht_hi, ht_lo = sem("ht_filled"), sem("ht_hi"), sem("ht_lo")
    router_hi_made, router_lo_made = sem("router_hi_made"), sem("router_lo_made")
    logits_ready, logit_made, expo_made = sem("logits_ready"), sem("logit_made"), sem("expo_made")
    chosen_made, places_ready, routed = sem("chosen_made"), sem("places_ready"), sem("routed")
    xs_hi, xs_lo = sem("xs_hi"), sem("xs_lo")
    now_made, pick_made = sem("now_made"), sem("pick_made")
    tp_filled, tp_hi, tp_freed = sem("tp_filled"), sem("tp_hi"), sem("tp_freed")
    esilu_made, emult_made = sem("esilu_made"), sem("emult_made")
    eo_hi_made, eo_lo_made = sem("eo_hi_made"), sem("eo_lo_made")

    Z_ORDER = (1, 0, 3, 2)
    DVE_TILES = (0, 1, 3)
    PE_TILE = 2
    OUT_ROWS = (4, 6, 0, 2)

    def down_tiles(d):
        return range(3 * d, min(3 * d + 3, FT))

    def words(c):
        j = (c - MOE0) % FFN_CHUNKS if c >= MOE0 else c % LAYER_CHUNKS - MIX_CHUNKS
        if j < 0:
            return 2048
        return 8 * TW if j < 16 else D * len(down_tiles(j - 16))

    def mixer_source(l, j):
        if j < 8:
            q, kh = Z_ORDER[j // 2], j % 2
            return a["w_in"][l, kh * 512:kh * 512 + 512, q * CC:q * CC + CC].rearrange("(t p) n -> p t n", p=P)
        k = OUT_ROWS[j - 8]
        return a["w_out"][l, k * P:(k + 2) * P, :].rearrange("(t p) n -> p t n", p=P)

    def ffn_source(j):
        if j < 16:
            w = a["ffn_wg"] if j % 2 == 0 else a["ffn_wu"]
            q = j // 2
            return w[0, :, q * TW:q * TW + TW].rearrange("(t p) n -> p t n", p=P)
        t = down_tiles(j - 16)
        return a["ffn_wd"][0, t[0] * P:(t[-1] + 1) * P, :].rearrange("(t p) n -> p t n", p=P)

    wg_v = a["moe_wg"].rearrange("l e (t p) n -> (l e) p t n", p=P)
    wu_v = a["moe_wu"].rearrange("l e (t p) n -> (l e) p t n", p=P)
    wd_v = a["moe_wd"].rearrange("l e (t p) n -> (l e) p t n", p=P)

    def expert_source(e, j):
        if j < 16:
            g, kh = j // 4, j % 2
            w = wg_v if j % 4 < 2 else wu_v
            return w[e, :, 4 * kh:4 * kh + 4, g * GW:g * GW + GW]
        t = down_tiles(j - 16)
        return wd_v[e, :, t[0]:t[-1] + 1, :]

    def chunk(i, j):
        return MOE0 + FFN_CHUNKS * i + j

    def slot_view(ring, s, rows, width):
        return ring[:, s, 0:rows * width].rearrange("p (t n) -> p t n", t=rows)

    def load(sp, c, src):
        if c >= RAWS:
            sp.wait_ge(lo_made, c - RAWS + 1)
        rows, width = src.shape[1], src.shape[2]
        sp.dma_start(slot_view(raw, c % RAWS, rows, width), src).then_inc(w_landed[c % RAWS], 16)

    def load_item(sp, i, j, src):
        sp.wait_ge(lo_made, chunk(i, j - RAWS + 1))
        rows, width = src.shape[1], src.shape[2]
        sp.dma_start(slot_view(raw, j % RAWS, rows, width), src).then_inc(w_landed[j % RAWS], 16)

    def make_high(act, c):
        act.wait_ge(w_landed[c % RAWS], 16 * (c // RAWS + 1))
        if c >= SPLITS:
            act.wait_ge(w_used, c - SPLITS + 1)
        n = words(c)
        nc.scalar.activation(high[:, c % SPLITS, 0:n], raw[:, c % RAWS, 0:n], ACT.Copy).then_inc(hi_made, 1)

    def make_high_item(act, i, j):
        act.wait_ge(w_landed[j % RAWS], 16 * (MOE0 // RAWS + j // RAWS + 1) + i * (16 * FFN_CHUNKS // RAWS))
        act.wait_ge(w_used, chunk(i, j - SPLITS + 1))
        n = words(chunk(0, j))
        nc.scalar.activation(high[:, j % SPLITS, 0:n], raw[:, j % RAWS, 0:n], ACT.Copy).then_inc(hi_made, 1)

    def make_low(dve, c):
        dve.wait_ge(hi_made, c + 1)
        n = words(c)
        nc.vector.tensor_tensor(low[:, c % SPLITS, 0:n], raw[:, c % RAWS, 0:n], f(high[:, c % SPLITS, 0:n]),
                                ALU.subtract).then_inc(lo_made, 1)

    def make_low_item(dve, i, j):
        dve.wait_ge(hi_made, chunk(i, j + 1))
        n = words(chunk(0, j))
        nc.vector.tensor_tensor(low[:, j % SPLITS, 0:n], raw[:, j % RAWS, 0:n], f(high[:, j % SPLITS, 0:n]),
                                ALU.subtract).then_inc(lo_made, 1)

    def keep_warm(bank, count):
        for _ in range(count):
            nc.tensor.transpose(ps[:, bank, 0:P], ident, ident)

    def three(out, xh, xl, wh, wl, first, last):
        nc.tensor.matmul(out, xh, wh, start=first, stop=False)
        nc.tensor.matmul(out, xh, wl, start=False, stop=False)
        return nc.tensor.matmul(out, xl, wh, start=False, stop=last)

    def row_product(hT, lT, tiles, s, acc_of, blocks, first, last, rings=None, done=None):
        hr, lr = rings or (high, low)
        wh, wl = (slot_view(r, s, len(tiles), D) for r in (hr, lr))
        def products(n, t, b):
            for half in range(2):
                c = slice(half * 512, half * 512 + 512)
                mm = three(ps[:, acc_of(b, half), :], hT[:, t, b * P:b * P + P], lT[:, t, b * P:b * P + P],
                           wh[:, n, c], wl[:, n, c], first and n == 0, last and n == len(tiles) - 1)
            return mm

        if done is not None:
            for b in range(blocks):
                for n, t in enumerate(tiles):
                    mm = products(n, t, b)
                if b < blocks - 1:
                    mm.then_inc(done, 1)
            return mm
        for n, t in enumerate(tiles):
            for b in range(blocks):
                mm = products(n, t, b)
        return mm

    BATCHES = ((0, 4), (4, 8), (8, 11), (11, 15), (15, 19), (19, 22))
    BATCH_GROUPS = (1, 2, 2, 3, 4, 4)
    GATHER_AFTER = {19: (0, 1), 21: (2, 3)}
    AFTER_T = {6: 0, 9: 1, 10: 2, 13: 3, 17: 4, 18: 5}

    def fill_no(i, pos):
        return 16 * i + pos

    def batch_of(tile):
        return next(n for n, (lo, hi) in enumerate(BATCHES) if lo <= tile < hi)


    NORMS = 7
    xm_landed, meta_sum, meta_std, meta_made = sem("xm_landed"), sem("meta_sum"), sem("meta_std"), sem("meta_made")
    mt_zero, mt_filled, mt_hi_made, mt_lo_made = sem("mt_zero"), sem("mt_filled"), sem("mt_hi_made"), sem("mt_lo_made")
    masks_made = sem("masks_made")
    bz_read, meta_read = sem("bz_read"), sem("meta_read")
    rope_made, qk_filled, qk_made = sem("rope_made"), sem("qk_filled"), sem("qk_made")
    sbz_filled, sb_log_made, sb_m_made, sbs_filled, sb_w_made, sbo_filled, sbo_made = (
        sem("sbz_filled"), sem("sb_log_made"), sem("sb_m_made"), sem("sbs_filled"), sem("sb_w_made"),
        sem("sbo_filled"), sem("sbo_made"))
    sc_filled, max_made, prob_made, sink_made, den_made = (
        sem("sc_filled"), sem("max_made"), sem("prob_made"), sem("sink_made"), sem("den_made"))
    pt_filled, pt_act, pt_dve, pv_done, swo_made = (
        sem("pt_filled"), sem("pt_act"), sem("pt_dve"), sem("pv_done"), sem("swo_made"))
    block_ready, swz_made = sem("block_ready"), sem("swz_made")
    ot_filled, ot_hi, ot_lo = sem("ot_filled"), sem("ot_hi"), sem("ot_lo")
    merged_made, x2_made, out_written = sem("merged_made"), sem("x2_made"), sem("out_written")

    upto, minus_ones = csec[:, 0:P], csec[:, P:2 * P]
    ANG = 2 * P + P + 4 * P

    def angle(n, which):
        return csec[:, ANG + 2 * HD * n + HD * which:ANG + 2 * HD * n + HD * which + HD]

    def words_b(c):
        return KT * Q2W if c < BCH_IN else 2 * D

    META_TILES = {1: (192, 320, 0), 2: (0, 320, 128), 3: (0, 320, 448), 4: (0, 256, 768), 8: (0, 256, 1024)}
    META_ORDER = sorted(META_TILES)
    SBO, SWO = O_SBQ, O_SWQ

    def gate_pieces(q):
        out = []
        for func, start, width, target in ((ACT.Silu, O_SBZ, SBW, lambda b: z_sb[:, b, :]), (ACT.Silu, O_SWZ, SWW, lambda b: z_sw[:, b, :]),
                                           (ACT.Sigmoid, O_GSB, D, lambda b: gsig[:, 0, b, :]),
                                           (ACT.Sigmoid, O_GSB + D, D, lambda b: gsig[:, 1, b, :])):
            lo, hi = max(start, q * Q2W), min(start + width, (q + 1) * Q2W)
            if lo < hi:
                out.append((func, lo - q * Q2W, hi - q * Q2W, [target(b)[:, lo - start:hi - start] for b in range(NB)]))
        return out

    SW_FIRST = 13
    SB_BANKS = (2, 2, 0, 2)
    SB_META = (4, 4, 5, 4)

    def sw_place(n):
        return 2 * (n % 2) + n // 4, (n // 2 % 2) * T

    def merge_bank(b, half):
        return 2 + 2 * b + half

    def second_loads(sp, n_items):
        sp.wait_ge(w_used, chunk(n_items, 0) - 4)
        sp.dma_start(xm[:, :], a["meta_tokens_2"]).then_inc(xm_landed, 16)
        sp.dma_start(gain_b[:, :], a["norm_gain_2"][0:1, :].to_broadcast([P, D])).then_inc(gain_b_landed, 16)
        sp.wait_ge(lo_made, chunk(n_items, 0))
        for c in range(BCH_IN + BCH_SB + BCH_SW + BCH_OUT):
            if c >= RAWSB:
                sp.wait_ge(blo_made, c - RAWSB + 1)
            if c < BCH_IN:
                src = a["w_in_2"][0, :, c * Q2W:c * Q2W + Q2W].rearrange("(t p) n -> p t n", p=P)
            else:
                n = c - BCH_IN
                w, n = ((a["w_branch_sb_2"], n) if n < BCH_SB else (a["w_branch_swa_2"], n - BCH_SB)
                        if n < BCH_SB + BCH_SW else (a["w_out_2"], n - BCH_SB - BCH_SW))
                src = w[0, 2 * n * P:(2 * n + 2) * P, :].rearrange("(t p) n -> p t n", p=P)
            sp.dma_start(slot_view(rawb, c % RAWSB, src.shape[1], src.shape[2]), src).then_inc(wb_landed[c % RAWSB], 16)
        for b in range(NB):
            sp.wait_ge(xn_made, 2 * NORMS - 1 + b)
            sp.dma_start(out[0, b * P:b * P + P, :], xn[:, b, :]).then_inc(out_written, 16)
        sp.wait_ge(out_written, 32)

    def second_small_loads(pool):
        pool.wait_ge(region_free, 1)
        pool.memset(f(mT_hi[:, :, :]), 0.0).then_inc(mt_zero, 1)
        pool.memset(f(mT_lo[:, :, :]), 0.0).then_inc(mt_zero, 1)
        pool.memset(sbkTm[:, :, :, :], 0.0).then_inc(mt_zero, 1)
        pool.dma_start(csec[:, :], a["c_second"]).then_inc(second_landed, 16)
        pool.dma_start(sinks[:, :], a["attn_sinks_2"][0:1, :].to_broadcast([P, SWH])).then_inc(second_landed, 16)
        pool.wait_ge(second_landed, 32)
        pool.tensor_copy(sbm[:, :], csec[:, 2 * P:3 * P]).then_inc(masks_made, 1)
        pool.tensor_copy(swm[:, :, :], csec[:, 3 * P:7 * P].rearrange("p (b n) -> p b n", b=NB)).then_inc(masks_made, 1)
        pool.tensor_copy(identb[:, :], ident).then_inc(masks_made, 1)

    def second_scalar(act, n_items, prepare, norm_std, xt_high):
        steps = [0]

        def step(ins):
            steps[0] += 1
            ins.then_inc(act_steps, 1)
            act.wait_ge(act_steps, steps[0])

        made = [0]

        def high_upto(c):
            while made[0] <= min(c, 29):
                c1 = made[0]
                act.wait_ge(wb_landed[c1 % RAWSB], 16 * (c1 // RAWSB + 1))
                if c1 >= SPLITS:
                    act.wait_ge(bw_used, c1 - SPLITS + 1)
                n = words_b(c1)
                nc.scalar.activation(highb[:, c1 % SPLITS, 0:n], rawb[:, c1 % RAWSB, 0:n], ACT.Copy).then_inc(bhi_made, 1)
                made[0] += 1

        prepare(ACT.Sqrt)
        act.wait_ge(tp_freed, fill_no(n_items, 4))
        norm_std(4, 0)
        norm_std(4, 1)
        act.wait_ge(xm_landed, 16)
        nc.scalar.activation(xm_junk[:, :], xm[:, :], ACT.Square, accum_out=meta_s[:, 0:1]).then_inc(meta_sum, 1)
        act.wait_ge(meta_sum, 1)
        nc.scalar.activation(meta_s[:, 1:2], meta_s[:, 0:1], ACT.Sqrt, bias=eps[0:META, 0:1], scale=1.0 / D).then_inc(meta_std, 1)
        act.wait_ge(xn_made, 9)
        norm_std(5, 0)
        norm_std(5, 1)
        high_upto(0)
        act.wait_ge(mt_filled, 1)
        act.wait_ge(mt_zero, 3)
        nc.scalar.activation(mT_hi[:, :, 0:META], ps[:, 2, 0:KT * META].rearrange("p (t n) -> p t n", t=KT),
                             ACT.Copy).then_inc(mt_hi_made, 1)
        xt_high(4, 0)
        xt_high(4, 1)
        for q in range(9):
            high_upto(q + 2)
            act.wait_ge(bw_used, q + 1)
            w = min(Q2W, QKV - q * Q2W)
            for b in range(NB):
                ins = nc.scalar.activation(qkv[:, b, q * Q2W:q * Q2W + w], ps[:, 2 * (q % 2) + b, 0:w], ACT.Copy)
                if q == 8:
                    ins = nc.scalar.activation(z_sb[:, b, 0:Q2W - w], ps[:, 2 * (q % 2) + b, w:Q2W], ACT.Silu)
                ins.then_inc(bz_read, 1)

        def read_block(q, b, bank):
            for func, lo, hi, targets in gate_pieces(q):
                ins = nc.scalar.activation(targets[b], ps[:, bank, lo:hi], func)
            ins.then_inc(bz_read, 1)

        def read_tile(q):
            act.wait_ge(bw_used, q + 1)
            for b in range(NB):
                read_block(q, b, 2 * (q % 2) + b)

        for q in (9, 10):
            high_upto(q + 2)
            read_tile(q)
        for n in range(10):
            act.wait_ge(qk_filled, n + 1)
            bank = ps[:, TP[n % 2], :]
            pair = bank.rearrange("p (t n) -> p t n", t=2)
            if n < 2:
                nc.scalar.activation(sbqT[:, 2 * n:2 * n + 2, :], pair, ACT.Copy, scale=HD ** -0.5).then_inc(qk_made, 1)
            elif n < 4:
                nc.scalar.activation(sbkT[:, 2 * n - 4:2 * n - 2, :], pair, ACT.Copy).then_inc(qk_made, 1)
            elif n == 4:
                for r in range(2):
                    rows = slice(64 * r, 64 * r + 64)
                    nc.scalar.activation(sbkTm[rows, :, r, :], bank[rows, 0:4 * META].rearrange("p (t n) -> p t n", t=4), ACT.Copy)
                nc.scalar.activation(swkTm[:, :, :], bank[:, 4 * META:6 * META].rearrange("p (t n) -> p t n", t=2),
                                     ACT.Copy).then_inc(qk_made, 1)
            elif n == 5:
                nc.scalar.activation(swkT[:, :, :], pair, ACT.Copy).then_inc(qk_made, 1)
            else:
                nc.scalar.activation(swqT[:, 2 * n - 12:2 * n - 10, :], pair, ACT.Copy, scale=HD ** -0.5).then_inc(qk_made, 1)

        def sb_log(p):
            s, meta = SB_BANKS[p], SB_META[p]
            act.wait_ge(sbz_filled, p + 1)
            if p:
                act.wait_ge(sb_m_made, 2 * p)
            nc.scalar.activation(sb_a[:, :, :], ps[:, s:s + 2, 0:3 * P], ACT.Abs)
            step(nc.scalar.activation(sb_am[:, :], ps[0:META, meta, :], ACT.Abs))
            nc.scalar.activation(sb_a[:, :, :], sb_a[:, :, :], ACT.Exp, scale=-1.0)
            step(nc.scalar.activation(sb_am[:, :], sb_am[:, :], ACT.Exp, scale=-1.0))
            nc.scalar.activation(sb_a[:, :, :], sb_a[:, :, :], ACT.Ln, bias=one[:, 0:1]).then_inc(sb_log_made, 1)
            nc.scalar.activation(sb_am[:, :], sb_am[:, :], ACT.Ln, bias=one[0:META, 0:1]).then_inc(sb_log_made, 1)

        def sb_weights(p):
            s, meta = SB_BANKS[p], SB_META[p]
            act.wait_ge(sbs_filled, p + 1)
            if p:
                act.wait_ge(sbo_filled, p)
            nc.scalar.activation(sb_w[:, :, :], ps[:, s:s + 2, 0:3 * P], ACT.Exp).then_inc(sb_w_made, 1)
            nc.scalar.activation(sb_wm[:, :], ps[0:META, meta, :], ACT.Exp).then_inc(sb_w_made, 1)

        sb_log(0)
        act.wait_ge(bw_used, 12)
        for b in range(NB):
            read_block(11, b, b)
        sb_weights(0)
        sb_log(1)
        act.wait_ge(bw_used, 13)
        for b in range(NB):
            read_block(12, b, b)
        sb_weights(1)
        sb_log(2)
        high_upto(13)
        sb_log(3)
        sb_weights(2)
        high_upto(14)
        sb_weights(3)

        for w in range(4):
            act.wait_ge(max_made, 2 * w + 2)
            if w:
                act.wait_ge(pt_filled, 4 * w)
            for n in range(8):
                ins = nc.scalar.activation(prob[:, n, :], ps[:, sw_place(n)[0], sw_place(n)[1]:sw_place(n)[1] + T], ACT.Exp,
                                           bias=nmax[:, n:n + 1], accum_out=den[:, n:n + 1])
                ins.then_inc(prob_made, 1)
            nc.scalar.activation(esink[:, :], esink[:, :], ACT.Exp).then_inc(sink_made, 1)
            for fl in (0, 2):
                k = 4 * w + fl
                act.wait_ge(pt_filled, k + 1)
                if k >= 2:
                    act.wait_ge(pv_done, k - 1)
                nc.scalar.activation(pt[:, 0, :], ps[:, TP[0], :], ACT.Copy).then_inc(pt_act, 1)
                if w < 3 and fl == 0:
                    act.wait_ge(block_ready, w + 1)
                    read_block(SW_FIRST + w, 0, 7)
            if w < 3:
                act.wait_ge(bw_used, SW_FIRST + w + 1)
                read_block(SW_FIRST + w, 1, 7)
                high_upto(SW_FIRST + w + 2)
        for q in range(SW_FIRST + 3, BCH_IN):
            high_upto(q + 2)
            if q == SW_FIRST + 3:
                act.wait_ge(swo_made, 4)
            read_tile(q)
            if q == SW_FIRST + 3:
                for m in range(2):
                    act.wait_ge(ot_filled, m + 1)
                    nc.scalar.activation(sbT_hi[:, 2 * m:2 * m + 2, :], ps[:, TP[m], :].rearrange("p (t n) -> p t n", t=2),
                                         ACT.Copy).then_inc(ot_hi, 1)
        xt_high(5, 0)
        xt_high(5, 1)
        high_upto(23)
        high_upto(25)
        high_upto(27)
        xt_high(6, 0)
        xt_high(6, 1)
        high_upto(29)
        prepare(ACT.Sqrt)
        act.wait_ge(x2_made, 2)
        norm_std(6, 0)
        norm_std(6, 1)

    def second_vector(dve, n_items, step, norm_sum, norm_apply, xt_low):
        made = [0]

        def low_upto(c):
            while made[0] <= min(c, 29):
                c1 = made[0]
                dve.wait_ge(bhi_made, c1 + 1)
                n = words_b(c1)
                nc.vector.tensor_tensor(lowb[:, c1 % SPLITS, 0:n], rawb[:, c1 % RAWSB, 0:n], f(highb[:, c1 % SPLITS, 0:n]),
                                        ALU.subtract).then_inc(blo_made, 1)
                made[0] += 1

        dve.wait_ge(tp_freed, fill_no(n_items, 4))
        norm_sum(4)
        norm_apply(4, x, 0)
        norm_apply(4, x, 1)
        dve.wait_ge(meta_std, 1)
        dve.wait_ge(gain_b_landed, 16)
        step(nc.vector.reciprocal(meta_s[:, 2:3], meta_s[:, 1:2]))
        nc.vector.scalar_tensor_tensor(xm[:, :], xm[:, :], meta_s[:, 2:3], gain_b[0:META, :], ALU.mult, ALU.mult).then_inc(meta_made, 1)
        dve.wait_ge(xn_made, 10)
        norm_sum(5)
        norm_apply(5, xn, 0)
        norm_apply(5, xn, 1)
        low_upto(0)
        dve.wait_ge(mt_hi_made, 1)
        nc.vector.tensor_tensor(mT_lo[:, :, 0:META], ps[:, 2, 0:KT * META].rearrange("p (t n) -> p t n", t=KT),
                                f(mT_hi[:, :, 0:META]), ALU.subtract).then_inc(mt_lo_made, 1)
        xt_low(4, 0)
        xt_low(4, 1)
        for q in range(9):
            low_upto(q + 2)
            if q in META_TILES:
                lo, hi, to = META_TILES[q]
                k = META_ORDER.index(q)
                dve.wait_ge(bw_used, q + 1)
                nc.vector.tensor_copy(meta_kv[0:META, to:to + hi - lo], ps[0:META, 6 + k % 2, 0:hi - lo]).then_inc(meta_read, 1)
        dve.wait_ge(bz_read, 18)
        dve.wait_ge(second_landed, 32)
        half = HD // 2

        def rotate(rows, src, heads, n):
            s = src.rearrange("p (h d) -> p h d", h=heads)
            tmp = rtmp[0:rows, 0:heads * HD].rearrange("p (h d) -> p h d", h=heads)
            c, sn = (angle(n, k)[0:rows, :].rearrange("p (o d) -> p o d", o=1) for k in (0, 1))
            nc.vector.tensor_tensor(tmp[:, :, 0:half], s[:, :, half:HD], sn[:, :, 0:half].to_broadcast([rows, heads, half]), ALU.mult)
            step(nc.vector.tensor_tensor(tmp[:, :, half:HD], s[:, :, 0:half], sn[:, :, half:HD].to_broadcast([rows, heads, half]), ALU.mult))
            step(nc.vector.tensor_tensor(s, s, c.to_broadcast([rows, heads, HD]), ALU.mult))
            step(nc.vector.tensor_tensor(s, s, tmp, ALU.add))

        dve.wait_ge(meta_read, 5)
        rotate(META, meta_kv[0:META, 1024:1152], KVH, 2)
        step(nc.vector.tensor_copy(swkm[:, :].rearrange("p (g u d) -> p g u d", g=KVH, u=2),
                                   meta_kv[0:META, 1024:1152].rearrange("p (g o d) -> p g o d", g=KVH, o=1)
                                   .to_broadcast([META, KVH, 2, HD])))
        for b in range(NB):
            rotate(P, qkv[:, b, O_SWQ:O_SWV], SWH + KVH, b)
            nc.vector.tensor_copy(swkk[:, b, :].rearrange("p (g u d) -> p g u d", g=KVH, u=2),
                                  qkv[:, b, O_SWK:O_SWV].rearrange("p (g o d) -> p g o d", g=KVH, o=1)
                                  .to_broadcast([P, KVH, 2, HD])).then_inc(rope_made, 1)
        low_upto(12)

        def sb_m(p):
            s, meta = SB_BANKS[p], SB_META[p]
            if p:
                dve.wait_ge(sbs_filled, p)
            dve.wait_ge(sb_log_made, 2 * p + 2)
            nc.vector.scalar_tensor_tensor(sb_m_[:, :, :], ps[:, s:s + 2, 0:3 * P], 0.0, sb_a[:, :, :], ALU.max, ALU.add).then_inc(sb_m_made, 1)
            nc.vector.scalar_tensor_tensor(sb_mm[:, :], ps[0:META, meta, :], 0.0, sb_am[:, :], ALU.max, ALU.add).then_inc(sb_m_made, 1)

        for p in range(4):
            sb_m(p)
            if p >= 2:
                low_upto(11 + p)
        for b in range(NB):
            dve.wait_ge(sbo_filled, 4)
            nc.vector.tensor_tensor(qkv[:, b, SBO:SBO + SBW], ps[:, 6 + b, :], z_sb[:, b, :], ALU.mult).then_inc(sbo_made, 1)
        def sw_max(w):
            g = w % 2
            dve.wait_ge(sc_filled, w + 1)
            step(nc.vector.tensor_reduce(mx[:, :].rearrange("p (q r) -> p r q", r=2),
                                         ps[:, 0:4, :].rearrange("p (r a) (u n) -> p r (a u) n", r=2, u=2), AX.X, ALU.max))
            step(nc.vector.tensor_tensor(mx[:, :], mx[:, :], sinks[:, 8 * g:8 * g + 8], ALU.max))
            if w:
                dve.wait_ge(den_made, w)
            nc.vector.tensor_scalar(nmax[:, :], mx[:, :], -1.0, None, ALU.mult).then_inc(max_made, 1)
            nc.vector.tensor_tensor(esink[:, :], sinks[:, 8 * g:8 * g + 8], mx[:, :], ALU.subtract).then_inc(max_made, 1)

        sw_max(0)
        for w in range(4):
            b = w // 2
            g = w % 2
            dve.wait_ge(sink_made, w + 1)
            step(nc.vector.tensor_tensor(den2[:, :], den[:, :], esink[:, :], ALU.add))
            nc.vector.reciprocal(rden[:, :], den2[:, :]).then_inc(den_made, 1)
            for fl in (1, 3):
                k = 4 * w + fl
                dve.wait_ge(pt_filled, k + 1)
                if k >= 2:
                    dve.wait_ge(pv_done, k - 1)
                nc.vector.tensor_copy(pt[:, 1, :], ps[:, TP[1], :]).then_inc(pt_dve, 1)
                if fl == 1 and w < 3:
                    sw_max(w + 1)
            dve.wait_ge(pv_done, 4 * w + 4)
            dve.wait_ge(den_made, w + 1)
            part = qkv[:, b, SWO + 512 * g:SWO + 512 * g + 512]
            nc.vector.tensor_tensor(part.rearrange("p (h d) -> p h d", h=8), ps[:, 6, :].rearrange("p (h d) -> p h d", h=8),
                                    rden[:, :].rearrange("p (h o) -> p h o", o=1).to_broadcast([P, 8, HD]),
                                    ALU.mult).then_inc(swo_made, 1)
            dve.wait_ge(swo_made, w + 1)
            dve.wait_ge(bz_read, 2 * (11 if w == 0 else SW_FIRST) + 2)
            nc.vector.tensor_tensor(part, part, z_sw[:, b, 512 * g:512 * g + 512], ALU.mult).then_inc(swz_made, 1)
            if w < 3:
                low_upto(SW_FIRST + w + 2)
        for q in range(SW_FIRST + 3, BCH_IN):
            low_upto(q + 2)
            if q == SW_FIRST + 3:
                for m in range(2):
                    dve.wait_ge(ot_hi, m + 1)
                    nc.vector.tensor_tensor(sbT_lo[:, 2 * m:2 * m + 2, :], ps[:, TP[m], :].rearrange("p (t n) -> p t n", t=2),
                                            f(sbT_hi[:, 2 * m:2 * m + 2, :]), ALU.subtract).then_inc(ot_lo, 1)
        xt_low(5, 0)
        xt_low(5, 1)
        low_upto(23)
        for b in range(NB):
            for half_ in range(2):
                c = slice(half_ * 512, half_ * 512 + 512)
                dve.wait_ge(bw_used, BCH_IN + BCH_SB)
                dve.wait_ge(bz_read, 2 * BCH_IN)
                nc.vector.tensor_tensor(merged[:, b, c], ps[:, DOWN[2 * b + half_], :], gsig[:, 0, b, c], ALU.mult).then_inc(merged_made, 1)
        low_upto(25)
        low_upto(27)
        for b in range(NB):
            for half_ in range(2):
                c = slice(half_ * 512, half_ * 512 + 512)
                g2 = gsig[:, 1, b, c]
                dve.wait_ge(bw_used, BCH_IN + BCH_SB + BCH_SW)
                step(nc.vector.tensor_tensor(g2, ps[:, merge_bank(b, half_), :], g2, ALU.mult))
                nc.vector.tensor_tensor(merged[:, b, c], merged[:, b, c], g2, ALU.add).then_inc(merged_made, 1)
        xt_low(6, 0)
        xt_low(6, 1)
        low_upto(29)
        def add_last(b):
            for half_ in range(2):
                part = x[:, b, half_ * 512:half_ * 512 + 512]
                if b == 0:
                    dve.wait_ge(acc_ready, 4)
                else:
                    dve.wait_ge(bw_used, BCH_IN + BCH_SB + BCH_SW + BCH_OUT)
                nc.vector.tensor_tensor(part, part, ps[:, DOWN[2 * b + half_], :], ALU.add).then_inc(x2_made, 1)

        add_last(0)
        norm_apply(6, xn, 0)
        add_last(1)
        dve.wait_ge(x2_made, 4)
        norm_sum(6)
        norm_apply(6, xn, 1)


    def second_tensor(pe, n_items, norm_transposes):
        keep_warm(3, 16)
        pe.wait_ge(meta_made, 1)
        for k in range(KT):
            mm = nc.tensor.transpose(ps[:, 2, k * META:k * META + META], xm[:, k * P:k * P + P], ident[0:META, 0:META])
        mm.then_inc(mt_filled, 1)
        keep_warm(3, 16)
        norm_transposes(5, 4, 0)
        norm_transposes(5, 4, 1)
        pe.wait_ge(mt_lo_made, 1)
        pe.wait_ge(xt_lo, 20)

        def tile_block(q, b, bank, kts):
            wh, wl = (slot_view(r, q % SPLITS, KT, Q2W) for r in (highb, lowb))
            for k in kts:
                mm = three(ps[:, bank, 0:Q2W], xT_hi[:, k, b * P:b * P + P], xT_lo[:, k, b * P:b * P + P],
                           wh[:, k, :], wl[:, k, :], k == 0, k == KT - 1)
            return mm

        def input_tile(q, first_bank=None):
            pe.wait_ge(blo_made, q + 1)
            if q in META_TILES:
                lo, hi, _ = META_TILES[q]
                n = META_ORDER.index(q)
                wh, wl = (slot_view(r, q % SPLITS, KT, Q2W) for r in (highb, lowb))
                if n >= 2:
                    pe.wait_ge(meta_read, n - 1)
                for k in range(KT):
                    three(ps[:, 6 + n % 2, 0:hi - lo], mT_hi[:, k, :], mT_lo[:, k, :], wh[:, k, lo:hi], wl[:, k, lo:hi],
                          k == 0, k == KT - 1)
            for b in range(NB):
                mm = tile_block(q, b, (2 * (q % 2) if first_bank is None else first_bank) + b, range(KT))
            mm.then_inc(bw_used, 1)

        def wait_read(q):
            pe.wait_ge(bz_read, 2 * q + 2)

        for q in range(11):
            if q >= 2:
                wait_read(q - 2)
            input_tile(q)
        pe.wait_ge(rope_made, 2)
        for n in range(10):
            if n >= 2:
                pe.wait_ge(qk_made, n - 1)
            bank = TP[n % 2]
            if n == 4:
                for t in range(4):
                    nc.tensor.transpose(ps[:, bank, t * META:t * META + META], meta_kv[0:META, t * P:t * P + P], ident[0:META, 0:META])
                for t in range(2):
                    mm = nc.tensor.transpose(ps[:, bank, (4 + t) * META:(5 + t) * META], swkm[:, t * P:t * P + P],
                                             ident[0:META, 0:META])
            else:
                for t in range(2):
                    for b in range(NB):
                        if n < 4:
                            first = (O_SBQ if n < 2 else O_SBK) + (2 * (n % 2) + t) * P
                            src = qkv[:, b, first:first + P]
                        elif n == 5:
                            src = swkk[:, b, t * P:t * P + P]
                        else:
                            first = O_SWQ + (2 * (n - 6) + t) * P
                            src = qkv[:, b, first:first + P]
                        mm = nc.tensor.transpose(ps[:, bank, (2 * t + b) * P:(2 * t + b + 1) * P], src, ident)
            mm.then_inc(qk_filled, 1)
        pe.wait_ge(qk_made, 10)
        pe.wait_ge(masks_made, 3)
        mmx = dict(skip_group_check=True)

        def sb_scores(p):
            s, meta = SB_BANKS[p], SB_META[p]
            if p == 0:
                wait_read(9)
            elif p == 2:
                wait_read(12)
            else:
                pe.wait_ge(sb_w_made, 2 if p == 1 else 4)
            for r in range(2):
                rows = slice(64 * r, 64 * r + 64)
                nc.tensor.matmul(ps[:, s + r, 0:T], sbkT[rows, p, 0:P], sbqT[rows, p, :], start=True, stop=False, **mmx)
                nc.tensor.matmul(ps[:, s + r, T:3 * P], sbkT[rows, p, P:T], sbqT[rows, p, P:T], start=False, stop=False, **mmx)
                nc.tensor.matmul(ps[:, s + r, 0:P], identb[:, :], sbm[:, :], start=False, stop=False, **mmx)
                nc.tensor.matmul(ps[:, s + r, T:3 * P], identb[:, :], sbm[:, :], start=False, stop=False, **mmx)
                mm = nc.tensor.matmul(ps[0:META, meta, r * T:r * T + T], sbkTm[:, p, r, :], sbqT[:, p, :],
                                      start=(r == 0), stop=False, **mmx)
            mm.then_inc(sbz_filled, 1)

        def sb_suffix(p):
            s, meta = SB_BANKS[p], SB_META[p]
            pe.wait_ge(sb_m_made, 2 * p + 2)
            for r in range(2):
                nc.tensor.matmul(ps[:, s + r, 0:T], upto, sb_m_[:, r, 0:T], start=False, stop=False, **mmx)
                nc.tensor.matmul(ps[:, s + r, T:3 * P], upto, sb_m_[:, r, T:3 * P], start=False, stop=False, **mmx)
                nc.tensor.matmul(ps[:, s + r, P:T], minus_ones, sb_m_[:, r, T:3 * P], start=False, stop=True, **mmx)
                c = r * T
                nc.tensor.matmul(ps[0:META, meta, c:c + T], upto[0:META, 0:META], sb_mm[:, c:c + T], start=False, stop=False, **mmx)
                nc.tensor.matmul(ps[0:META, meta, c:c + T], minus_ones[:, 0:META], sb_m_[:, r, 0:T], start=False, stop=False, **mmx)
                mm = nc.tensor.matmul(ps[0:META, meta, c + P:c + T], minus_ones[:, 0:META], sb_m_[:, r, T:3 * P],
                                      start=False, stop=True, **mmx)
            mm.then_inc(sbs_filled, 1)

        def sb_output(p):
            pe.wait_ge(sb_w_made, 2 * p + 2)
            for r in range(2):
                c = HD * (2 * p + r)
                v0, v1 = (qkv[:, b, O_SBV + c:O_SBV + c + HD] for b in range(NB))
                vm = meta_kv[0:META, 512 + c:512 + c + HD]
                o0, o1 = (ps[:, 6 + b, c:c + HD] for b in range(NB))
                nc.tensor.matmul(o0, sb_w[:, r, 0:P], v0, start=True, stop=False)
                nc.tensor.matmul(o0, sb_wm[:, r * T:r * T + P], vm, start=False, stop=True)
                nc.tensor.matmul(o1, sb_w[:, r, P:T], v0, start=True, stop=False)
                nc.tensor.matmul(o1, sb_w[:, r, T:3 * P], v1, start=False, stop=False)
                mm = nc.tensor.matmul(o1, sb_wm[:, r * T + P:r * T + T], vm, start=False, stop=True)
            mm.then_inc(sbo_filled, 1)

        sb_scores(0)
        wait_read(10)
        input_tile(11, 0)
        keep_warm(5, 14)
        sb_suffix(0)
        pe.wait_ge(blo_made, 13)
        wait_read(11)
        tile_block(12, 0, 0, range(KT))
        sb_output(0)
        sb_scores(1)
        tile_block(12, 1, 1, range(KT)).then_inc(bw_used, 1)
        keep_warm(5, 36)
        sb_suffix(1)
        sb_scores(2)
        sb_output(1)
        sb_scores(3)
        sb_suffix(2)
        sb_output(2)
        sb_suffix(3)
        sb_output(3)

        def sw_scores(w):
            b, g = w // 2, w % 2
            if w:
                pe.wait_ge(prob_made, 8 * w)
            else:
                pe.wait_ge(sb_w_made, 8)
            for n in range(8):
                bank, c = sw_place(n)
                rows, tile = slice(64 * (n % 2), 64 * (n % 2) + 64), 4 * g + n // 2
                if c == 0:
                    nc.tensor.matmul(ps[:, bank, :].rearrange("p (u n) -> p u n", u=2), identb[:, :],
                                     swm[:, b:b + 1, :].to_broadcast([P, 2, T]), start=True, stop=False, **mmx)
                qT = swqT[rows, tile, b * P:b * P + P]
                if b == 0:
                    nc.tensor.matmul(ps[:, bank, c:c + META], qT, swkTm[rows, g, :], start=False, stop=False, **mmx)
                    mm = nc.tensor.matmul(ps[:, bank, c + P:c + T], qT, swkT[rows, g, 0:P], start=False, stop=True, **mmx)
                else:
                    mm = nc.tensor.matmul(ps[:, bank, c:c + T], qT, swkT[rows, g, :], start=False, stop=True, **mmx)
            mm.then_inc(sc_filled, 1)

        def pt_fill(w, fl):
            k = 4 * w + fl
            if k >= 2:
                pe.wait_ge(pt_act if k % 2 == 0 else pt_dve, k // 2)
            else:
                pe.wait_ge(qk_made, 10)
            pe.wait_ge(prob_made, 8 * w + 2 * fl + 2)
            for n in range(2):
                for kb in range(2):
                    mm = nc.tensor.transpose(ps[:, TP[k % 2], (2 * n + kb) * P:(2 * n + kb + 1) * P],
                                             prob[:, 2 * fl + n, kb * P:kb * P + P], ident)
            mm.then_inc(pt_filled, 1)

        def sw_output(w, fl):
            b, g = w // 2, w % 2
            k = 4 * w + fl
            pe.wait_ge(pt_act if k % 2 == 0 else pt_dve, k // 2 + 1)
            if fl == 0:
                if w:
                    pe.wait_ge(swo_made, w)
                else:
                    pe.wait_ge(sbo_made, 1)
            vc = O_SWV + HD * g
            for n in range(2):
                c = HD * (2 * fl + n)
                o = ps[:, 6, c:c + HD]
                if b == 0:
                    nc.tensor.matmul(o, pt[0:META, k % 2, 2 * n * P:2 * n * P + P], meta_kv[0:META, 1152 + HD * g:1152 + HD * g + HD],
                                     start=True, stop=False)
                else:
                    nc.tensor.matmul(o, pt[:, k % 2, 2 * n * P:2 * n * P + P], qkv[:, 0, vc:vc + HD], start=True, stop=False)
                mm = nc.tensor.matmul(o, pt[:, k % 2, (2 * n + 1) * P:(2 * n + 2) * P], qkv[:, b, vc:vc + HD],
                                      start=False, stop=True)
            mm.then_inc(pv_done, 1)

        def gate_block(w, b):
            if w < 3:
                q = SW_FIRST + w
                pe.wait_ge(blo_made, q + 1)
                if w == 0 and b == 0:
                    pe.wait_ge(sbo_made, 2)
                else:
                    pe.wait_ge(bz_read, 2 * q + b)
                tile_block(q, b, 7, range(KT)).then_inc(bw_used if b else block_ready, 1)

        sw_scores(0)
        for w in range(4):
            gate_block(w, 0)
            pt_fill(w, 0)
            pt_fill(w, 1)
            sw_output(w, 0)
            if w < 3:
                sw_scores(w + 1)
            pt_fill(w, 2)
            sw_output(w, 1)
            gate_block(w, 1)
            pt_fill(w, 3)
            sw_output(w, 2)
            sw_output(w, 3)
        pe.wait_ge(prob_made, 32)
        for q in range(SW_FIRST + 3, BCH_IN):
            if q >= SW_FIRST + 5:
                wait_read(q - 2)
            input_tile(q)
            if q == SW_FIRST + 3:
                pe.wait_ge(sbo_made, 2)
                for m in range(2):
                    for t in range(2):
                        for b in range(NB):
                            first = SBO + (2 * m + t) * P
                            mm = nc.tensor.transpose(ps[:, TP[m], (2 * t + b) * P:(2 * t + b + 1) * P], qkv[:, b, first:first + P], ident)
                    mm.then_inc(ot_filled, 1)
        pe.wait_ge(swz_made, 4)
        pe.wait_ge(ot_lo, 2)
        big_transposes(lambda b, k: qkv[:, b, SWO + k * P:SWO + k * P + P])
        pe.wait_ge(xt_lo, 24)

        def branch(c, tiles, hT, lT, acc, first, last):
            pe.wait_ge(blo_made, c + 1)
            out_last = c == BCH_IN + BCH_SB + BCH_SW + BCH_OUT - 1
            mm = row_product(hT, lT, tiles, c % SPLITS, acc, NB, first, last, (highb, lowb), acc_ready if out_last else None)
            mm.then_inc(bw_used, 1)

        def down_bank(b, half):
            return DOWN[2 * b + half]

        wait_read(BCH_IN - 1)
        for n in range(BCH_SB):
            branch(BCH_IN + n, (2 * n, 2 * n + 1), sbT_hi, sbT_lo, down_bank, n == 0, n == BCH_SB - 1)
        for n in range(BCH_SW):
            branch(BCH_IN + BCH_SB + n, (2 * n, 2 * n + 1), xT_hi, xT_lo, merge_bank, n == 0, n == BCH_SW - 1)
        pe.wait_ge(merged_made, 4)
        keep_warm(DOWN[0], 44)
        pe.wait_ge(merged_made, 8)
        big_transposes(lambda b, k: merged[:, b, k * P:k * P + P])
        pe.wait_ge(xt_lo, 28)
        for n in range(BCH_OUT):
            branch(26 + n, (2 * n, 2 * n + 1), xT_hi, xT_lo, down_bank, n == 0, n == BCH_OUT - 1)

    def big_transposes(src):
        for b in range(NB):
            for m in range(2):
                for kk in range(4):
                    mm = nc.tensor.transpose(ps[:, 4 + 2 * b + m, kk * P:kk * P + P], src(b, 4 * m + kk), ident)
                mm.then_inc(xt_filled, 1)

    DENSE_AFTER = {2: (0,), 4: (1,), 6: (2, 3), 8: (4,), 10: (5,), 12: (6, 7), 14: (8,), 16: (9, 10)}

    def dense_free(q):
        return -(-(-(-TW * (q - 3) // P)) // 2)

    def dense_transposes(pe, j):
        for m in DENSE_AFTER.get(j, ()):
            pe.wait_ge(mult_made, 2 * (-(-(2 * m + 2) * P // TW)))
            if m >= 2:
                pe.wait_ge(ht_lo, m - 1)
            for kk in range(2):
                t = (2 * m + kk) % (4 * TW // P)
                for b in range(NB):
                    mm = nc.tensor.transpose(ps[:, TP[m % 2], (2 * kk + b) * P:(2 * kk + b + 1) * P],
                                             h[:, b, t * P:t * P + P], ident)
            mm.then_inc(ht_filled, 1)

    with nc.Block() as block:

        @block.sync
        def _(sp):
            for b in range(NB):
                sp.dma_start(x[:, b, :], a["x"][0, b * P:b * P + P, :]).then_inc(x_landed[b], 16)
            sp.dma_start(gain[:, :], a["norm_mix"][0:1, :].to_broadcast([P, D])).then_inc(gain_landed[0], 16)
            sp.dma_start(small[:, :], a["c_small"]).then_inc(small_landed, 16)
            c = 0
            for l in range(2):
                for j in range(MIX_CHUNKS):
                    load(sp, c, mixer_source(l, j))
                    c += 1
                if l == 0:
                    for j in range(FFN_CHUNKS):
                        load(sp, c, ffn_source(j))
                        c += 1
            for j in range(FFN_CHUNKS):
                load(sp, c, expert_source(0, j))
                c += 1
            with sp.Fori(1, NE) as i:
                for j in range(FFN_CHUNKS):
                    load_item(sp, i, j, expert_source(i, j))
            sp.wait_ge(routed, 1)
            n_items = sp.value_load(plan[0:1, 3:4], min_val=NE - 1, max_val=ITEMS - 1) + 1
            with sp.Fori(NE, ITEMS) as i:
                with sp.If(i < n_items):
                    e = sp.value_load(plan[0:1, bass.ds(i - NE, 1)], min_val=0, max_val=NE - 1)
                    for j in range(FFN_CHUNKS):
                        load_item(sp, i, j, expert_source(e, j))
            second_loads(sp, n_items)

        @block.gpsimd
        def _(pool):
            def load_gain(n, src):
                pool.wait_ge(xn_made, 2 * n)
                pool.dma_start(gain[:, :], src.to_broadcast([P, D])).then_inc(gain_landed[1], 16)

            def load_mix(l):
                rows = rows16[:, :]
                pool.dma_start(cmix[:, :], a["c_mix"]).then_inc(mix_landed, 16)
                pool.dma_start(rows[0:4, :], a["sgu_b"][l]).then_inc(mix_landed, 16)
                for n, name in enumerate(("conv_b", "conv_ng", "conv_nb")):
                    pool.dma_start(rows[4 + 4 * n:8 + 4 * n, :], a[name][l].rearrange("(t p) -> t p", p=P)).then_inc(mix_landed, 16)
                pool.dma_start(conv_rows[:, :], a["conv_w"][l, :, 0, :]).then_inc(mix_landed, 16)
                pool.dma_start(sgu_rows[:, :, :], a["sgu_w"][l].rearrange("h t s -> t h s")).then_inc(mix_landed, 16)
                pool.dma_start(sgu_g[:, :], a["sgu_ng"][l:l + 1, :].to_broadcast([P, CC])).then_inc(mix_landed, 16)
                pool.dma_start(sgu_o[:, :], a["sgu_nb"][l:l + 1, :].to_broadcast([P, CC])).then_inc(mix_landed, 16)

            def diagonals(l):
                pool.wait_ge(prep_made, 2 * l + 2)
                for k in range(TAPS):
                    if k * P == NB * D:
                        pool.wait_ge(ct_filled, 2 * l + 2)
                    w = cols[:, 16 + TAPS * PE_TILE + k:17 + TAPS * PE_TILE + k]
                    ins = pool.tensor_scalar(diag[:, k, :], ident, w, None, ALU.mult)
                ins.then_inc(diag_made, 1)

            def sgu_gain(l):
                for b in range(NB):
                    pool.wait_ge(vnorm_made, NB * SH * l + SH * (b + 1))
                    pool.tensor_tensor(v[:, b, :], v[:, b, :], sgu_g[:, :], ALU.mult).then_inc(vg_made, 1)
                    pool.wait_ge(vg_made, NB * l + b + 1)
                    pool.tensor_tensor(v[:, b, :], v[:, b, :], sgu_o[:, :], ALU.add).then_inc(vn_made, 1)

            load_mix(0)
            pool.dma_start(croute[:, :], a["c_route"]).then_inc(route_landed, 16)
            pool.dma_start(router[:, :, :], a["moe_router"][0].rearrange("(t p) e -> p t e", p=P)).then_inc(route_landed, 16)
            pool.wait_ge(small_landed, 16)
            pool.wait_ge(mix_landed, 16 * 9)
            diagonals(0)
            sgu_gain(0)
            load_gain(1, a["norm_ffn"][0:1, :])
            load_gain(2, a["norm_mix"][1:2, :])
            pool.wait_ge(x_made, 8)
            load_mix(1)
            pool.wait_ge(mix_landed, 16 * 18)
            diagonals(1)
            sgu_gain(1)
            load_gain(3, a["norm_ffn"][1:2, :])
            load_gain(4, a["norm_final"].rearrange("(o d) -> o d", o=1))
            second_small_loads(pool)
            load_gain(5, a["final_norm_gain_2"].rearrange("(o d) -> o d", o=1))

        @block.scalar
        def _(act):
            made = [0]
            tables = [0]

            def high_upto(c):
                while made[0] <= c:
                    make_high(act, made[0])
                    made[0] += 1

            def prepare(func):
                tables[0] += 1
                nc.scalar.activation(unused[:, tables[0] - 1:tables[0]], eps[:, :], func)

            def norm_std(n, b):
                if b == 0:
                    nc.scalar.activation(xn[:, 0, :], x[:, 0, :], ACT.Square, accum_out=sumsq[:, 0:1]).then_inc(sumsq_made[0], 1)
                act.wait_ge(sumsq_made[b], n + 1)
                nc.scalar.activation(std[:, b:b + 1], sumsq[:, b:b + 1], ACT.Sqrt, bias=eps[:, 0:1], scale=1.0 / D).then_inc(std_made, 1)

            def xt_high(tn, b):
                for m in range(2):
                    act.wait_ge(xt_filled, 4 * tn + 2 * b + m + 1)
                    nc.scalar.activation(xT_hi[:, 4 * m:4 * m + 4, b * P:b * P + P],
                                         ps[:, 4 + 2 * b + m, :].rearrange("p (t n) -> p t n", t=4), ACT.Copy).then_inc(xt_hi, 1)

            def norm(n, tn):
                norm_std(n, 0)
                xt_high(tn, 0)
                norm_std(n, 1)
                xt_high(tn, 1)

            def mixer(l):
                c0 = LAYER_CHUNKS * l
                high_upto(c0 + 3)
                for b in range(NB):
                    act.wait_ge(w_used, c0 + 2)
                    nc.scalar.activation(sig[:, b, :], ps[:, b, :], ACT.Sigmoid).then_inc(sig_made, 1)
                high_upto(c0 + 6)
                for m in range(2):
                    act.wait_ge(ct_filled, 2 * l + m + 1)
                    nc.scalar.activation(cT[:, 2 * m:2 * m + 2, TAPS - 1:], ps[:, TP[m], :].rearrange("p (t n) -> p t n", t=2),
                                         ACT.Copy).then_inc(ct_made, 1)
                high_upto(c0 + 7)
                for b in range(NB):
                    act.wait_ge(w_used, c0 + 6)
                    nc.scalar.activation(v[:, b, :], ps[:, b, :], ACT.Gelu).then_inc(v_made, 1)
                high_upto(c0 + 8)
                prepare(ACT.Sqrt)
                act.wait_ge(vvar_made, NB * SH * (l + 1))
                nc.scalar.activation(vstd[:, :], vmv[:, :, 1], ACT.Sqrt, bias=eps[:, 0:1]).then_inc(vstd_made, 1)
                for n in range(NB * SH):
                    act.wait_ge(vnorm_ready, l + 1)
                    b, hh = n // SH, n % SH
                    part = v[:, b, hh * P:hh * P + P]
                    nc.scalar.activation(part, part, ACT.Identity, bias=vmv[:, n, 0:1], scale=vrstd[:, n:n + 1]).then_inc(vnorm_made, 1)
                high_upto(c0 + 9)
                for b in range(NB):
                    act.wait_ge(w_used, c0 + 8)
                    nc.scalar.activation(u[:, b, :], ps[:, 2 + b, :], ACT.Gelu).then_inc(u_made, 1)
                high_upto(c0 + 10)
                act.wait_ge(pe_conv, l + 1)
                nc.scalar.activation(yT[:, PE_TILE, :], ps[:, 6, 0:T], ACT.Identity,
                                     bias=cols[:, 4 + PE_TILE:5 + PE_TILE]).then_inc(y2_made, 1)
                for m in range(2):
                    act.wait_ge(gt_filled, 2 * l + m + 1)
                    nc.scalar.activation(xT_hi[:, 4 + 2 * m:6 + 2 * m, :], ps[:, TP[m], :].rearrange("p (t n) -> p t n", t=2),
                                         ACT.Copy).then_inc(cat_hi, 1)
                high_upto(c0 + 11)
                prepare(ACT.Sqrt)
                for m in range(2):
                    act.wait_ge(yc_filled, 2 * l + m + 1)
                    nc.scalar.activation(sq[:, 2 * m:2 * m + 2, :], ps[:, TP[m], :].rearrange("p (t n) -> p t n", t=2),
                                         ACT.Square).then_inc(sq_made, 1)
                act.wait_ge(var_filled, l + 1)
                nc.scalar.activation(std8[:, :], ps[0:8, 2, 0:T], ACT.Sqrt, bias=eps[0:8, 0:1]).then_inc(std8_made, 1)
                prepare(ACT.Silu)
                for m in range(2):
                    act.wait_ge(yn_made, 2 * l + m + 1)
                    for t in (2 * m, 2 * m + 1):
                        ins = nc.scalar.activation(sq[:, t, :], yT[:, t, :], ACT.Silu, scale=cols[:, 8 + t:9 + t],
                                                   bias=cols[:, 12 + t:13 + t])
                        ins.then_inc(cs_made, 1)
                    act.wait_ge(cs_made, 4 * l + 2 * m + 2)
                    nc.scalar.activation(xT_hi[:, 2 * m:2 * m + 2, :], sq[:, 2 * m:2 * m + 2, :], ACT.Copy).then_inc(cat_hi, 1)

            act.wait_ge(eps_made, 1)
            prepare(ACT.Sqrt)
            act.wait_ge(x_landed[0], 16)
            norm_std(0, 0)
            norm_std(0, 1)
            high_upto(0)
            xt_high(0, 0)
            xt_high(0, 1)
            mixer(0)
            c0 = MIX_CHUNKS
            high_upto(c0 + 1)
            prepare(ACT.Sqrt)
            act.wait_ge(x_made, 2)
            norm(1, 1)

            def dense_silu(q):
                for b in range(NB):
                    act.wait_ge(w_used, MIX_CHUNKS + 2 * q + 1)
                    if q >= 4:
                        act.wait_ge(ht_filled, dense_free(q))
                    nc.scalar.activation(h[:, b, (q % 4) * TW:(q % 4) * TW + TW], ps[:, b, :][:, 0:TW], ACT.Silu).then_inc(silu_made, 1)

            def dense_hidden_high(m):
                act.wait_ge(ht_filled, m + 1)
                nc.scalar.activation(hT_hi[:, 2 * m:2 * m + 2, :], ps[:, TP[m % 2], :].rearrange("p (t n) -> p t n", t=2),
                                     ACT.Copy).then_inc(ht_hi, 1)

            for j in range(FFN_CHUNKS):
                high_upto(c0 + min(j + 2, FFN_CHUNKS + 1))
                if j < 16 and j % 2 == 0:
                    dense_silu(j // 2)
                for m in DENSE_AFTER.get(j, ()):
                    dense_hidden_high(m)
            act.wait_ge(route_landed, 32)
            nc.scalar.activation(router_hi[:, :, :], router[:, :, :], ACT.Copy).then_inc(router_hi_made, 1)
            prepare(ACT.Sqrt)
            act.wait_ge(x_made, 6)
            norm(2, 2)
            mixer(1)
            high_upto(MOE0 + 1)
            prepare(ACT.Sqrt)
            act.wait_ge(x_made, 10)
            norm(3, 3)
            for b in range(NB):
                nc.scalar.activation(xn_hi[:, b, :], xn[:, b, :], ACT.Copy).then_inc(xs_hi, 1)
            prepare(ACT.Exp)
            act.wait_ge(logit_made, 1)
            nc.scalar.activation(share[:, :, :], share[:, :, :], ACT.Exp).then_inc(expo_made, 1)

            def gathered_high(fill, p):
                act.wait_ge(tp_filled, fill + 1)
                nc.scalar.activation(xe_hi[:, p * 2 * P:(p + 1) * 2 * P], ps[:, TP[p % 2], 0:2 * P], ACT.Copy).then_inc(tp_hi, 1)

            def item(i, mh, finish):
                first = isinstance(i, int)
                if not first:
                    mh(i, 0)
                    mh(i, 1)
                if not first:
                    finish(i)
                mh(i, 2)
                for j in range(3, FFN_CHUNKS + 2):
                    if j < FFN_CHUNKS:
                        mh(i, j)
                    c = j - 2
                    if c < 16 and c % 4 == 1:
                        g = c // 4
                        act.wait_ge(w_used, chunk(i, c) + 1)
                        if first and g == 0:
                            act.wait_ge(routed, 1)
                        for t in range(2):
                            nc.scalar.activation(eh[:, g * GW + t * TW:g * GW + t * TW + TW], ps[:, t, 0:TW],
                                                 ACT.Silu).then_inc(esilu_made, 1)
                    if c in AFTER_T:
                        n = AFTER_T[c]
                        lo, hi = BATCHES[n]
                        act.wait_ge(tp_filled, fill_no(i, 6 + n) + 1)
                        nc.scalar.activation(eT_hi[:, lo:hi, :].rearrange("p t n -> p (t n)"),
                                             ps[:, TP[n % 2], 0:(hi - lo) * P], ACT.Copy).then_inc(tp_hi, 1)
                    for p in GATHER_AFTER.get(c, ()):
                        gathered_high(fill_no(i, 12 + p), p)

            def finish(i):
                act.wait_ge(w_used, chunk(i, 0))
                for half in range(2):
                    nc.scalar.activation(eo_hi[:, half * 512:half * 512 + 512], ps[:, 6 + half, :], ACT.Copy).then_inc(eo_hi_made, 1)

            def static_high(i, j):
                if chunk(0, j) >= made[0]:
                    high_upto(chunk(0, j))

            def high_item(i, j):
                make_high_item(act, i, j)

            for p in range(4):
                gathered_high(p, p)
            item(0, static_high, finish)
            with act.Fori(1, NE) as i:
                item(i, high_item, finish)
            act.wait_ge(routed, 1)
            n_items = act.value_load(plan[0:1, 3:4], min_val=NE - 1, max_val=ITEMS - 1) + 1
            with act.Fori(NE, ITEMS) as i:
                with act.If(i < n_items):
                    item(i, high_item, finish)
            finish(n_items)
            second_scalar(act, n_items, prepare, norm_std, xt_high)

        @block.vector
        def _(dve):
            made = [0]
            steps = [0]

            def low_upto(c):
                while made[0] <= c:
                    make_low(dve, made[0])
                    made[0] += 1

            def step(ins):
                steps[0] += 1
                ins.then_inc(dve_steps, 1)
                dve.wait_ge(dve_steps, steps[0])

            def norm_sum(n):
                nc.vector.tensor_tensor_reduce(out=xn[:, 1, :], in0=x[:, 1, :], in1=x[:, 1, :], scale=1.0, scalar=0.0,
                                               op0=ALU.mult, op1=ALU.add, accum_out=sumsq[:, 1:2]).then_inc(sumsq_made[1], 1)

            def norm_apply(n, target, b):
                dve.wait_ge(std_made, 2 * n + b + 1)
                nc.vector.reciprocal(rstd[:, b:b + 1], std[:, b:b + 1]).then_inc(rstd_made, 1)
                dve.wait_ge(rstd_made, 2 * n + b + 1)
                if n == 5:
                    dve.wait_ge(gain_b_landed, 16)
                else:
                    dve.wait_ge(gain_landed[min(n, 1)], 16 * max(n - (n == 6), 1))
                nc.vector.scalar_tensor_tensor(target[:, b, :], x[:, b, :], rstd[:, b:b + 1], (gain_b if n == 5 else gain)[:, :], ALU.mult,
                                               ALU.mult).then_inc(xn_made, 1)

            def xt_low(tn, b):
                for m in range(2):
                    dve.wait_ge(xt_hi, 4 * tn + 2 * b + m + 1)
                    nc.vector.tensor_tensor(xT_lo[:, 4 * m:4 * m + 4, b * P:b * P + P],
                                            ps[:, 4 + 2 * b + m, :].rearrange("p (t n) -> p t n", t=4),
                                            f(xT_hi[:, 4 * m:4 * m + 4, b * P:b * P + P]), ALU.subtract).then_inc(xt_lo, 1)

            def add_output(n, b):
                for half in range(2):
                    part = x[:, b, half * 512:half * 512 + 512]
                    if b == 0:
                        dve.wait_ge(acc_ready, n + 1)
                    else:
                        dve.wait_ge(w_used, (MIX_CHUNKS, LAYER_CHUNKS, MOE0)[n])
                    nc.vector.tensor_tensor(part, part, ps[:, DOWN[2 * b + half], :], ALU.add).then_inc(x_made, 1)

            def add_and_norm(n):
                add_output(n, 0)
                norm_apply(n + 1, xn, 0)
                add_output(n, 1)
                dve.wait_ge(x_made, 4 * n + 4)
                norm_sum(n + 1)
                xt_low(n + 1, 0)
                norm_apply(n + 1, xn, 1)
                low_upto((MIX_CHUNKS, LAYER_CHUNKS, MOE0)[n] + 1)
                xt_low(n + 1, 1)

            def mixer(l):
                c0 = LAYER_CHUNKS * l
                low_upto(c0 + 4)
                dve.wait_ge(prep_filled, 2 * l + 2)
                nc.vector.tensor_copy(cols[:, :], ps[:, 6, 0:16 + CT * TAPS]).then_inc(prep_made, 1)
                nc.vector.tensor_tensor(wsT[:, :, :], ps[:, 7, :].rearrange("p (h t) -> p h t", h=SH),
                                        causal.rearrange("p (o t) -> p o t", o=1).to_broadcast([P, SH, P]),
                                        ALU.mult).then_inc(prep_made, 1)
                low_upto(c0 + 5)
                for b in range(NB):
                    dve.wait_ge(w_used, c0 + 4)
                    dve.wait_ge(sig_made, 2 * l + b + 1)
                    nc.vector.tensor_tensor(c_tok[:, b, :], sig[:, b, :], ps[:, 2 + b, :], ALU.mult).then_inc(c_made, 1)
                nc.vector.memset(cT[:, :, 0:TAPS - 1], 0.0).then_inc(pad_made, 1)
                dve.wait_ge(pad_made, l + 1)
                low_upto(c0 + 6)
                dve.wait_ge(prep_made, 2 * l + 2)
                base = len(DVE_TILES) * TAPS * l

                def conv(first_tap, last_tap):
                    for k in range(first_tap, last_tap):
                        for n, t in enumerate(DVE_TILES, base + len(DVE_TILES) * k):
                            w = cols[:, 16 + TAPS * t + k:17 + TAPS * t + k]
                            src = cT[:, t, k:k + T]
                            if k == 0:
                                dve.wait_ge(ct_made, 2 * l + t // 2 + 1)
                                ins = nc.vector.tensor_scalar(yT[:, t, :], src, w, cols[:, 4 + t:5 + t], ALU.mult, ALU.add)
                            else:
                                dve.wait_ge(conv_step, n - len(DVE_TILES) + 1)
                                ins = nc.vector.scalar_tensor_tensor(yT[:, t, :], src, w, yT[:, t, :], ALU.mult, ALU.add)
                            ins.then_inc(conv_step, 1)

                conv(0, 2)
                low_upto(c0 + 7)
                conv(2, 3)
                for n in range(NB * SH):
                    b, hh = n // SH, n % SH
                    dve.wait_ge(v_made, 2 * l + b + 1)
                    nc.vector.bn_stats(vstat[:, n, :], v[:, b, hh * P:hh * P + P]).then_inc(vvar_stats, 1)
                for n in range(NB * SH):
                    dve.wait_ge(vvar_stats, NB * SH * l + n + 1)
                    nc.vector.bn_aggr(vmv[:, n, :], vstat[:, n, :]).then_inc(vvar_made, 1)
                conv(3, 5)
                dve.wait_ge(vstd_made, l + 1)
                step(nc.vector.reciprocal(vrstd[:, :], vstd[:, :]))
                nc.vector.scalar_tensor_tensor(vmv[:, :, 0], vmv[:, :, 0], -1.0, vrstd[:, :], ALU.mult,
                                               ALU.mult).then_inc(vnorm_ready, 1)
                low_upto(c0 + 8)
                conv(5, 12)
                low_upto(c0 + 9)
                for b in range(NB):
                    dve.wait_ge(sp_filled, 2 * l + b + 1)
                    dve.wait_ge(u_made, 2 * l + b + 1)
                    for hh in range(SH):
                        part = u[:, b, hh * P:hh * P + P]
                        ins = nc.vector.scalar_tensor_tensor(part, ps[:, b, hh * P:hh * P + P], cols[:, hh:hh + 1], part,
                                                             ALU.add, ALU.mult)
                    ins.then_inc(g_made, 1)
                conv(12, 19)
                for m in range(2):
                    dve.wait_ge(cat_hi, 4 * l + m + 1)
                    nc.vector.tensor_tensor(xT_lo[:, 4 + 2 * m:6 + 2 * m, :], ps[:, TP[m], :].rearrange("p (t n) -> p t n", t=2),
                                            f(xT_hi[:, 4 + 2 * m:6 + 2 * m, :]), ALU.subtract).then_inc(cat_lo, 1)
                low_upto(c0 + 10)
                conv(19, TAPS)
                low_upto(c0 + 11)
                for m in range(2):
                    dve.wait_ge(sq_made, 2 * l + m + 1)
                    nc.vector.tensor_copy(yT[:, 2 * m:2 * m + 2, :], ps[:, TP[m], :].rearrange("p (t n) -> p t n", t=2)
                                          ).then_inc(yc_made, 1)
                dve.wait_ge(std8_made, l + 1)
                nc.vector.reciprocal(rstd8[:, :], std8[:, :]).then_inc(rstd8_made, 1)
                for m in range(2):
                    dve.wait_ge(rb_filled, 2 * l + m + 1)
                    dve.wait_ge(yc_made, 2 * l + m + 1)
                    nc.vector.tensor_tensor(yT[:, 2 * m:2 * m + 2, :], yT[:, 2 * m:2 * m + 2, :],
                                            ps[:, 3 - m, :].rearrange("p (t n) -> p t n", t=2), ALU.mult).then_inc(yn_made, 1)
                for m in range(2):
                    dve.wait_ge(cat_hi, 4 * l + 3 + m)
                    nc.vector.tensor_tensor(xT_lo[:, 2 * m:2 * m + 2, :], sq[:, 2 * m:2 * m + 2, :],
                                            f(xT_hi[:, 2 * m:2 * m + 2, :]), ALU.subtract).then_inc(cat_lo, 1)
                low_upto(c0 + MIX_CHUNKS)

            nc.vector.memset(eps[:, :], EPS).then_inc(eps_made, 1)
            dve.wait_ge(x_landed[1], 16)
            norm_sum(0)
            for b in range(NB):
                dve.wait_ge(x_landed[b], 16)
                norm_apply(0, xn, b)
            low_upto(0)
            xt_low(0, 0)
            xt_low(0, 1)
            mixer(0)
            add_and_norm(0)
            c0 = MIX_CHUNKS

            for j in range(FFN_CHUNKS):
                low_upto(c0 + min(j + 2, FFN_CHUNKS + 1))
                if j < 16 and j % 2 == 1:
                    q = j // 2
                    for b in range(NB):
                        dve.wait_ge(w_used, MIX_CHUNKS + 2 * q + 2)
                        dve.wait_ge(silu_made, 2 * q + b + 1)
                        part = h[:, b, (q % 4) * TW:(q % 4) * TW + TW]
                        nc.vector.tensor_tensor(part, part, ps[:, 2 + b, 0:TW], ALU.mult).then_inc(mult_made, 1)
                for m in DENSE_AFTER.get(j, ()):
                    dve.wait_ge(ht_hi, m + 1)
                    nc.vector.tensor_tensor(hT_lo[:, 2 * m:2 * m + 2, :], ps[:, TP[m % 2], :].rearrange("p (t n) -> p t n", t=2),
                                            f(hT_hi[:, 2 * m:2 * m + 2, :]), ALU.subtract).then_inc(ht_lo, 1)
            dve.wait_ge(router_hi_made, 1)
            nc.vector.tensor_tensor(router_lo[:, :, :], router[:, :, :], f(router_hi[:, :, :]), ALU.subtract).then_inc(router_lo_made, 1)
            add_and_norm(1)
            mixer(1)
            add_and_norm(2)
            for b in range(NB):
                dve.wait_ge(xs_hi, b + 1)
                nc.vector.tensor_tensor(xn_lo[:, b, :], xn[:, b, :], f(xn_hi[:, b, :]), ALU.subtract).then_inc(xs_lo, 1)
            dve.wait_ge(logits_ready, 1)
            step(nc.vector.tensor_copy(logit[:, :, :], ps[:, 0, 0:NB * NE].rearrange("p (b e) -> p b e", b=NB)))
            step(nc.vector.tensor_reduce(top[:, :], logit[:, :, :], AX.X, ALU.max))
            nc.vector.tensor_tensor(share[:, :, :], logit[:, :, :],
                                    top[:, :].rearrange("p (b o) -> p b o", o=1).to_broadcast([P, NB, NE]),
                                    ALU.subtract).then_inc(logit_made, 1)
            for b in range(NB):
                other = logit[:, b:b + 1, :].to_broadcast([P, NE, NE])
                own = logit[:, b, :].rearrange("p (e o) -> p e o", o=1).to_broadcast([P, NE, NE])
                nc.vector.tensor_tensor(above[:, b, :, :], other, own, ALU.is_gt)
                step(nc.vector.tensor_tensor(equal[:, b, :, :], other, own, ALU.is_equal))
                step(nc.vector.tensor_tensor(equal[:, b, :, :], equal[:, b, :, :], earlier, ALU.mult))
                step(nc.vector.tensor_tensor(above[:, b, :, :], above[:, b, :, :], equal[:, b, :, :], ALU.add))
                step(nc.vector.tensor_reduce(rank[:, b, :], above[:, b, :, :], AX.X, ALU.add))
            nc.vector.tensor_scalar(chosen[:, :, :], rank[:, :, :], 1.5, None, ALU.is_lt).then_inc(chosen_made, 1)
            dve.wait_ge(chosen_made, 1)
            dve.wait_ge(expo_made, 1)
            step(nc.vector.tensor_tensor(share[:, :, :], share[:, :, :], chosen[:, :, :], ALU.mult))
            step(nc.vector.tensor_reduce(total[:, :], share[:, :, :], AX.X, ALU.add))
            step(nc.vector.reciprocal(total[:, :], total[:, :]))
            step(nc.vector.tensor_tensor(share[:, :, :], share[:, :, :],
                                         total[:, :].rearrange("p (b o) -> p b o", o=1).to_broadcast([P, NB, NE]), ALU.mult))
            dve.wait_ge(places_ready, 1)
            step(nc.vector.scalar_tensor_tensor(place_in[:, :, :], ps[:, 1, 0:NB * NE].rearrange("p (b e) -> p b e", b=NB), 1.0,
                                                chosen[:, :, :], ALU.add, ALU.mult))
            step(nc.vector.tensor_scalar(place_in[:, :, :], place_in[:, :, :], -1.0, None, ALU.add))
            step(nc.vector.tensor_scalar(crowd[:, :], ps[:, 1, NB * NE:(NB + 1) * NE], P + 0.5, None, ALU.is_gt))
            for b in range(NB):
                step(nc.vector.tensor_copy(items[:, 0:NE, b], place_in[:, b, :]))
                step(nc.vector.tensor_copy(items[:, 0:NE, 2 + b], share[:, b, :]))
            def add_scattered(pos, half):
                for b in range(NB):
                    part = x[:, b, half * 512:half * 512 + 512]
                    dve.wait_ge(tp_filled, pos + b + 1)
                    nc.vector.scalar_tensor_tensor(part, ps[:, TP[b], :], gates_now[:, b:b + 1], part, ALU.mult,
                                                   ALU.add).then_inc(tp_freed, 1)

            def finish(i):
                for half in range(2):
                    dve.wait_ge(eo_hi_made, 2 * i + half - 1)
                    nc.vector.tensor_tensor(eo_lo[:, half * 512:half * 512 + 512], ps[:, 6 + half, :],
                                            f(eo_hi[:, half * 512:half * 512 + 512]), ALU.subtract).then_inc(eo_lo_made, 1)

            def select(i):
                row = items[:, i:i + 1, :] if isinstance(i, int) else items[:, bass.ds(i, 1), :]
                nc.vector.tensor_copy(now[:, :], row[:, 0, 0:2]).then_inc(now_made, 1)
                dve.wait_ge(now_made, 2 * i + 1)
                for b in range(NB):
                    nc.vector.tensor_scalar(pick[:, b, :], iota, now[:, b:b + 1], None, ALU.is_equal).then_inc(pick_made, 1)

            def gathered_low(i, p):
                dve.wait_ge(tp_hi, 10 * i + p + 1)
                nc.vector.tensor_copy(xe_lo[:, p * 2 * P:(p + 1) * 2 * P], ps[:, TP[p % 2], 2 * P:4 * P]).then_inc(tp_freed, 1)

            def item(i, ml):
                first = isinstance(i, int)
                row = items[:, i:i + 1, :] if first else items[:, bass.ds(i, 1), :]
                ml(i, 0)
                ml(i, 1)
                if not first:
                    finish(i)
                ml(i, 2)
                for j in range(3, FFN_CHUNKS + 2):
                    if j < FFN_CHUNKS:
                        ml(i, j)
                    c = j - 2
                    if c < 16 and c % 4 == 3:
                        g = c // 4
                        dve.wait_ge(w_used, chunk(i, c) + 1)
                        for t in range(2):
                            dve.wait_ge(esilu_made, 8 * i + 2 * g + t + 1)
                            part = eh[:, g * GW + t * TW:g * GW + t * TW + TW]
                            nc.vector.tensor_tensor(part, part, ps[:, 2 + t, 0:TW], ALU.mult).then_inc(emult_made, 1)
                    if c == 3 and not first:
                        add_scattered(fill_no(i, 0), 0)
                    if c == 4 and not first:
                        add_scattered(fill_no(i, 2), 1)
                    if c == 4:
                        if not first:
                            dve.wait_ge(tp_freed, fill_no(i, 3) + 1)
                        nc.vector.tensor_copy(gates_now[:, :], row[:, 0, 2:4]).then_inc(now_made, 1)
                        dve.wait_ge(now_made, 2 * i + 2)
                    if c == 5:
                        for b in range(NB):
                            dve.wait_ge(tp_filled, fill_no(i, 4 + b) + 1)
                            nc.vector.tensor_copy(drop[:, b, :], ps[:, TP[b], 0:P]).then_inc(tp_freed, 1)
                    if c in AFTER_T:
                        n = AFTER_T[c]
                        lo, hi = BATCHES[n]
                        dve.wait_ge(tp_hi, 10 * i + 4 + n + 1)
                        nc.vector.tensor_tensor(eT_lo[:, lo:hi, :].rearrange("p t n -> p (t n)"), ps[:, TP[n % 2], 0:(hi - lo) * P],
                                                f(eT_hi[:, lo:hi, :]).rearrange("p t n -> p (t n)"),
                                                ALU.subtract).then_inc(tp_freed, 1)
                    if c == 16:
                        select(i + 1)
                    for p in GATHER_AFTER.get(c, ()):
                        gathered_low(i + 1, p)

            def static_low(i, j):
                if chunk(0, j) >= made[0]:
                    low_upto(chunk(0, j))

            def low_item(i, j):
                make_low_item(dve, i, j)

            select(0)
            for p in range(4):
                gathered_low(0, p)
            step(nc.vector.tensor_tensor(crowds[:, :, :], crowd[:, :].rearrange("p (o e) -> p o e", o=1).to_broadcast([P, NE, NE]),
                                         earlier, ALU.mult))
            step(nc.vector.tensor_reduce(crowd_at[:, :], crowds[:, :, :], AX.X, ALU.add))
            for k in range(ITEMS - NE):
                step(nc.vector.scalar_tensor_tensor(which[:, k, :], crowd_at[:, :], float(k), crowd[:, :], ALU.is_equal, ALU.mult))
                for n, row in enumerate((place_in[:, 0, :], place_in[:, 1, :], share[:, 0, :], share[:, 1, :])):
                    step(nc.vector.tensor_tensor_reduce(out=dots[:, k, n, :], in0=which[:, k, :], in1=row, scale=1.0, scalar=0.0,
                                                        op0=ALU.mult, op1=ALU.add, accum_out=items[:, NE + k, n:n + 1]))
                step(nc.vector.tensor_tensor_reduce(out=dots[:, k, 4, :], in0=which[:, k, :], in1=number, scale=1.0, scalar=0.0,
                                                    op0=ALU.mult, op1=ALU.add, accum_out=planf[:, k:k + 1]))
            step(nc.vector.tensor_scalar(items[:, NE:ITEMS, 0:NB], items[:, NE:ITEMS, 0:NB], -float(P), None, ALU.add))
            step(nc.vector.tensor_reduce(planf[:, 3:4], crowd[:, :], AX.X, ALU.add))
            step(nc.vector.tensor_scalar(planf[:, 3:4], planf[:, 3:4], float(NE - 1), None, ALU.add))
            step(nc.vector.memset(items[:, ITEMS, :], -1.0))
            nc.vector.tensor_copy(plan[:, :], planf[:, :]).then_inc(routed, 1)

            item(0, static_low)
            with dve.Fori(1, NE) as i:
                item(i, low_item)
            dve.wait_ge(routed, 1)
            n_items = dve.value_load(plan[0:1, 3:4], min_val=NE - 1, max_val=ITEMS - 1) + 1
            with dve.Fori(NE, ITEMS) as i:
                with dve.If(i < n_items):
                    item(i, low_item)
            finish(n_items)
            nc.vector.memset(one[:, :], 1.0).then_inc(region_free, 1)
            add_scattered(fill_no(n_items, 0), 0)
            add_scattered(fill_no(n_items, 2), 1)
            second_vector(dve, n_items, step, norm_sum, norm_apply, xt_low)

        @block.tensor
        def _(pe):
            def norm_transposes(n, tn, b):
                pe.wait_ge(xn_made, 2 * n + b + 1)
                for m in range(2):
                    for kk in range(4):
                        k = 4 * m + kk
                        mm = nc.tensor.transpose(ps[:, 4 + 2 * b + m, kk * P:kk * P + P], xn[:, b, k * P:k * P + P], ident)
                    mm.then_inc(xt_filled, 1)

            def first_products(n, product):
                if n:
                    keep_warm(3, 30)
                for b in range(NB):
                    norm_transposes(n, n, b)
                    pe.wait_ge(xt_lo, 4 * n + 2 * b + 2)
                    if b == 0 and n:
                        pe.wait_ge(x_made, 4 * n)
                    mm = product(b)
                return mm

            def token_transposes(src, banks, count):
                for m in range(2):
                    for kk in range(2):
                        for b in range(NB):
                            t = 2 * m + kk
                            mm = nc.tensor.transpose(ps[:, banks[m], (2 * kk + b) * P:(2 * kk + b + 1) * P],
                                                     src[:, b, t * P:t * P + P], ident)
                    mm.then_inc(count, 1)

            def mixer(l):
                c0 = LAYER_CHUNKS * l
                for j in range(8):
                    c = c0 + j
                    q, kh = j // 2, j % 2
                    if j:
                        pe.wait_ge(lo_made, c + 1)
                    if j == 4:
                        pe.wait_ge(sig_made, 2 * l + 2)
                    if j == 6:
                        pe.wait_ge(c_made, 2 * l + 2)
                    wh, wl = (slot_view(r, c % SPLITS, 4, 512) for r in (high, low))

                    def product(b):
                        pe.wait_ge(lo_made, c + 1)
                        for k in range(4):
                            kt = 4 * kh + k
                            mm = three(ps[:, 2 * (q % 2) + b, :], xT_hi[:, kt, b * P:b * P + P], xT_lo[:, kt, b * P:b * P + P],
                                       wh[:, k, :], wl[:, k, :], kt == 0, kt == KT - 1)
                        return mm

                    if j == 0:
                        mm = first_products(2 * l, product)
                    else:
                        for b in range(NB):
                            mm = product(b)
                    mm.then_inc(w_used, 1)
                    if j == 2:
                        pe.wait_ge(mix_landed, 16 * 9 * (l + 1))
                        nc.tensor.transpose(ps[:, 6, 0:16], rows16[:, :], ident[0:16, 0:16])
                        for t in range(CT):
                            mm = nc.tensor.transpose(ps[:, 6, 16 + TAPS * t:16 + TAPS * (t + 1)], conv_rows[:, t * P:t * P + P],
                                                     ident[0:TAPS, 0:TAPS])
                        mm.then_inc(prep_filled, 1)
                        for hh in range(SH):
                            mm = nc.tensor.transpose(ps[:, 7, hh * P:hh * P + P], sgu_rows[:, hh, :], ident)
                        mm.then_inc(prep_filled, 1)
                    if j == 4:
                        pe.wait_ge(c_made, 2 * l + 2)
                        token_transposes(c_tok, TP, ct_filled)
                pe.wait_ge(prep_made, 2 * l + 2)
                pe.wait_ge(diag_made, l + 1)
                pe.wait_ge(ct_made, 2 * l + 2)
                pe.wait_ge(pad_made, l + 1)

                def conv(first_tap, last_tap):
                    for k in range(first_tap, last_tap):
                        mm = nc.tensor.matmul(ps[:, 6, 0:T], diag[:, k, :], cT[:, PE_TILE, k:k + T], start=(k == 0),
                                              stop=(k == TAPS - 1))
                    return mm

                conv(0, 16)
                for b in range(NB):
                    pe.wait_ge(vn_made, 2 * l + b + 1)
                    for hh in range(SH):
                        mm = nc.tensor.matmul(ps[:, b, hh * P:hh * P + P], wsT[:, hh, :], v[:, b, hh * P:hh * P + P],
                                              start=True, stop=True)
                    mm.then_inc(sp_filled, 1)
                conv(16, TAPS).then_inc(pe_conv, 1)
                pe.wait_ge(g_made, 2 * l + 2)
                token_transposes(u, TP, gt_filled)

                def out_chunk(n):
                    c = c0 + 8 + n
                    pe.wait_ge(lo_made, c + 1)
                    k = OUT_ROWS[n]
                    mm = row_product(xT_hi, xT_lo, (k, k + 1), c % SPLITS, lambda b, half: DOWN[2 * b + half], NB,
                                     n == 0, n == 3, done=acc_ready if n == 3 else None)
                    mm.then_inc(w_used, 1)

                keep_warm(3, 22)
                pe.wait_ge(cat_lo, 4 * l + 2)
                pe.wait_ge(y2_made, l + 1)
                out_chunk(0)
                out_chunk(1)
                keep_warm(3, 24)
                pe.wait_ge(conv_step, len(DVE_TILES) * TAPS * (l + 1))
                for m in range(2):
                    for kk in range(2):
                        mm = nc.tensor.matmul(ps[:, TP[m], kk * T:kk * T + T], centre, yT[:, 2 * m + kk, :], start=True, stop=True)
                    mm.then_inc(yc_filled, 1)
                for t in range(CT):
                    pe.wait_ge(sq_made, 2 * l + t // 2 + 1)
                    mm = nc.tensor.matmul(ps[0:8, 2, 0:T], mean8[:, t, :], sq[:, t, :], start=(t == 0), stop=(t == CT - 1))
                mm.then_inc(var_filled, 1)
                keep_warm(3, 14)
                pe.wait_ge(rstd8_made, l + 1)
                for m in range(2):
                    for kk in range(2):
                        mm = nc.tensor.matmul(ps[:, 3 - m, kk * T:kk * T + T], spread8[:, 2 * m + kk, :], rstd8[:, :],
                                              start=True, stop=True)
                    mm.then_inc(rb_filled, 1)
                pe.wait_ge(cat_lo, 4 * l + 3)
                out_chunk(2)
                pe.wait_ge(cat_lo, 4 * l + 4)
                out_chunk(3)

            pe.wait_ge(small_landed, 16)
            mixer(0)
            c0 = MIX_CHUNKS
            for j in range(16):
                q, up = j // 2, j % 2
                c = c0 + j
                if j:
                    pe.wait_ge(lo_made, c + 1)
                if q:
                    pe.wait_ge(mult_made if up else silu_made, 2 * q)
                wh, wl = (slot_view(r, c % SPLITS, KT, TW) for r in (high, low))

                def product(b):
                    pe.wait_ge(lo_made, c + 1)
                    for k in range(KT):
                        mm = three(ps[:, 2 * up + b, 0:TW], xT_hi[:, k, b * P:b * P + P], xT_lo[:, k, b * P:b * P + P],
                                   wh[:, k, :], wl[:, k, :], k == 0, k == KT - 1)
                    return mm

                if j == 0:
                    mm = first_products(1, product)
                else:
                    for b in range(NB):
                        mm = product(b)
                mm.then_inc(w_used, 1)
                dense_transposes(pe, j)
            for d in range(8):
                c = c0 + 16 + d
                pe.wait_ge(lo_made, c + 1)
                tiles = down_tiles(d)
                pe.wait_ge(ht_lo, tiles[-1] // 2 + 1)
                if d == 0:
                    pe.wait_ge(silu_made, 16)
                mm = row_product(hT_hi, hT_lo, tiles, c % SPLITS, lambda b, half: DOWN[2 * b + half], NB, d == 0,
                                 d == 7, done=acc_ready if d == 7 else None)
                mm.then_inc(w_used, 1)
                dense_transposes(pe, 16 + d)
            mixer(1)
            pe.wait_ge(router_lo_made, 1)

            def router_product(b):
                for k in range(KT):
                    mm = three(ps[:, 0, b * NE:b * NE + NE], xT_hi[:, k, b * P:b * P + P], xT_lo[:, k, b * P:b * P + P],
                               router_hi[:, k, :], router_lo[:, k, :], k == 0, k == KT - 1)
                return mm

            first_products(3, router_product).then_inc(logits_ready, 1)
            keep_warm(3, 24)
            pe.wait_ge(chosen_made, 1)
            nc.tensor.matmul(ps[:, 1, 0:NE], before, chosen[:, 0, :], start=True, stop=True)
            nc.tensor.matmul(ps[:, 1, NE:2 * NE], before, chosen[:, 1, :], start=True, stop=False)
            nc.tensor.matmul(ps[:, 1, NE:2 * NE], ones, chosen[:, 0, :], start=False, stop=True)
            nc.tensor.matmul(ps[:, 1, 2 * NE:3 * NE], ones, chosen[:, 0, :], start=True, stop=False)
            nc.tensor.matmul(ps[:, 1, 2 * NE:3 * NE], ones, chosen[:, 1, :], start=False, stop=True).then_inc(places_ready, 1)
            keep_warm(3, 36)
            pe.wait_ge(xs_lo, 2)

            def scatter(first_fill, half):
                c = slice(half * 512, half * 512 + 512)
                for b in range(NB):
                    pe.wait_ge(tp_freed, first_fill + b - 1)
                    nc.tensor.matmul(ps[:, TP[b], :], drop[:, b, :], eo_hi[:, c], start=True, stop=False)
                    nc.tensor.matmul(ps[:, TP[b], :], drop[:, b, :], eo_lo[:, c], start=False, stop=True).then_inc(tp_filled, 1)

            def gather(fill, p):
                if not isinstance(fill, int) or fill >= 2:
                    pe.wait_ge(tp_freed, fill - 1)
                for part, base in ((xn_hi, 0), (xn_lo, 2 * P)):
                    for kk in range(2):
                        k = 2 * p + kk
                        for b in range(NB):
                            mm = nc.tensor.matmul(ps[:, TP[p % 2], base + kk * P:base + kk * P + P],
                                                  part[:, b, k * P:k * P + P], pick[:, b, :], start=(b == 0), stop=(b == 1))
                mm.then_inc(tp_filled, 1)

            def item(i):
                first = isinstance(i, int)
                for j in range(16):
                    g, up, kh = j // 4, j % 4 // 2, j % 2
                    pe.wait_ge(lo_made, chunk(i, j) + 1)
                    if j == 0:
                        pe.wait_ge(tp_freed, 4 if first else fill_no(i, 0))
                    if kh == 0 and not (first and g == 0):
                        pe.wait_ge(emult_made if up else esilu_made, 8 * i + 2 * g)
                    wh, wl = (slot_view(r, j % SPLITS, 4, GW) for r in (high, low))
                    for k in range(4):
                        kt = 4 * kh + k
                        for t in range(2):
                            c = slice(t * TW, t * TW + TW)
                            mm = three(ps[:, 2 * up + t, 0:TW], xe_hi[:, kt * P:kt * P + P], xe_lo[:, kt * P:kt * P + P],
                                       wh[:, k, c], wl[:, k, c], kt == 0, kt == KT - 1)
                    mm.then_inc(w_used, 1)
                    if j == 3 and not first:
                        pe.wait_ge(eo_lo_made, 2 * i)
                        scatter(fill_no(i, 0), 0)
                    if j == 4 and not first:
                        scatter(fill_no(i, 2), 1)
                    if j == 5:
                        for b in range(NB):
                            pe.wait_ge(tp_freed, fill_no(i, 4 + b) - 1)
                            nc.tensor.transpose(ps[:, TP[b], 0:P], f(pick[:, b, :]), ident).then_inc(tp_filled, 1)
                    hidden_transposes(i, j)
                for d in range(8):
                    j = 16 + d
                    tiles = down_tiles(d)
                    pe.wait_ge(lo_made, chunk(i, j) + 1)
                    pe.wait_ge(tp_freed, fill_no(i, 6 + batch_of(tiles[-1])) + 1)
                    row_product(eT_hi, eT_lo, tiles, j % SPLITS, lambda b, half: 6 + half, 1, d == 0,
                                d == 7).then_inc(w_used, 1)
                    hidden_transposes(i, j)
                    if j in GATHER_AFTER:
                        pe.wait_ge(pick_made, 2 * i + 4)
                        for p in GATHER_AFTER[j]:
                            gather(fill_no(i, 12 + p), p)

            def hidden_transposes(i, j):
                if j in AFTER_T:
                    n = AFTER_T[j]
                    lo, hi = BATCHES[n]
                    pe.wait_ge(emult_made, 8 * i + 2 * BATCH_GROUPS[n])
                    pe.wait_ge(tp_freed, fill_no(i, 6 + n) - 1)
                    for t in range(lo, hi):
                        mm = nc.tensor.transpose(ps[:, TP[n % 2], (t - lo) * P:(t - lo + 1) * P], eh[:, t * P:t * P + P], ident)
                    mm.then_inc(tp_filled, 1)

            pe.wait_ge(pick_made, 2)
            for p in range(4):
                gather(p, p)
            item(0)
            with pe.Fori(1, NE) as i:
                item(i)
            pe.wait_ge(routed, 1)
            n_items = pe.value_load(plan[0:1, 3:4], min_val=NE - 1, max_val=ITEMS - 1) + 1
            with pe.Fori(NE, ITEMS) as i:
                with pe.If(i < n_items):
                    item(i)
            pe.wait_ge(eo_lo_made, 2 * n_items)
            scatter(fill_no(n_items, 0), 0)
            scatter(fill_no(n_items, 2), 1)
            second_tensor(pe, n_items, norm_transposes)



_INS = ["x", "norm_mix", "w_in", "conv_w", "conv_b", "conv_ng", "conv_nb", "sgu_ng", "sgu_nb", "sgu_w", "sgu_b", "w_out",
        "norm_ffn", "ffn_wg", "ffn_wu", "ffn_wd", "moe_router", "moe_wg", "moe_wu", "moe_wd", "norm_final",
        "meta_tokens_2", "norm_gain_2", "w_in_2", "w_branch_sb_2", "w_branch_swa_2", "w_out_2", "attn_sinks_2",
        "final_norm_gain_2"]


def kernel(**inputs):
    import concourse.bacc as bacc
    from concourse.bass_utils import run_bass_kernel_spmd

    nc = bacc.Bacc("TRN2", target_bir_lowering=False, num_devices=1)
    arrays, given = {}, {}
    named = {name: np.ascontiguousarray(inputs[name]) for name in _INS}
    named.update(constants())
    for name, value in named.items():
        arrays[f"in_{name}"] = value
        given[name] = nc.dram_tensor(f"in_{name}", value.shape, mybir.dt.from_np(value.dtype), kind="ExternalInput").ap()
    out = nc.dram_tensor("out_x", (1, T, D), F32, kind="ExternalOutput").ap()
    model_program(nc, given, out)
    r = run_bass_kernel_spmd(nc, [arrays], core_ids=[0])
    return r.results[0]["out_x"]
```
